# Optimizing a Trainium2 kernel written in Bass

```python
import math
import jax
import jax.numpy as jnp
from jax import lax
import numpy as np

D_MODEL = 1024
BATCH = 1
SEQ = 1024
DEPTH = 2
DEC_BATCH = 8
DEC_SEQ = 4
PAST_LEN = 2048
PAGE_SIZE = 128

N_EVEN = (DEPTH + 1) // 2
N_ODD = DEPTH // 2
CONV_CH = D_MODEL // 2
CONV_W = 3
DA_HEADS = 4
DA_DIM = D_MODEL // (4 * DA_HEADS)
DA_WIDTH = 2 * DA_HEADS * DA_DIM
IN0 = 3 * CONV_CH + 3 * DA_WIDTH
ML_HEADS = 4
ML_DIM = D_MODEL // ML_HEADS
ML_CHUNK = 64
IN1 = 4 * D_MODEL + 2 * ML_HEADS
D_FF = -(-8 * D_MODEL // (3 * 256)) * 256
Q_BLOCK = 128
EPS = 1e-6

kernel_name = "hybrid_conv_diffattn_mlstm_decode_step"

def rmsnorm(x, g):
    xf = x.astype(jnp.float32)
    y = xf * lax.rsqrt(jnp.mean(xf * xf, axis=-1, keepdims=True) + EPS)
    return (y * g.astype(jnp.float32)).astype(x.dtype)

def swiglu(x, w_gu, w_down):
    gate, up = jnp.split(x @ w_gu, 2, axis=-1)
    return (jax.nn.silu(gate) * up) @ w_down

def lambda_init(layer):
    return 0.8 - 0.6 * math.exp(-0.3 * layer)

def short_conv(u, conv_w, buf):
    s = u.shape[1]
    ext = jnp.concatenate([buf.astype(u.dtype), u], axis=1)
    y = ext[:, 0:s] * conv_w[0]
    for j in range(1, CONV_W):
        y = y + ext[:, j:j + s] * conv_w[j]
    return y, ext[:, s:]

def diff_attend(q, k, v, mask, lam):
    s = jnp.einsum('bqhcd,bkhcd->bhcqk', q, k).astype(jnp.float32) * (DA_DIM ** -0.5)
    s = jnp.where(mask, s, -jnp.inf)
    p = jax.nn.softmax(s, axis=-1)
    w = p[:, :, 0] - lam * p[:, :, 1]
    return jnp.einsum('bhqk,bkhe->bqhe', w.astype(v.dtype), v)

def mixer_conv_diffattn(u, conv_buf, past_k, past_v, w_in, conv_w, lam_vec, subln_g, w_out, lam_init):
    b, s, _ = u.shape
    proj = u @ w_in
    gate_b, gate_c, xin, q, k, v = jnp.split(
        proj, [CONV_CH, 2 * CONV_CH, 3 * CONV_CH, 3 * CONV_CH + DA_WIDTH, 3 * CONV_CH + 2 * DA_WIDTH], axis=-1)
    conv_y, conv_new = short_conv(gate_c * xin, conv_w, conv_buf)
    y_conv = gate_b * conv_y
    lf = lam_vec.astype(jnp.float32)
    lam = jnp.exp(jnp.sum(lf[0] * lf[1])) - jnp.exp(jnp.sum(lf[2] * lf[3])) + lam_init
    q = q.reshape(b, s, DA_HEADS, 2, DA_DIM)
    k_rows = k.reshape(b, s, DA_HEADS, 2 * DA_DIM)
    v_rows = v.reshape(b, s, DA_HEADS, 2 * DA_DIM)
    if past_k is None:
        keys = k_rows.reshape(b, s, DA_HEADS, 2, DA_DIM)
        n_blk = s // Q_BLOCK
        q_blocks = jnp.moveaxis(q.reshape(b, n_blk, Q_BLOCK, DA_HEADS, 2, DA_DIM), 1, 0)
        k_pos = jnp.arange(s)

        def one_block(args):
            q_blk, i = args
            q_pos = i * Q_BLOCK + jnp.arange(Q_BLOCK)
            return diff_attend(q_blk, keys, v_rows, k_pos[None, :] <= q_pos[:, None], lam)

        attn = lax.map(one_block, (q_blocks, jnp.arange(n_blk)))
        attn = jnp.moveaxis(attn, 0, 1).reshape(b, s, DA_HEADS, 2 * DA_DIM)
    else:
        p = past_k.shape[1]
        keys = jnp.concatenate([past_k.astype(k_rows.dtype), k_rows], axis=1).reshape(b, p + s, DA_HEADS, 2, DA_DIM)
        vals = jnp.concatenate([past_v.astype(v_rows.dtype), v_rows], axis=1)
        mask = jnp.arange(p + s)[None, :] <= (p + jnp.arange(s))[:, None]
        attn = diff_attend(q, keys, vals, mask, lam)
    attn = rmsnorm(attn, subln_g) * (1.0 - lam_init)
    mixed = jnp.concatenate([y_conv, attn.reshape(b, s, DA_WIDTH)], axis=-1) @ w_out
    return mixed, k_rows, v_rows, conv_new

def mlstm_chunkwise(q, k, v, log_i, log_f, c0, n0, m0):
    b, s, h, dh = q.shape
    L = ML_CHUNK if s % ML_CHUNK == 0 else s
    nc = s // L

    def chunks(a):
        a = a.reshape((b, nc, L, h) + a.shape[3:])
        return jnp.moveaxis(jnp.moveaxis(a, 1, 0), 3, 2)

    tri = jnp.tril(jnp.ones((L, L), dtype=bool))

    def step(carry, xs):
        c, n, m = carry
        qi, ki, vi, li, lf = xs
        bc = jnp.cumsum(lf, axis=-1)
        mt = bc + jnp.maximum(m[..., None], lax.cummax(li - bc, axis=2))
        log_d = bc[..., :, None] - bc[..., None, :] + li[..., None, :] - mt[..., :, None]
        dmat = jnp.exp(jnp.where(tri, log_d, -jnp.inf))
        inter = jnp.exp(bc + m[..., None] - mt)
        sqk = jnp.einsum('bhtd,bhsd->bhts', qi, ki) * dmat
        num = inter[..., None] * jnp.einsum('bhtd,bhde->bhte', qi, c) + jnp.einsum('bhts,bhse->bhte', sqk, vi)
        den = inter * jnp.einsum('bhtd,bhd->bht', qi, n) + jnp.sum(sqk, axis=-1)
        h_til = num / jnp.maximum(jnp.abs(den), jnp.exp(-mt))[..., None]
        m_end = mt[..., -1]
        w_end = jnp.exp(bc[..., -1:] - bc + li - m_end[..., None])
        decay = jnp.exp(bc[..., -1] + m - m_end)
        wk = w_end[..., None] * ki
        c_new = decay[..., None, None] * c + jnp.einsum('bhsd,bhse->bhde', wk, vi)
        n_new = decay[..., None] * n + jnp.sum(wk, axis=2)
        return (c_new, n_new, m_end), h_til

    (c, n, m), hs = lax.scan(step, (c0, n0, m0), (chunks(q), chunks(k), chunks(v), chunks(log_i), chunks(log_f)))
    hs = jnp.transpose(hs, (1, 0, 3, 2, 4)).reshape(b, s, h, dh)
    return hs, c, n, m

def mixer_mlstm(u, c0, n0, m0, w_in, b_if, mh_g, w_out):
    b, s, _ = u.shape
    proj = u @ w_in
    q, k, v, o, gates = jnp.split(proj, [D_MODEL, 2 * D_MODEL, 3 * D_MODEL, 4 * D_MODEL], axis=-1)
    gates = gates.astype(jnp.float32) + b_if.astype(jnp.float32)
    log_i = gates[..., :ML_HEADS]
    log_f = jax.nn.log_sigmoid(gates[..., ML_HEADS:])

    def heads(a):
        return a.astype(jnp.float32).reshape(b, s, ML_HEADS, ML_DIM)

    h_til, c, n, m = mlstm_chunkwise(heads(q), heads(k) * (ML_DIM ** -0.5), heads(v), log_i, log_f,
                                     c0.astype(jnp.float32), n0.astype(jnp.float32), m0.astype(jnp.float32))
    hcell = jax.nn.sigmoid(heads(o)) * h_til
    hc = hcell - jnp.mean(hcell, axis=-1, keepdims=True)
    hn = hc * lax.rsqrt(jnp.mean(hc * hc, axis=-1, keepdims=True) + EPS)
    hn = hn.reshape(b, s, D_MODEL) * mh_g.astype(jnp.float32)
    return hn.astype(u.dtype) @ w_out, c, n, m

def trunk(x, state_conv, cache_k, cache_v, page_table, state_C, state_n, state_m, norms,
          w_in0, conv_w0, lam0, subln_g0, w_out0, w_in1, b_if1, mh_g1, w_out1, w_gu, w_down):
    h = x
    ks, vs, convs, cs, ns, ms = [], [], [], [], [], []
    for layer in range(DEPTH):
        j = layer // 2
        g = norms[layer]
        u = rmsnorm(h, g[0])
        if layer % 2 == 0:
            if cache_k is None:
                past_k = None
                past_v = None
            else:
                nb = page_table.shape[0]
                past_k = cache_k[j, page_table].reshape(nb, -1, DA_HEADS, 2 * DA_DIM)
                past_v = cache_v[j, page_table].reshape(nb, -1, DA_HEADS, 2 * DA_DIM)
            mix, k_rows, v_rows, conv_new = mixer_conv_diffattn(
                u, state_conv[j], past_k, past_v, w_in0[j], conv_w0[j], lam0[j], subln_g0[j], w_out0[j],
                lambda_init(layer))
            ks.append(k_rows)
            vs.append(v_rows)
            convs.append(conv_new)
        else:
            mix, c, n, m = mixer_mlstm(u, state_C[j], state_n[j], state_m[j], w_in1[j], b_if1[j], mh_g1[j], w_out1[j])
            cs.append(c)
            ns.append(n)
            ms.append(m)
        h = h + rmsnorm(mix, g[1])
        h = h + rmsnorm(swiglu(rmsnorm(h, g[2]), w_gu[layer], w_down[layer]), g[3])
    return h, jnp.stack(ks), jnp.stack(vs), jnp.stack(convs), jnp.stack(cs), jnp.stack(ns), jnp.stack(ms)

def setup_inputs(seed: int = 0) -> dict:
    key = jax.random.key(seed)
    ks = jax.random.split(key, 24)
    n_pages = PAST_LEN // PAGE_SIZE
    n_used = DEC_BATCH * n_pages
    n_phys = n_used + n_used // 4

    def nrm(k, shape, scale):
        return jax.random.normal(k, shape, jnp.float32) * scale

    return {
        'x_prompt': nrm(ks[0], (BATCH, SEQ, D_MODEL), 1.0),
        'x_sample': nrm(ks[1], (DEC_BATCH, DEC_SEQ, D_MODEL), 1.0),
        'cache_k': nrm(ks[2], (N_EVEN, n_phys, PAGE_SIZE, DA_HEADS, 2 * DA_DIM), 1.0),
        'cache_v': nrm(ks[3], (N_EVEN, n_phys, PAGE_SIZE, DA_HEADS, 2 * DA_DIM), 1.0),
        'state_conv': nrm(ks[4], (N_EVEN, DEC_BATCH, CONV_W - 1, CONV_CH), 1.0),
        'state_C': nrm(ks[5], (N_ODD, DEC_BATCH, ML_HEADS, ML_DIM, ML_DIM), ML_DIM ** -0.5),
        'state_n': nrm(ks[6], (N_ODD, DEC_BATCH, ML_HEADS, ML_DIM), 1.0),
        'state_m': nrm(ks[7], (N_ODD, DEC_BATCH, ML_HEADS), 1.0),
        'page_table': jax.random.permutation(ks[8], n_phys)[:n_used].reshape(DEC_BATCH, n_pages).astype(jnp.int32),
        'norms': 1.0 + nrm(ks[9], (DEPTH, 4, D_MODEL), 0.05),
        'w_in0': nrm(ks[10], (N_EVEN, D_MODEL, IN0), D_MODEL ** -0.5),
        'conv_w0': nrm(ks[11], (N_EVEN, CONV_W, CONV_CH), CONV_W ** -0.5),
        'lam0': nrm(ks[12], (N_EVEN, 4, DA_DIM), 0.1),
        'subln_g0': 1.0 + nrm(ks[13], (N_EVEN, 2 * DA_DIM), 0.05),
        'w_out0': nrm(ks[14], (N_EVEN, D_MODEL, D_MODEL), D_MODEL ** -0.5),
        'w_in1': nrm(ks[15], (N_ODD, D_MODEL, IN1), D_MODEL ** -0.5),
        'b_if1': jnp.concatenate([nrm(ks[16], (N_ODD, ML_HEADS), 0.1),
                                  3.0 + nrm(ks[17], (N_ODD, ML_HEADS), 0.1)], axis=-1),
        'mh_g1': 1.0 + nrm(ks[18], (N_ODD, D_MODEL), 0.05),
        'w_out1': nrm(ks[19], (N_ODD, D_MODEL, D_MODEL), D_MODEL ** -0.5),
        'w_gu': nrm(ks[20], (DEPTH, D_MODEL, 2 * D_FF), D_MODEL ** -0.5),
        'w_down': nrm(ks[21], (DEPTH, D_FF, D_MODEL), D_FF ** -0.5),
    }

def reference(x_prompt, x_sample, cache_k, cache_v, state_conv, state_C, state_n, state_m, page_table,
              norms, w_in0, conv_w0, lam0, subln_g0, w_out0, w_in1, b_if1, mh_g1, w_out1, w_gu, w_down):
    bp = x_prompt.shape[0]
    conv0 = jnp.zeros((N_EVEN, bp, CONV_W - 1, CONV_CH), x_prompt.dtype)
    c0 = jnp.zeros((N_ODD, bp, ML_HEADS, ML_DIM, ML_DIM), jnp.float32)
    n0 = jnp.zeros((N_ODD, bp, ML_HEADS, ML_DIM), jnp.float32)
    m0 = jnp.zeros((N_ODD, bp, ML_HEADS), jnp.float32)
    y_prompt, k_p, v_p, conv_p, c_p, n_p, m_p = trunk(
        x_prompt, conv0, None, None, None, c0, n0, m0, norms,
        w_in0, conv_w0, lam0, subln_g0, w_out0, w_in1, b_if1, mh_g1, w_out1, w_gu, w_down)
    y_sample, k_s, v_s, conv_s, c_s, n_s, m_s = trunk(
        x_sample, state_conv, cache_k, cache_v, page_table, state_C, state_n, state_m, norms,
        w_in0, conv_w0, lam0, subln_g0, w_out0, w_in1, b_if1, mh_g1, w_out1, w_gu, w_down)
    return (y_prompt, y_sample, k_p, v_p, conv_p, c_p, n_p, m_p, k_s, v_s, conv_s, c_s, n_s, m_s)


_drawn_inputs = setup_inputs


def setup_inputs(seed=0):
    import zlib

    import numpy as np

    out = dict(_drawn_inputs(seed))
    spreads = {}
    factors = {}
    for name, (base, spread) in spreads.items():
        noise = np.random.default_rng([zlib.crc32(name.encode()), seed]).standard_normal(out[name].shape)
        drawn = base * np.exp(spread * noise) if base else spread * noise
        out[name] = jnp.asarray(drawn.astype(out[name].dtype))
    for name, factor in factors.items():
        out[name] = (out[name] * factor).astype(out[name].dtype)
    return out
```

```python
import math
from contextlib import ExitStack

import concourse.bass as bass
from concourse import mybir

F32 = mybir.dt.float32
F16 = mybir.dt.float16
I32 = mybir.dt.int32
ALU = mybir.AluOpType
ACT = mybir.ActivationFunctionType
AX = mybir.AxisListType
ds = bass.ds

P = 128
D = 1024
KD = D // P
SEQ = 1024
NB, NS = 8, 4
TS = NB * NS
T = SEQ + TS
GW = T // 3
NTT = SEQ // P + 1
CH = D // 2
HEADS = 4
HC = CH // P
PAGE = 128
NPG = 16
DFF = 2816
KF = 11
WS = 64.0
EPS = 1e-6
LAM_INIT = 0.8 - 0.6 * math.exp(0.0)
BIG = 1e30
MLD = 256
SCALE_DA = 64 ** -0.5
RING = 8


class Chain:

    def __init__(self, eng, sem):
        self.eng, self.sem, self.base, self.n = eng, sem, 0, 0

    def link(self, ins):
        self.mark(ins)
        self.sync()

    def mark(self, ins):
        self.n += 1
        ins.then_inc(self.sem, 1)

    def sync(self):
        self.eng.wait_ge(self.sem, self.base + self.n)

    def enter(self, i, per):
        self.start, self.per = self.base + self.n, per
        self.base, self.n = i * per + self.start, 0

    def leave(self, times):
        assert self.n == self.per, (self.sem, "marks in the body:", self.n, "declared:", self.per)
        self.base, self.n = self.start + self.per * times, 0


def build(nc, x_p, x_s, cache_k, cache_v, state_conv, state_C, state_n, state_m, page_table, norms, w_in0,
          conv_w0, lam0, subln_g0, w_out0, w_in1, b_if1, mh_g1, w_out1, w_gu, w_down, y_p, y_s, k_p, v_p,
          conv_p, C_p, n_p, m_p, k_s, v_s, conv_s, C_s, n_s, m_s):
    ctx = ExitStack()
    with ctx:
        def sb(name, shape, dt=F32):
            return ctx.enter_context(nc.sbuf_tensor(name, shape, dt))

        def sem(name):
            return ctx.enter_context(nc.semaphore(name))

        hT = sb("hT", [P, KD, T])
        u = sb("u", [P, 2, KD, T], F16)
        w_raw = sb("w_raw", [P, 2, KF * P])
        w_split = sb("w_split", [P, 2, 2, KF * P], F16)
        arena = sb("arena", [P, 28, T])
        ident = sb("ident", [P, P])
        ones = sb("ones", [P, P])
        gains = sb("gains", [P, 88])
        causal = sb("causal", [P, P])
        dmask = sb("dmask", [P, P])
        dmask_s = sb("dmask_s", [TS, TS])
        smask = sb("smask", [TS, NB * 2 * NS])
        bmask = sb("bmask", [TS, NB])
        sel = sb("sel", [HEADS, HEADS, P])
        small = sb("small", [P, 400])
        roots = sb("roots", [P, 3, NTT])
        ps = ctx.enter_context(nc.psum_tensor("ps", [P, 8, 512], F32))

        GN = lambda layer, which: (layer * 4 + which) * KD
        GM, GS, GC = 64, 72, 73

        def rows(a, n):
            return arena[:, a:a + n, :]

        def half(region, tiles):
            return region.rearrange("p a t -> p (a t)").bitcast(F16).rearrange(
                "p (l k t) -> p l k t", l=2, k=tiles)

        def group(bank):
            return ps[:, bank:bank + 3, 0:GW]

        def flat(bank, n):
            return ps[:, bank:bank + -(-n // 512), :].rearrange("p b w -> p (b w)")[:, 0:n]

        def alone(eng):
            eng.sem_inc(passed[eng.engine], 1)

        def by3(row):
            return row.rearrange("p (g t) -> p g t", g=3)

        mix = half(rows(0, 8), KD)
        hid = half(rows(0, KF), KF)
        ybuf = rows(11, 8)
        tmp = [arena[:, 19, :], arena[:, 20, :]]
        hidf = arena[:, 21, :]
        gate = arena[:, 22, :]
        sq = [arena[:, 23, :], arena[:, 24, :]]
        ssq = arena[:, 25, :]
        diag_row = arena[:, 26, :]

        w_loaded = [sem("w_loaded0"), sem("w_loaded1")]
        w_hi = sem("w_hi")
        w_ready = sem("w_ready")
        mm_done = sem("mm_done")
        evac = [sem("evac0"), sem("evac1")]
        passed = {e.engine: sem(f"passed{i}") for i, e in enumerate((nc.sync, nc.scalar, nc.gpsimd))}
        const_ready = sem("const_ready")
        gain_loaded = sem("gain_loaded")
        gain_t = sem("gain_t")
        x_loaded = [sem(f"x_loaded{i}") for i in range(NTT)]
        x_t = sem("x_t")
        x_ev = [sem("x_ev0"), sem("x_ev1")]
        sq_ready = sem("sq_ready")
        ssq_added = sem("ssq_added")
        root_sum = sem("root_sum")
        root_in, root_out = sem("root_in"), sem("root_out")
        root_diag = sem("root_diag")
        root_done = sem("root_done")
        h_ready = sem("h_ready")
        t_ready = sem("t_ready")
        u_hi = sem("u_hi")
        u_ready = sem("u_ready")
        hid_hi = sem("hid_hi")
        hid_ready = sem("hid_ready")
        y_t = sem("y_t")
        y_ev = [sem("y_ev0"), sem("y_ev1")]
        out_done = sem("out_done")
        act_c, dve_c, pool_c = sem("act_c"), sem("dve_c"), sem("pool_c")
        outs = [0]

        def over_pairs(eng, n, body, chain=None, per=0):
            if n > 2:
                with eng.Fori(0, n // 2 - 1) as i:
                    if chain:
                        chain.enter(i, per)
                    body(i, 0, False)
                    body(i, 1, False)
                if chain:
                    chain.leave(n // 2 - 1)
            body(n // 2 - 1, 0, False)
            body(n // 2 - 1, 1, True)

        def load_tile(sp, c, r, src, kt, n=P, wait=True):
            s = c % 2
            if wait:
                sp.wait_ge(w_ready, c - 1 + 2 * r)
            alone(sp)
            sp.dma_start(w_raw[:, s, 0:kt * n].rearrange("p (k n) -> p k n", k=kt), src).then_inc(w_loaded[s], 16)

        def split_hi(act, c, r, kt, n=P, first=False):
            s = c % 2
            act.wait_ge(w_loaded[s], 16 * (c // 2 + 1) + 16 * r)
            if not first:
                act.wait_ge(mm_done, c - 1 + 2 * r)
            act.activation(w_split[:, s, 0, 0:kt * n], w_raw[:, s, 0:kt * n], ACT.Copy, scale=WS).then_inc(w_hi, 1)

        def split_lo(dve, c, r, kt, n=P):
            s = c % 2
            dve.wait_ge(w_hi, c + 1 + 2 * r)
            dve.scalar_tensor_tensor(w_split[:, s, 1, 0:kt * n], w_raw[:, s, 0:kt * n], WS,
                                     w_split[:, s, 0, 0:kt * n], ALU.mult, ALU.subtract).then_inc(w_ready, 1)

        def products(pe, c, r, x, kt, m=P, n=P, col=0, bank=None, signal=True):
            s = c % 2
            pe.wait_ge(w_ready, c + 1 + 2 * r)
            pe.wait_ge(evac[s], c // 2 + r)
            b = 3 * s if bank is None else bank
            for k in range(kt):
                for q, (wp, xp) in enumerate(((0, 0), (0, 1), (1, 0))):
                    for g in range(3):
                        ins = pe.matmul(ps[0:m, b + g, 0:GW], w_split[:, s, wp, k * n + col:k * n + col + m],
                                        x[:, xp, k, g * GW:(g + 1) * GW],
                                        start=(k == 0 and q == 0), stop=(k == kt - 1 and q == 2))
            if signal:
                ins.then_inc(mm_done, 1)

        QK, V, CXB, WO0 = 0, 8, 12, 24
        FF0 = 32
        GATES, QKVO, WO1 = FF0 + 60, FF0 + 61, FF0 + 93
        FF1 = WO1 + 8
        END = FF1 + 60

        def at(c, r):
            return c + 1 + 2 * r

        def out_of_banks(c, r):
            return c // 2 + 1 + r

        def w_cols(w, col):
            return w.rearrange("(k p) n -> p k n", p=P)[:, :, col]

        def one(ap):
            return ap.rearrange("p (a t) -> p a t", a=1)

        def add_squares(pool, n):
            for k in range(KD):
                pool.wait_ge(sq_ready, KD * n + k + 1)
                if k == 0:
                    if n:
                        pool.wait_ge(root_sum, norm_q(n - 1) + 1)
                    pool.tensor_copy(ssq, sq[k % 2]).then_inc(ssq_added, 1)
                else:
                    pool.wait_ge(ssq_added, KD * n + k)
                    pool.tensor_tensor(ssq, ssq, sq[k % 2], ALU.add).then_inc(ssq_added, 1)

        def square(act, n, k, r, src):
            if not (n == 0 and k < 2 and isinstance(r, int) and r == 0):
                act.wait_ge(ssq_added, KD * n + k - 1 + 2 * r)
            act.activation(sq[k % 2], src, ACT.Square).then_inc(sq_ready, 1)

        def tiles_of(width):
            return [(t, min(P, width - t * P)) for t in range(-(-width // P))]

        def pe_roots(pe, q, d, srcs, diag, width, bank):
            for t, w in tiles_of(width):
                for k, src in enumerate(srcs):
                    ins = pe.matmul(ps[0:w, 6, t:t + 1], src[:, t * P:t * P + w], ones[:, 0:1], start=(k == 0),
                                    stop=(k == len(srcs) - 1))
            ins.then_inc(root_sum, 1)
            for t, w in tiles_of(width):
                pe.wait_ge(root_diag, d + t + 1)
                ins = pe.matmul(flat(bank, width)[:, t * P:t * P + w], ones[0:w, :], diag[0:w, t * P:t * P + w],
                                start=True, stop=True)
            ins.then_inc(root_done, 1)

        def act_roots(act, q, n):
            act.wait_ge(root_in, q + 1)
            act.activation(roots[:, 1, 0:n], roots[:, 0, 0:n], ACT.Abs_reciprocal_sqrt).then_inc(root_out, 1)

        def dve_roots(dve, chain, q, d, diag, width, eps):
            ts = tiles_of(width)
            dve.wait_ge(root_sum, q + 1)
            full = sum(w == P for _, w in ts)
            x, y, z = (roots[:, i, 0:len(ts)] for i in range(3))
            ins = dve.tensor_scalar(roots[:, 0, 0:full], ps[:, 6, 0:full], eps, None, ALU.add)
            if full < len(ts):
                w = ts[-1][1]
                ins = dve.tensor_scalar(roots[0:w, 0, full:full + 1], ps[0:w, 6, full:full + 1], eps, None, ALU.add)
            ins.then_inc(root_in, 1)
            dve.wait_ge(root_in, q + 1)
            dve.wait_ge(root_out, q + 1)
            chain.link(dve.tensor_tensor(z, x, y, ALU.mult))
            chain.link(dve.tensor_tensor(z, z, y, ALU.mult))
            chain.link(dve.tensor_scalar(z, z, -0.5, 1.5, ALU.mult, ALU.add))
            chain.link(dve.tensor_tensor(z, z, y, ALU.mult))
            for t, w in ts:
                dve.tensor_scalar(diag[0:w, t * P:t * P + w], ident[0:w, 0:w], z[0:w, t:t + 1], None,
                                  ALU.mult).then_inc(root_diag, 1)
            dve.wait_ge(root_done, q + 1)

        def norm_q(n):
            return 0 if n == 0 else HEADS + 1 + n if n < 5 else 2 * HEADS + 1 + n

        def norm_d(n):
            return 0 if n == 0 else 42 + 9 * (n - 1) if n < 5 else 78 + 9 * HEADS + 9 * (n - 5)

        HEAD_Q, HEAD_D, SAMPLE_Q, SAMPLE_D, ML_Q, ML_D = 1, 9, 1 + HEADS, 9 + 8 * HEADS, 2 + HEADS + 4, 78

        def pe_norm(pe, n, bank):
            pe.wait_ge(ssq_added, KD * (n + 1))
            pe_roots(pe, norm_q(n), norm_d(n), [ssq], diag_row, T, bank)

        def dve_after(dve, chain, n, layer, which, m):
            dve_roots(dve, chain, norm_q(n), norm_d(n), diag_row, T, D * EPS)
            rs = flat(0, T)
            col = GN(layer, which)
            for k in range(KD):
                chain.link(dve.tensor_tensor(tmp[k % 2], ybuf[:, k, :], rs, ALU.mult))
                dve.scalar_tensor_tensor(hT[:, k, :], tmp[k % 2], gains[:, col + k:col + k + 1], hT[:, k, :],
                                         ALU.mult, ALU.add).then_inc(h_ready, 1)

        def act_before(act, n, h0, m):
            for k in range(KD):
                if n:
                    act.wait_ge(h_ready, h0 + k + 1)
                square(act, n, k, 0, hT[:, k, :])
            act_roots(act, norm_q(n), NTT)
            for k in range(KD):
                act.wait_ge(t_ready, KD * m + k + 1)
                act.activation(u[:, 0, k, :], tmp[k % 2], ACT.Copy).then_inc(u_hi, 1)

        def dve_before(dve, chain, n, layer, which, m):
            dve_roots(dve, chain, norm_q(n), norm_d(n), diag_row, T, D * EPS)
            rs = flat(3, T)
            col = GN(layer, which)
            def lo(k):
                dve.wait_ge(u_hi, KD * m + k + 1)
                dve.tensor_tensor(u[:, 1, k, :], tmp[k % 2], u[:, 0, k, :], ALU.subtract).then_inc(u_ready, 1)
            for k in range(KD):
                if k >= 2:
                    dve.wait_ge(u_ready, KD * m + k - 1)
                dve.scalar_tensor_tensor(tmp[k % 2], hT[:, k, :], gains[:, col + k:col + k + 1], rs,
                                         ALU.mult, ALU.mult).then_inc(t_ready, 1)
                if k:
                    lo(k - 1)
            lo(KD - 1)

        def act_project(act, c0, stage, kt_next):
            def tile(i, j, last):
                split_hi(act, c0 + j + 1, i, kt_next if last else KD)
                act.wait_ge(mm_done, at(c0 + j, i))
                alone(act)
                yt = ybuf[:, ds(2 * i + j, 1), :] if not isinstance(i, int) else ybuf[:, 2 * i + j:2 * i + j + 1, :]
                yt = yt.rearrange("p a (g t) -> p (a g) t", g=3)
                act.activation(yt, group(3 * ((c0 + j) % 2)), ACT.Copy,
                               scale=1 / WS).then_inc(evac[(c0 + j) % 2], 1)
                act.wait_ge(evac[(c0 + j) % 2], out_of_banks(c0 + j, i))
                act.wait_ge(ssq_added, KD * stage + j - 1 + 2 * i)
                alone(act)
                act.activation(by3(sq[j]), yt, ACT.Square).then_inc(sq_ready, 1)
            over_pairs(act, 8, tile)

        def dve_splits(dve, c0, n, kt_next):
            over_pairs(dve, n, lambda i, j, last: split_lo(dve, c0 + j + 1, i, kt_next if last else KD))

        def load_ffn(sp, c0, layer):
            for half_ in range(2):
                c = c0 + 30 * half_
                r0 = half_ * KF * P
                over_pairs(sp, 22, lambda i, j, last: load_tile(
                    sp, c + j, i, w_cols(w_gu[layer], ds(r0 + j * DFF + i * P, P)), KD))
                over_pairs(sp, 8, lambda i, j, last: load_tile(
                    sp, c + 22 + j, i, w_cols(w_down[layer, r0:r0 + KF * P, :], ds((2 * i + j) * P, P)), KF))

        def pe_ffn(pe, c0, layer, m):
            pe.wait_ge(u_ready, KD * (m + 1))
            for half_ in range(2):
                c = c0 + 30 * half_
                over_pairs(pe, 22, lambda i, j, last: products(pe, c + j, i, u, KD))
                pe.wait_ge(hid_ready, 22 * layer + 11 * (half_ + 1))
                over_pairs(pe, 8, lambda i, j, last: products(pe, c + 22 + j, i, hid, KF))

        def act_ffn(act, c0, layer, stage, more):
            for half_ in range(2):
                c, n0 = c0 + 30 * half_, 22 * layer + 11 * half_
                a, b = c % 2, (c + 1) % 2

                def gate_up(i, j, last):
                    split_hi(act, c + j + 1, i, KF if last else KD)
                    if j == 0:
                        act.wait_ge(mm_done, at(c, i))
                        act.wait_ge(evac[b], (c + 1) // 2 + i)
                        act.activation(by3(gate), group(3 * a), ACT.Silu, scale=1 / WS).then_inc(evac[a], 1)
                    else:
                        act.wait_ge(evac[b], out_of_banks(c + 1, i))
                        alone(act)
                        act.activation(hid[:, 0, ds(i, 1), :], one(hidf), ACT.Copy).then_inc(hid_hi, 1)
                over_pairs(act, 22, gate_up)

                def down(i, j, last):
                    e = c + 22 + j
                    if not last or more or half_ == 0:
                        split_hi(act, e + 1, i, KD if last else KF, n=8 if last and half_ else P)
                    yt = ybuf[:, ds(2 * i + j, 1), :].rearrange("p a (g t) -> p (a g) t", g=3)
                    if half_ == 0:
                        act.wait_ge(mm_done, at(e, i))
                        alone(act)
                        act.activation(yt, group(3 * (e % 2)), ACT.Copy, scale=1 / WS).then_inc(evac[e % 2], 1)
                    else:
                        act.wait_ge(evac[e % 2], out_of_banks(e, i))
                        act.wait_ge(ssq_added, KD * stage + j - 1 + 2 * i)
                        alone(act)
                        act.activation(by3(sq[j]), yt, ACT.Square).then_inc(sq_ready, 1)
                over_pairs(act, 8, down)

        def dve_ffn(dve, c0, layer, more):
            for half_ in range(2):
                c, n0 = c0 + 30 * half_, 22 * layer + 11 * half_
                a, b = c % 2, (c + 1) % 2

                def gate_up(i, j, last):
                    split_lo(dve, c + j + 1, i, KF if last else KD)
                    if j == 0:
                        return
                    dve.wait_ge(mm_done, at(c + 1, i))
                    dve.wait_ge(evac[a], out_of_banks(c, i))
                    dve.wait_ge(hid_hi, n0 + i)
                    dve.wait_ge(hid_ready, n0 + i)
                    dve.scalar_tensor_tensor(by3(hidf), group(3 * b), 1 / WS, by3(gate),
                                             ALU.mult, ALU.mult).then_inc(evac[b], 1)
                    dve.wait_ge(evac[b], out_of_banks(c + 1, i))
                    dve.wait_ge(hid_hi, n0 + i + 1)
                    dve.tensor_tensor(hid[:, 1, ds(i, 1), :], one(hidf), hid[:, 0, ds(i, 1), :],
                                      ALU.subtract).then_inc(hid_ready, 1)
                over_pairs(dve, 22, gate_up)

                def down(i, j, last):
                    e = c + 22 + j
                    if not last or more or half_ == 0:
                        split_lo(dve, e + 1, i, KD if last else KF, n=8 if last and half_ else P)
                    if half_ == 0:
                        return
                    yt = ybuf[:, ds(2 * i + j, 1), :].rearrange("p a (g t) -> p (a g) t", g=3)
                    dve.wait_ge(mm_done, at(e, i))
                    dve.scalar_tensor_tensor(yt, group(3 * (e % 2)), 1 / WS, yt,
                                             ALU.mult, ALU.add).then_inc(evac[e % 2], 1)
                over_pairs(dve, 8, down)

        qT, kT, vT = rows(8, 4), rows(12, 4), rows(16, 4)
        gate_c = arena[:, 20, :]
        conv_in = rows(21, 2).rearrange("p a t -> p (a t)")
        conv_p_in = conv_in[:, 0:SEQ + 2]
        conv_s_in = conv_in[:, SEQ + 2:SEQ + 2 + NB * 6].rearrange("p (b t) -> p b t", b=NB)
        conv_y, y_b = arena[:, 23, :], arena[:, 24, :]
        u_row = u.rearrange("p l k t -> p (l k t)").bitcast(F32).rearrange("p (a t) -> p a t", t=T)
        prob = [u_row[:, i, 0:SEQ] for i in range(4)]
        ring = u_row[:, 4:8, :].rearrange("p a t -> p (a t)")[:, 0:RING * CH].rearrange("p (r c) -> p r c", r=RING)
        q_h, k_h, v_h = arena[:, 20, 0:SEQ], arena[:, 21, :], arena[:, 22, :]
        v_nat, k_nat, att = arena[:, 23, 0:SEQ], arena[:, 27, 0:SEQ], arena[:, 24, 0:SEQ]
        prob_t = [arena[:, 25, 0:SEQ], arena[:, 26, 0:SEQ]]
        q_pages = sb("q_pages", [P, NB, HEADS, 8])
        kv_s_nat = sb("kv_s_nat", [TS, 2, HEADS, P])
        stT = sb("stT", [P, HC, 2 * NB])
        conv_new = sb("conv_new", [P, HC, 2 + 2 * NB])
        lam_rows = small[:, 0:256]
        lam_prod = small[:, 256:384]
        lam_e = small[:, 384:386]
        neg_lam = small[:, 386:387]
        mx, neg_mx = small[:, 388:390], small[:, 390:394]
        lsum, rl = small[:, 394:398], small[:, 398:400]
        k_page_t = [arena[:, 22, 0:CH], arena[:, 22, CH:2 * CH]]
        probs_s = [arena[:, 20, 0:17 * 32], arena[:, 21, 0:17 * 32]]
        self_s = arena[0:TS, 23, 0:256].rearrange("p (h n) -> p h n", h=HEADS)
        att_s = arena[:, 24, 0:P].rearrange("p (h t) -> p h t", h=HEADS)
        sm_max, sm_bc, sm_sum, sm_rl, sm_o = (arena[:, 25, 32 * i:32 * i + 32] for i in range(5))
        sm_col, sm_dg = arena[0:32, 25, 160:161], arena[0:32, 25, 192:224]
        page_ids = sb("page_ids", [1, NB * NPG], I32)

        lam_loaded, misc_t, misc_ev = sem("lam_loaded"), sem("misc_t"), sem("misc_ev")
        lam_ready = sem("lam_ready")
        gate_c_used = sem("gate_c_used")
        yb_hi, mix_ready = sem("yb_hi"), sem("mix_ready")
        conv_saved = sem("conv_saved")
        cur_ready = sem("cur_ready")
        vk_t = sem("vk_t")
        v_ev, k_ev = sem("v_ev"), sem("k_ev")
        kv_stored = sem("kv_stored")
        s_done = sem("s_done")
        nm_ready = sem("nm_ready")
        p_ready = sem("p_ready")
        w_comb = sem("w_comb")
        pt_t = sem("pt_t")
        pt_ev = sem("pt_ev")
        pv_done = sem("pv_done")
        pv_ev = sem("pv_ev")
        asq_ready = sem("asq_ready")
        at_ready, mix_hi = sem("at_ready"), sem("mix_hi")
        head_done = sem("head_done")
        page_loaded = [sem(f"page_loaded{i}") for i in range(RING)]
        page_used = sem("page_used")
        ids_loaded = sem("ids_loaded")
        kp_t = sem("kp_t")
        kp_ev = [sem("kp_ev0"), sem("kp_ev1")]
        kp_used = sem("kp_used")
        qp_ready, self_done, self_ready = sem("qp_ready"), sem("self_done"), sem("self_ready")
        mx_ready, mx_t, dg_ready, mx_bc = sem("mx_ready"), sem("mx_t"), sem("dg_ready"), sem("mx_bc")
        sub_ready, ps_exp, sum_ready, sum_bc = sem("sub_ready"), sem("ps_exp"), sem("sum_ready"), sem("sum_bc")
        rl_ready, pvs_done, pvs_ev = sem("rl_ready"), sem("pvs_done"), sem("pvs_ev")
        spilled, restored = sem("spilled"), sem("restored")

        def act_proj0(act, chain):
            def qk(i, j, last):
                split_hi(act, QK + j + 1, i, KD)
                if j == 0:
                    act.wait_ge(mm_done, at(QK, i))
                    alone(act)
                    act.activation(qT[:, ds(i, 1), :].rearrange("p a (g t) -> p (a g) t", g=3), group(0), ACT.Copy,
                                   scale=1 / WS).then_inc(evac[0], 1)
            over_pairs(act, 8, qk)

            def v(i, j, last):
                split_hi(act, V + j + 1, i, KD)
                if j == 0:
                    act.wait_ge(mm_done, at(V, i))
                    alone(act)
                    act.activation(vT[:, ds(2 * i, 1), :].rearrange("p a (g t) -> p (a g) t", g=3), group(0),
                                   ACT.Copy, scale=1 / WS).then_inc(evac[0], 1)
            over_pairs(act, 4, v)
            with act.Fori(0, 2) as i:
                for m in range(6):
                    c, r = CXB + m, 3 * i
                    split_hi(act, c + 1, r, KD)
                    if m % 3 == 0:
                        act.wait_ge(mm_done, at(c, r))
                        act.wait_ge(gate_c_used, 2 * i + m // 3)
                        act.activation(by3(gate_c), group(3 * (c % 2)), ACT.Copy,
                                       scale=1 / WS).then_inc(evac[c % 2], 1)
                    if m % 3 == 2:
                        act.wait_ge(evac[c % 2], out_of_banks(c, r))
                        alone(act)
                        act.activation(mix[:, 0, ds(2 * i + m // 3, 1), :], one(y_b), ACT.Copy).then_inc(yb_hi, 1)

        def dve_proj0(dve, chain):
            def qk(i, j, last):
                split_lo(dve, QK + j + 1, i, KD)
                if j:
                    dve.wait_ge(mm_done, at(QK + 1, i))
                    dve.tensor_scalar(kT[:, ds(i, 1), :].rearrange("p a (g t) -> p (a g) t", g=3), group(3), 1 / WS,
                                      None, ALU.mult).then_inc(evac[1], 1)
            over_pairs(dve, 8, qk)

            def v(i, j, last):
                split_lo(dve, V + j + 1, i, KD)
                if j:
                    dve.wait_ge(mm_done, at(V + 1, i))
                    dve.tensor_scalar(vT[:, ds(2 * i + 1, 1), :].rearrange("p a (g t) -> p (a g) t", g=3), group(3),
                                      1 / WS, None, ALU.mult).then_inc(evac[1], 1)
            over_pairs(dve, 4, v)
            per = 2 * 7
            with dve.Fori(0, 2) as i:
                chain.enter(i, per)
                for m in range(6):
                    c, r = CXB + m, 3 * i
                    h = 2 * i + m // 3
                    b = 3 * (c % 2)
                    split_lo(dve, c + 1, r, KD)
                    if m % 3 == 1:
                        chain.mark(dve.tensor_copy(conv_s_in[:, :, 0:2], stT[:, ds(h, 1), :].rearrange(
                            "p a (b t) -> p (a b) t", b=NB)))
                        dve.wait_ge(mm_done, at(c, r))
                        dve.wait_ge(evac[(c - 1) % 2], out_of_banks(c - 1, r))
                        dve.scalar_tensor_tensor(
                            conv_p_in[:, 2:2 + 2 * GW].rearrange("p (g t) -> p g t", g=2), ps[:, b:b + 2, 0:GW],
                            1 / WS, gate_c[:, 0:2 * GW].rearrange("p (g t) -> p g t", g=2), ALU.mult, ALU.mult)
                        chain.mark(dve.scalar_tensor_tensor(
                            conv_p_in[:, 2 + 2 * GW:2 + SEQ], ps[:, b + 2, 0:SEQ - 2 * GW], 1 / WS,
                            gate_c[:, 2 * GW:SEQ], ALU.mult, ALU.mult))
                        dve.scalar_tensor_tensor(
                            conv_s_in[:, :, 2:6], ps[:, b + 2, SEQ - 2 * GW:GW].rearrange("p (b t) -> p b t", b=NB),
                            1 / WS, gate_c[:, SEQ:T].rearrange("p (b t) -> p b t", b=NB),
                            ALU.mult, ALU.mult).then_inc(evac[c % 2], 1)
                        dve.wait_ge(evac[c % 2], out_of_banks(c, r))
                        chain.sync()
                        chain.mark(dve.tensor_copy(conv_new[:, ds(h, 1), 0:2], one(conv_p_in[:, SEQ:SEQ + 2])))
                        chain.mark(dve.tensor_copy(
                            conv_new[:, ds(h, 1), 2:2 + 2 * NB].rearrange("p a (b t) -> p (a b) t", b=NB),
                            conv_s_in[:, :, 4:6]))
                        for k in range(3):
                            w = gains[:, ds(GC + k * HC + h, 1)]
                            yp, ys = conv_y[:, 0:SEQ], conv_y[:, SEQ:T].rearrange("p (b t) -> p b t", b=NB)
                            xp, xs = conv_p_in[:, k:k + SEQ], conv_s_in[:, :, k:k + NS]
                            if k == 0:
                                dve.tensor_scalar(yp, xp, w, None, ALU.mult)
                                chain.link(dve.tensor_scalar(ys, xs, w, None, ALU.mult))
                            elif k == 1:
                                dve.scalar_tensor_tensor(yp, xp, w, yp, ALU.mult, ALU.add)
                                chain.link(dve.scalar_tensor_tensor(ys, xs, w, ys, ALU.mult, ALU.add))
                            else:
                                chain.mark(dve.scalar_tensor_tensor(yp, xp, w, yp, ALU.mult, ALU.add))
                                dve.scalar_tensor_tensor(ys, xs, w, ys, ALU.mult, ALU.add).then_inc(gate_c_used, 1)
                    if m % 3 == 2:
                        dve.wait_ge(mm_done, at(c, r))
                        dve.wait_ge(gate_c_used, 2 * i + m // 3 + 1)
                        chain.sync()
                        dve.wait_ge(yb_hi, 2 * i + m // 3)
                        dve.wait_ge(mix_ready, 2 * i + m // 3)
                        dve.scalar_tensor_tensor(by3(y_b), group(b), 1 / WS, by3(conv_y), ALU.mult,
                                                 ALU.mult).then_inc(evac[c % 2], 1)
                        dve.wait_ge(evac[c % 2], out_of_banks(c, r))
                        dve.wait_ge(yb_hi, 2 * i + m // 3 + 1)
                        dve.tensor_tensor(mix[:, 1, ds(h, 1), :], one(y_b), mix[:, 0, ds(h, 1), :],
                                          ALU.subtract).then_inc(mix_ready, 1)
            chain.leave(2)

        def pe_heads(pe):
            with pe.Fori(0, HEADS) as h:
                def transposes(src, n):
                    for tt in range(NTT):
                        w = P if tt < NTT - 1 else TS
                        ins = pe.transpose(ps[0:w, 4 + tt // 4, (tt % 4) * P:(tt % 4 + 1) * P],
                                           src[:, tt * P:tt * P + w], ident[:, :])
                    ins.then_inc(vk_t, 1)
                pe.wait_ge(cur_ready, 3 * h + 1)
                pe.wait_ge(head_done, h)
                transposes(v_h, 0)
                pe.wait_ge(cur_ready, 3 * h + 2)
                pe.wait_ge(v_ev, h + 1)
                transposes(k_h, 1)
                pe.wait_ge(cur_ready, 3 * h + 3)

                def scores(n):
                    i, c = n // 2, n % 2
                    if n < 2:
                        pe.wait_ge(p_ready, 16 * h)
                    else:
                        pe.wait_ge(p_ready, 16 * h + n - 1)
                    w = (i + 1) * P
                    for j in range(0, w, 512):
                        ins = pe.matmul(ps[:, 2 * (n % 2) + j // 512, 0:min(512, w - j)],
                                        q_h[64 * c:64 * c + 64, i * P:(i + 1) * P],
                                        k_h[64 * c:64 * c + 64, j:min(j + 512, w)], start=True, stop=True)
                    ins.then_inc(s_done, 1)
                scores(0)
                scores(1)
                pe.wait_ge(k_ev, h + 1)
                for i in range(8):
                    if i < 7:
                        scores(2 * i + 2)
                        scores(2 * i + 3)
                    pe.wait_ge(w_comb, 8 * h + i + 1)
                    pe.wait_ge(pt_ev, 8 * h + i)
                    for j in range(i + 1):
                        ins = pe.transpose(flat(4, 1024)[:, j * P:(j + 1) * P], prob[2 * (i % 2)][:, j * P:(j + 1) * P],
                                           ident[:, :])
                    ins.then_inc(pt_t, 1)
                    pe.wait_ge(pt_ev, 8 * h + i + 1)
                    if i < 2:
                        pe.wait_ge(pv_ev, 8 * h)
                    else:
                        pe.wait_ge(pv_ev, 8 * h + i - 1)
                    for j in range(i + 1):
                        ins = pe.matmul(ps[:, 6 + i % 2, 0:P], v_nat[:, j * P:(j + 1) * P],
                                        prob_t[i % 2][:, j * P:(j + 1) * P], start=(j == 0), stop=(j == i))
                    ins.then_inc(pv_done, 1)
                pe.wait_ge(asq_ready, h + 1)
                pe_roots(pe, HEAD_Q + h, HEAD_D + 8 * h, [k_h], v_h, SEQ, 4)

        def act_heads(act):
            with act.Fori(0, HEADS) as h:
                act.wait_ge(vk_t, 2 * h + 1)
                act.activation(v_nat, flat(4, 1024), ACT.Copy)
                act.activation(kv_s_nat[:, 1, ds(h, 1), :], ps[0:TS, 6:7, 0:P], ACT.Copy).then_inc(v_ev, 1)

                def exp(n):
                    i, w = n // 2, (n // 2 + 1) * P
                    act.wait_ge(nm_ready, 16 * h + n + 1)
                    if i >= 2:
                        act.wait_ge(pt_t, 8 * h + i - 1)
                    act.activation(prob[n % 4][:, 0:w], flat(2 * (n % 2), 1024)[:, 0:w], ACT.Exp,
                                   bias=neg_mx[:, n % 4:n % 4 + 1], scale=SCALE_DA,
                                   accum_out=lsum[:, n % 4:n % 4 + 1]).then_inc(p_ready, 1)
                exp(0)
                exp(1)

                def out(i):
                    act.wait_ge(pv_done, 8 * h + i + 1)
                    act.activation(att[:, i * P:(i + 1) * P], ps[:, 6 + i % 2, 0:P], ACT.Copy).then_inc(pv_ev, 1)
                for i in range(8):
                    if i < 7:
                        exp(2 * i + 2)
                        exp(2 * i + 3)
                    act.wait_ge(pt_t, 8 * h + i + 1)
                    if i >= 2:
                        act.wait_ge(pv_done, 8 * h + i - 1)
                    act.activation(prob_t[i % 2][:, 0:(i + 1) * P], flat(4, 1024)[:, 0:(i + 1) * P],
                                   ACT.Copy).then_inc(pt_ev, 1)
                    if i:
                        out(i - 1)
                out(7)
                act.wait_ge(pv_ev, 8 * h + 8)
                act.activation(k_h[:, 0:SEQ], att, ACT.Square).then_inc(asq_ready, 1)
                act_roots(act, HEAD_Q + h, 8)
                act.wait_ge(at_ready, h + 1)
                alone(act)
                act.activation(mix[:, 0, ds(HC + h, 1), 0:SEQ], one(q_h), ACT.Copy,
                               scale=gains[:, GS:GS + 1]).then_inc(mix_hi, 1)

        def dve_heads(dve, chain):
            per = 16 * 2 + 8 * 3 + 4
            with dve.Fori(0, HEADS) as h:
                chain.enter(h, per)

                def maxima(n):
                    i, w = n // 2, (n // 2 + 1) * P
                    s = flat(2 * (n % 2), 1024)
                    dve.wait_ge(s_done, 16 * h + n + 1)
                    chain.link(dve.tensor_tensor(s[:, i * P:w], s[:, i * P:w], causal[:, :], ALU.add))
                    chain.link(dve.tensor_reduce(mx[:, n % 2:n % 2 + 1], s[:, 0:w], AX.X, ALU.max))
                    dve.tensor_scalar(neg_mx[:, n % 4:n % 4 + 1], mx[:, n % 2:n % 2 + 1], -SCALE_DA, None,
                                      ALU.mult).then_inc(nm_ready, 1)
                maxima(0)
                maxima(1)
                dve.wait_ge(vk_t, 2 * h + 2)
                dve.tensor_copy(k_nat, flat(4, 1024))
                dve.tensor_copy(kv_s_nat[:, 0, ds(h, 1), :], ps[0:TS, 6:7, 0:P]).then_inc(k_ev, 1)
                for i in range(8):
                    if i < 7:
                        maxima(2 * i + 2)
                        maxima(2 * i + 3)
                    a, w = 2 * (i % 2), (i + 1) * P
                    dve.wait_ge(p_ready, 16 * h + 2 * i + 2)
                    dve.wait_ge(w_comb, 8 * h + i)
                    chain.link(dve.reciprocal(rl, lsum[:, a:a + 2]))
                    chain.link(dve.tensor_scalar(rl[:, 1:2], rl[:, 1:2], neg_lam, None, ALU.mult))
                    chain.link(dve.tensor_scalar(prob[a + 1][:, 0:w], prob[a + 1][:, 0:w], rl[:, 1:2], None, ALU.mult))
                    dve.scalar_tensor_tensor(prob[a][:, 0:w], prob[a][:, 0:w], rl[:, 0:1], prob[a + 1][:, 0:w],
                                             ALU.mult, ALU.add).then_inc(w_comb, 1)
                dve_roots(dve, chain, HEAD_Q + h, HEAD_D + 8 * h, v_h, SEQ, P * EPS)
                dve.tensor_tensor(q_h, att, flat(4, SEQ), ALU.mult).then_inc(at_ready, 1)
                dve.wait_ge(mix_hi, h + 1)
                dve.scalar_tensor_tensor(mix[:, 1, ds(HC + h, 1), 0:SEQ], one(q_h), gains[:, GS:GS + 1],
                                         mix[:, 0, ds(HC + h, 1), 0:SEQ], ALU.mult,
                                         ALU.subtract).then_inc(head_done, 1)
            chain.leave(HEADS)

        def load_pages(sp):
            sp.wait_ge(ids_loaded, 16)
            sp.wait_ge(mm_done, CXB + 12)
            with sp.Fori(0, NB // 2) as i:
                for f in range(4 * NPG):
                    b, cache = (f // NPG) % 2, cache_k if f < 2 * NPG else cache_v
                    n = (2 * i + b) * NPG + f % NPG
                    page = sp.value_load(page_ids[0:1, ds(n, 1)], min_val=0, max_val=cache_k.shape[1] - 1)
                    if f >= RING:
                        sp.wait_ge(page_used, 4 * NPG * i + f - RING + 1)
                    else:
                        sp.wait_ge(page_used, 4 * NPG * i)
                    alone(sp)
                    sp.dma_start(ring[:, f % RING, :],
                                 cache[0, ds(page, 1), :, :, :].rearrange("a t h e -> (a t) (h e)")
                                 ).then_inc(page_loaded[f % RING], 16)

        def pe_samples(pe):
            pe.wait_ge(qp_ready, 1)
            for h in range(HEADS):
                ins = pe.matmul(ps[0:TS, 0, h * 64:(h + 1) * 64], kT[:, h, SEQ:T], q_pages[:, :, h, :],
                                start=True, stop=True)
            ins.then_inc(self_done, 1)
            pe.wait_ge(self_ready, 1)
            with pe.Fori(0, NB // 2) as i:
                def page_ready(f):
                    pe.wait_ge(page_loaded[f % RING], 16 * (4 * NPG // RING * i + f // RING + 1))

                def key_page(f):
                    page_ready(f)
                    pe.wait_ge(kp_ev[f % 2], NPG * i + f // 2)
                    for h in range(HEADS):
                        ins = pe.transpose(ps[:, f % 2, h * P:(h + 1) * P], ring[:, f % RING, h * P:(h + 1) * P],
                                           ident[:, :])
                    ins.then_inc(page_used, 1)

                def key_scores(f):
                    pe.wait_ge(kp_ev[f % 2], NPG * i + f // 2 + 1)
                    b, p = f // NPG, f % NPG
                    if p == 0:
                        pe.wait_ge(sub_ready, 2 * i)
                    for h in range(HEADS):
                        ins = pe.matmul(ps[:, 2 + b, p * 32 + h * 8:p * 32 + h * 8 + 8],
                                        k_page_t[f % 2][:, h * P:(h + 1) * P],
                                        q_pages[:, ds(2 * i + b, 1), h, :].rearrange("p a n -> p (a n)"),
                                        start=True, stop=True)
                    ins.then_inc(kp_used, 1)

                def top(b):
                    pe.wait_ge(mx_ready, 2 * i + b + 1)
                    pe.wait_ge(sub_ready, 2 * i + b)
                    pe.wait_ge(rl_ready, 2 * i + b)
                    pe.transpose(ps[0:32, 6, 0:P], sm_max, ident[:, :]).then_inc(mx_t, 1)
                    pe.wait_ge(dg_ready, 2 * i + b + 1)
                    pe.matmul(ps[:, 7, 0:32], ones[0:32, :], sm_dg, start=True, stop=True).then_inc(mx_bc, 1)

                def values(b):
                    pe.wait_ge(ps_exp, 2 * i + b + 1)
                    pe.wait_ge(pvs_ev, 2 * i + b)
                    for p in range(NPG):
                        f = (2 + b) * NPG + p
                        page_ready(f)
                        for h in range(HEADS):
                            ins = pe.matmul(ps[:, 4 + b, h * 8:h * 8 + 8], ring[:, f % RING, h * P:(h + 1) * P],
                                            probs_s[b][:, p * 32 + h * 8:p * 32 + h * 8 + 8],
                                            start=(p == 0 and h == 0), stop=False, skip_group_check=True)
                        ins.then_inc(page_used, 1)
                    for h in range(HEADS):
                        ins = pe.matmul(ps[:, 4 + b, h * 8:h * 8 + 8], kv_s_nat[:, 1, h, :],
                                        probs_s[b][0:TS, 512 + h * 8:512 + h * 8 + 8],
                                        start=False, stop=(h == HEADS - 1), skip_group_check=True)
                    ins.then_inc(pvs_done, 1)

                def total(b):
                    pe.wait_ge(sum_ready, 2 * i + b + 1)
                    pe.matmul(ps[:, 6, 0:32], ones[:, :], sm_sum, start=True, stop=True).then_inc(sum_bc, 1)

                for b in range(2):
                    for p in range(NPG):
                        f = b * NPG + p
                        key_page(f)
                        if p:
                            key_scores(f - 1)
                        if b and p == 4:
                            top(0)
                        if b and p == 12:
                            total(0)
                    key_scores(b * NPG + NPG - 1)
                values(0)
                top(1)
                total(1)
                values(1)
            pe.wait_ge(asq_ready, HEADS + 1)
            pe_roots(pe, SAMPLE_Q, SAMPLE_D, [arena[:, 26, 0:P]], arena[:, 26, P:2 * P], P, 4)

        def evac_page(eng, i, f):
            eng.wait_ge(kp_used, 2 * NPG * i + f - 1) if f >= 2 else eng.wait_ge(kp_used, 2 * NPG * i)
            eng.wait_ge(page_used, 4 * NPG * i + f + 1)

        def act_samples(act):
            with act.Fori(0, NB // 2) as i:
                def exp(b):
                    act.wait_ge(sub_ready, 2 * i + b + 1)
                    act.activation(probs_s[b][:, 0:512], probs_s[b][:, 0:512], ACT.Exp, scale=SCALE_DA)
                    act.activation(probs_s[b][0:TS, 512:544], probs_s[b][0:TS, 512:544], ACT.Exp,
                                   scale=SCALE_DA).then_inc(ps_exp, 1)
                for f in range(0, 2 * NPG, 2):
                    evac_page(act, i, f)
                    act.activation(k_page_t[0], ps[:, 0, :], ACT.Copy).then_inc(kp_ev[0], 1)
                    if f == NPG + 6:
                        exp(0)
                exp(1)
            act.wait_ge(pvs_ev, NB)
            act.activation(arena[:, 26, 0:P], arena[:, 24, 0:P], ACT.Square).then_inc(asq_ready, 1)
            act_roots(act, SAMPLE_Q, 1)
            act.wait_ge(at_ready, HEADS + 1)
            act.activation(mix[:, 0, HC:KD, SEQ:T], arena[:, 27, 0:P].rearrange("p (h t) -> p h t", h=HEADS), ACT.Copy,
                           scale=gains[:, GS:GS + 1]).then_inc(mix_hi, 1)

        def dve_samples(dve, chain):
            dve.wait_ge(kv_stored, 32 * HEADS)
            chain.link(dve.memset(q_pages[:, :, :, :], 0.0))
            for c in range(2):
                q = qT[64 * c:64 * c + 64, :, SEQ:T].rearrange("p h (b t) -> p b h t", b=NB)
                ins = dve.tensor_copy(q_pages[64 * c:64 * c + 64, :, :, NS * c:NS * c + NS], q)
                if c == 0:
                    chain.link(ins)
            ins.then_inc(qp_ready, 1)
            dve.wait_ge(self_done, 1)
            dve.tensor_tensor(self_s, ps[0:TS, 0, 0:256].rearrange("p (h n) -> p h n", h=HEADS),
                              smask[:, :].rearrange("p (a n) -> p a n", a=1).to_broadcast([TS, HEADS, 64]),
                              ALU.add).then_inc(self_ready, 1)
            dve.wait_ge(self_ready, 1)
            per = 2 * 5
            with dve.Fori(0, NB // 2) as i:
                chain.enter(i, per)

                def own(b):
                    return self_s[:, :, ds(16 * i + 8 * b, 8)]

                def max_a(b):
                    dve.wait_ge(kp_used, 2 * NPG * i + NPG * (b + 1))
                    chain.link(dve.tensor_reduce(sm_max, ps[:, 2 + b, :].rearrange("p (g n) -> p n g", n=32), AX.X,
                                                 ALU.max))
                    m = sm_max[0:TS, :].rearrange("p (h n) -> p h n", h=HEADS)
                    dve.tensor_tensor(m, m, own(b), ALU.max).then_inc(mx_ready, 1)
                    dve.wait_ge(mx_t, 2 * i + b + 1)
                    chain.link(dve.tensor_reduce(sm_col, ps[0:32, 6, 0:P], AX.X, ALU.max))
                    dve.tensor_scalar(sm_dg, ident[0:32, 0:32], sm_col, None, ALU.mult).then_inc(dg_ready, 1)
                    dve.wait_ge(mx_bc, 2 * i + b + 1)
                    chain.link(dve.tensor_copy(sm_bc, ps[:, 7, 0:32]))
                    if b == 0:
                        dve.wait_ge(pvs_done, 2 * i)
                    dve.tensor_tensor(probs_s[b][:, 0:512].rearrange("p (g n) -> p g n", n=32),
                                      ps[:, 2 + b, :].rearrange("p (g n) -> p g n", n=32),
                                      sm_bc.rearrange("p (a n) -> p a n", a=1).to_broadcast([P, NPG, 32]),
                                      ALU.subtract)
                    dve.tensor_tensor(probs_s[b][0:TS, 512:544].rearrange("p (h n) -> p h n", h=HEADS), own(b),
                                      sm_bc[0:TS, :].rearrange("p (h n) -> p h n", h=HEADS),
                                      ALU.subtract).then_inc(sub_ready, 1)

                def sums(b):
                    dve.wait_ge(ps_exp, 2 * i + b + 1)
                    chain.link(dve.tensor_reduce(sm_sum, probs_s[b][:, 0:512].rearrange("p (g n) -> p n g", n=32),
                                                 AX.X, ALU.add))
                    dve.tensor_tensor(sm_sum[0:TS, :], sm_sum[0:TS, :], probs_s[b][0:TS, 512:544],
                                      ALU.add).then_inc(sum_ready, 1)
                    dve.wait_ge(sum_bc, 2 * i + b + 1)
                    dve.reciprocal(sm_rl, ps[:, 6, 0:32]).then_inc(rl_ready, 1)

                def out(b):
                    dve.wait_ge(rl_ready, 2 * i + b + 1)
                    dve.wait_ge(pvs_done, 2 * i + b + 1)
                    chain.link(dve.tensor_tensor(sm_o, ps[:, 4 + b, 0:32], sm_rl, ALU.mult))
                    o = sm_o.rearrange("p (h c t) -> p h c t", h=HEADS, c=2)
                    dve.scalar_tensor_tensor(att_s[:, :, ds(8 * i + 4 * b, 4)], o[:, :, 1, :], neg_lam,
                                             o[:, :, 0, :], ALU.mult, ALU.add).then_inc(pvs_ev, 1)

                for f in range(1, 2 * NPG, 2):
                    evac_page(dve, i, f)
                    dve.tensor_copy(k_page_t[1], ps[:, 1, :]).then_inc(kp_ev[1], 1)
                    if f == NPG + 3:
                        max_a(0)
                    if f == NPG + 11:
                        sums(0)
                out(0)
                max_a(1)
                sums(1)
                out(1)
            chain.leave(NB // 2)
            dve_roots(dve, chain, SAMPLE_Q, SAMPLE_D, arena[:, 26, P:2 * P], P, P * EPS)
            dve.wait_ge(pvs_ev, NB)
            t = arena[:, 27, 0:P]
            dve.tensor_tensor(t, arena[:, 24, 0:P], flat(4, P), ALU.mult).then_inc(at_ready, 1)
            dve.wait_ge(mix_hi, HEADS + 1)
            dve.scalar_tensor_tensor(mix[:, 1, HC:KD, SEQ:T], t.rearrange("p (h t) -> p h t", h=HEADS),
                                     gains[:, GS:GS + 1], mix[:, 0, HC:KD, SEQ:T], ALU.mult,
                                     ALU.subtract).then_inc(mix_ready, 1)

        hn = mix
        q1, k1, v1, o1 = rows(8, 2), rows(10, 2), rows(12, 2), rows(14, 2)
        flat_rows = lambda a, n: rows(a, n).rearrange("p a t -> p (a t)")
        wk = flat_rows(16, 3)[:, 0:NTT * MLD].rearrange("p (c d) -> p c d", c=NTT)
        vn = flat_rows(19, 4)[:, 0:NTT * 384].rearrange("p (c e) -> p c e", c=NTT)
        m_bc, i_bc, e_bc = arena[:, 23, :], arena[:, 24, :], arena[:, 25, :]
        state = [flat_rows(26, 2)[:, 768 * i:768 * (i + 1)].rearrange("p (k e) -> p k e", k=2) for i in range(2)]
        sd = flat_rows(10, 2)[:, 0:NTT * P]
        dec = flat_rows(12, 2)[:, 0:NTT * P]
        hcell = v1
        m_row, i_row, e_row = (hT[0:HEADS, k, :] for k in range(3))
        cs = [hT[:, 3 + i, 0:768].rearrange("p (k e) -> p k e", k=2) for i in range(2)]
        cs_new = [hT[:, 5 + i, 0:768].rearrange("p (k e) -> p k e", k=2) for i in range(2)]
        wk_b = [hT[0:TS, 7, MLD * i:MLD * (i + 1)] for i in range(2)]
        den_, rec_ = hT[:, 3, 768:896], hT[:, 5, 768:896]
        intra = hT[:, 7, 512:608]
        n_nat = hT[0:1 + NB, 7, 640:896]
        r = lambda k: arena[0:HEADS, k, :]
        li, fx, fa, fe, fl, bc, aa, we, mt = (r(16 + k) for k in range(9))
        acol = sb("acol", [P, 2, NTT, HEADS])
        a_h = sb("a_h", [P, 2, NTT])
        sel_h = sb("sel_h", [HEADS, P])
        reset = hT[0:HEADS, 4, :]
        m_prev = sb("m_prev", [HEADS, 16])
        m_last = sb("m_last", [HEADS, 16])
        m_out = sb("m_out", [HEADS, 1 + NB])
        decay = sb("decay", [HEADS, 16])
        d_h = sb("d_h", [P, 16])
        b_if = sb("b_if", [HEADS, 2])
        nT = sb("nT", [P, NB, HEADS, 2])
        n_h = sb("n_h", [P, NB, 2])
        n_new = sb("n_new", [P, 2, 1 + NB])
        g_h = sb("g_h", [P, 2])
        spill = nc.dram_tensor("h_spill", (P, KD, T), F32, kind="Internal").ap()

        bif_loaded, m0_loaded = sem("bif_loaded"), sem("m0_loaded")
        r_act, r_dve = sem("r_act"), sem("r_dve")
        col_t, col_ev = sem("col_t"), sem("col_ev")
        rows_ready = sem("rows_ready")
        m_stored = sem("m_stored")
        selh_ready = sem("selh_ready")
        bc_t, bc_act, bc_dve = sem("bc_t"), sem("bc_act"), sem("bc_dve")
        kn_t, kn_ev, vn_t, vn_ev = sem("kn_t"), sem("kn_ev"), sem("vn_t"), sem("vn_ev")
        st_done, dx_ready, dec_ready, sd_ready, qi_ready = (sem(n) for n in ("st_done", "dx_ready", "dec_ready",
                                                                             "sd_ready", "qi_ready"))
        up_done, state_ready, num_done, num_ev = sem("up_done"), sem("state_ready"), sem("num_done"), sem("num_ev")
        cs_loaded, nc_ready, wkb_ready = [sem("cs_loaded0"), sem("cs_loaded1")], sem("nc_ready"), sem("wkb_ready")
        intra_done, intra_ev, inter_done = sem("intra_done"), sem("intra_ev"), sem("inter_done")
        ups_done, cs_ready, cs_stored = sem("ups_done"), sem("cs_ready"), [sem("cs_stored0"), sem("cs_stored1")]
        state_stored, n_made, n_t, n_ev, n_stored = sem("state_stored"), sem("n_made"), sem("n_t"), sem("n_ev"), sem("n_stored")
        hc_ready, mean_done, hd_ready, hsq_ready = (sem(n) for n in ("hc_ready", "mean_done", "hd_ready", "hsq_ready"))
        hn_ready, hn_hi, hn_done = sem("hn_ready"), sem("hn_hi"), sem("hn_done")

        def chunks(row):
            return row[:, 0:SEQ].rearrange("p (c t) -> p c t", t=P)

        def samples(row):
            return row[:, SEQ:T].rearrange("p (b t) -> p b t", b=NB)

        def pe_gates(pe):
            pe.wait_ge(u_ready, KD * 3)
            pe.wait_ge(evac[1], GATES // 2)
            products(pe, GATES, 0, u, KD, m=HEADS, n=8, col=0, bank=0, signal=False)
            products(pe, GATES, 0, u, KD, m=HEADS, n=8, col=HEADS, bank=3)
            pe.wait_ge(evac[0], GATES // 2 + 1)
            pe.wait_ge(rows_ready, 1)
            for k, src in enumerate((aa, we)):
                for c in range(NTT):
                    w = P if c < NTT - 1 else TS
                    ins = pe.transpose(ps[0:w, 6, (k * NTT + c) * HEADS:(k * NTT + c + 1) * HEADS],
                                       src[:, c * P:c * P + w], ident[0:HEADS, 0:HEADS])
            ins.then_inc(col_t, 1)

        def act_gates(act, chain):
            split_hi(act, QKVO, 0, KD)
            act.wait_ge(mm_done, GATES + 1)
            act.wait_ge(bif_loaded, 16)
            act.activation(by3(li), ps[0:HEADS, 0:3, 0:GW], ACT.Identity, scale=1 / WS, bias=b_if[:, 0:1])
            act.activation(by3(fx), ps[0:HEADS, 3:6, 0:GW], ACT.Identity, scale=1 / WS,
                           bias=b_if[:, 1:2]).then_inc(evac[0], 1)
            act.wait_ge(r_dve, 1)
            chain.link(act.activation(fe, fa, ACT.Exp, scale=-1.0))
            act.activation(fl, fe, ACT.Ln, bias=1.0).then_inc(r_act, 1)
            act.wait_ge(r_dve, 2)
            act.activation(we, we, ACT.Exp)
            act.activation(i_row, i_row, ACT.Exp)
            act.activation(decay[:, :], decay[:, :], ACT.Exp)
            act.activation(e_row, mt, ACT.Exp, scale=-1.0).then_inc(rows_ready, 1)

        def dve_gates(dve, chain):
            split_lo(dve, QKVO, 0, KD)
            dve.wait_ge(spilled, 16)
            chain.link(dve.memset(reset, 1.0))
            dve.memset(chunks(reset)[:, :, 0:1], 0.0)
            chain.mark(dve.memset(samples(reset)[:, :, 0:1], 0.0))
            chain.mark(dve.memset(m_prev[:, 0:1], 0.0))
            chain.mark(dve.memset(acol[:, :, :, :], 0.0))
            dve.wait_ge(evac[0], GATES // 2 + 1)
            dve.scalar_tensor_tensor(fa, fx, -1.0, fx, ALU.mult, ALU.max).then_inc(r_dve, 1)
            chain.link(dve.tensor_scalar(mt, fx, 0.0, None, ALU.min))
            dve.wait_ge(r_act, 1)
            chain.link(dve.tensor_tensor(fl, mt, fl, ALU.subtract))
            chain.link(dve.tensor_tensor_scan(bc, reset, fl, 0.0, ALU.mult, ALU.add))
            chain.link(dve.tensor_tensor(aa, li, bc, ALU.subtract))
            dve.wait_ge(m0_loaded, 16)
            for c in range(8):
                m_c, a_c = m_row[:, c * P:(c + 1) * P], aa[:, c * P:(c + 1) * P]
                chain.link(dve.tensor_tensor_scan(m_c, a_c, a_c, m_prev[:, c:c + 1], ALU.max, ALU.max))
                if c < 7:
                    chain.link(dve.tensor_tensor(m_prev[:, c + 1:c + 2], bc[:, c * P + P - 1:c * P + P],
                                                 m_row[:, c * P + P - 1:c * P + P], ALU.add))
            for t in range(NS):
                before = m_prev[:, 8:16] if t == 0 else samples(m_row)[:, :, t - 1]
                chain.link(dve.tensor_tensor(samples(m_row)[:, :, t], before, samples(aa)[:, :, t], ALU.max))
            chain.mark(dve.tensor_copy(m_last[:, 0:8], chunks(m_row)[:, :, P - 1]))
            chain.link(dve.tensor_copy(m_last[:, 8:16], samples(m_row)[:, :, NS - 1]))
            dve.tensor_tensor(chunks(we), chunks(aa), m_last[:, 0:8].rearrange("p (c a) -> p c a", a=1).to_broadcast(
                [HEADS, 8, P]), ALU.subtract)
            dve.tensor_tensor(samples(we), samples(aa), m_last[:, 8:16].rearrange("p (c a) -> p c a", a=1)
                              .to_broadcast([HEADS, NB, NS]), ALU.subtract)
            dve.tensor_tensor(chunks(i_row), m_prev[:, 0:8].rearrange("p (c a) -> p c a", a=1).to_broadcast(
                [HEADS, 8, P]), chunks(m_row), ALU.subtract)
            dve.tensor_tensor(samples(i_row), m_prev[:, 8:16].rearrange("p (c a) -> p c a", a=1).to_broadcast(
                [HEADS, NB, NS]), samples(m_row), ALU.subtract)
            dve.tensor_tensor(decay[:, :], m_prev[:, :], m_last[:, :], ALU.subtract)
            chain.link(dve.tensor_tensor(mt, bc, m_row, ALU.add))
            dve.tensor_copy(m_out[:, 0:1], mt[:, SEQ - 1:SEQ])
            dve.tensor_copy(m_out[:, 1:1 + NB], samples(mt)[:, :, NS - 1]).then_inc(r_dve, 1)
            dve.wait_ge(col_t, 1)
            dve.tensor_copy(acol[:, :, 0:8, :], ps[:, 6, 0:2 * NTT * HEADS].rearrange(
                "p (k c h) -> p k c h", k=2, c=NTT)[:, :, 0:8, :])
            chain.mark(dve.tensor_copy(acol[0:TS, :, 8:9, :], ps[0:TS, 6, 0:2 * NTT * HEADS].rearrange(
                "p (k c h) -> p k c h", k=2, c=NTT)[:, :, 8:9, :]))
            chain.mark(dve.memset(vn[:, :, MLD:384], 1.0))
            chain.sync()

        def head_src(h, m):
            return w_cols(w_in1[0], ds((m // 2) * D + (m % 2) * P + h * MLD, P))

        def act_mlstm(act):
            with act.Fori(0, HEADS) as h:
                for m in range(8):
                    c, r_ = QKVO + m, 4 * h
                    split_hi(act, c + 1, r_, KD)
                    if m in (2, 3):
                        continue
                    act.wait_ge(mm_done, at(c, r_))
                    if m == 0:
                        act.wait_ge(hn_done, h)
                    dst = {0: q1, 4: v1, 6: o1}[m - m % 2][:, m % 2, :]
                    act.activation(by3(dst), group(3 * (c % 2)), ACT.Sigmoid if m >= 6 else ACT.Copy,
                                   scale=1 / WS).then_inc(evac[c % 2], 1)
                act.wait_ge(bc_t, 4 * h + 1)
                act.activation(by3(m_bc), group(0), ACT.Copy).then_inc(bc_act, 1)
                act.wait_ge(bc_t, 4 * h + 3)
                act.activation(by3(e_bc), group(0), ACT.Copy).then_inc(bc_act, 1)
                for t in range(5):
                    act.wait_ge(vn_t, 5 * h + t + 1)
                    if t < 4:
                        act.activation(vn[:, 2 * t:2 * t + 2, 0:MLD],
                                       ps[:, 7, :].rearrange("p (a e) -> p a e", a=2), ACT.Copy).then_inc(vn_ev, 1)
                    else:
                        act.activation(vn[0:TS, 8, 0:MLD], ps[0:TS, 7, 0:MLD], ACT.Copy).then_inc(vn_ev, 1)
                act.wait_ge(dx_ready, h + 1)
                act.activation(dec[:, 0:SEQ], dec[:, 0:SEQ], ACT.Exp, scale=-1.0)
                act.activation(dec[0:TS, SEQ:SEQ + TS], dec[0:TS, SEQ:SEQ + TS], ACT.Exp,
                               scale=-1.0).then_inc(dec_ready, 1)
                for b in range(NB):
                    act.wait_ge(inter_done, NB * h + b - 1) if b >= 2 else act.wait_ge(inter_done, NB * h)
                    act.wait_ge(cs_ready, NB * h + b - 1) if b >= 2 else act.wait_ge(cs_ready, NB * h)
                    if b == 0:
                        act.wait_ge(selh_ready, h + 1)
                    act.activation(cs[b % 2][:, :, MLD:384],
                                   n_h[:, b, :].rearrange("p (k a) -> p k a", a=1).to_broadcast([P, 2, P]),
                                   ACT.Copy).then_inc(nc_ready, 1)
                act.wait_ge(hd_ready, h + 1)
                act.activation(k1[:, :, :], hcell[:, :, :], ACT.Square).then_inc(hsq_ready, 1)
                act_roots(act, ML_Q + h, NTT)
                for k in range(2):
                    act.wait_ge(hn_ready, 2 * h + k + 1)
                    alone(act)
                    act.activation(hn[:, 0, ds(2 * h + k, 1), :], q1[:, k:k + 1, :], ACT.Copy,
                                   scale=g_h[:, k:k + 1]).then_inc(hn_hi, 1)

        def pe_mlstm(pe):
            with pe.Fori(0, HEADS) as h:
                for m in range(8):
                    if m == 0:
                        pe.wait_ge(hn_done, h)
                    products(pe, QKVO + m, 4 * h, u, KD)
                pe.wait_ge(selh_ready, h + 1)
                pe.wait_ge(evac[0], out_of_banks(QKVO + 7, 4 * h))
                pe.wait_ge(evac[1], out_of_banks(QKVO + 6, 4 * h))
                for n, (src, bank) in enumerate(((m_row, 0), (i_row, 3), (e_row, 0))):
                    if n == 2:
                        pe.wait_ge(bc_act, 2 * h + 1)
                    for g in range(3):
                        ins = pe.matmul(ps[:, bank + g, 0:GW], sel_h[:, :], src[:, g * GW:(g + 1) * GW],
                                        start=True, stop=True)
                    ins.then_inc(bc_t, 1)
                pe.matmul(ps[:, 6, 0:16], sel_h[:, :], decay[:, :], start=True, stop=True).then_inc(bc_t, 1)
                for t in range(5):
                    for src, bank, done, out in ((k1, 6, kn_t, kn_ev), (v1, 7, vn_t, vn_ev)):
                        if bank == 6 and t == 0:
                            pe.wait_ge(bc_dve, 2 * h + 2)
                        else:
                            pe.wait_ge(out, 5 * h + t)
                        for tt in range(2 * t, min(2 * t + 2, NTT)):
                            w = P if tt < NTT - 1 else TS
                            for k in range(2):
                                o = (tt % 2) * MLD + k * P
                                ins = pe.transpose(ps[0:w, bank, o:o + P], src[:, k, tt * P:tt * P + w], ident[:, :])
                        ins.then_inc(done, 1)
                pe.wait_ge(bc_act, 2 * h + 2)
                for c in range(NTT):
                    w = P if c < NTT - 1 else TS
                    for k in range(2):
                        ins = pe.matmul(ps[0:w, c // 4, (c % 4) * P:(c % 4) * P + w], k1[:, k, c * P:c * P + w],
                                        q1[:, k, c * P:c * P + w], start=(k == 0), stop=(k == 1))
                ins.then_inc(st_done, 1)
                pe.wait_ge(kn_ev, 5 * h + 5)
                pe.wait_ge(vn_ev, 5 * h + 5)
                pe.wait_ge(bc_dve, 2 * h + 1)

                def update(c):
                    if c >= 2:
                        pe.wait_ge(state_ready, 8 * h + c - 1)
                    for k in range(2):
                        ins = pe.matmul(ps[:, 3 + 2 * (c % 2) + k, 0:384], wk[:, c, k * P:(k + 1) * P], vn[:, c, :],
                                        start=True, stop=True)
                    ins.then_inc(up_done, 1)

                def numerators(c):
                    if c == 0:
                        pe.wait_ge(sd_ready, h + 1)
                        pe.wait_ge(qi_ready, h + 1)
                    else:
                        pe.wait_ge(state_ready, 8 * h + c)
                    if c >= 2:
                        pe.wait_ge(num_ev, 8 * h + c - 1)
                    bank = 7 if c % 2 == 0 else 0
                    for j in range(3):
                        o = ps[:, bank, j * P:(j + 1) * P]
                        for k in range(2 if c else 0):
                            pe.matmul(o, state[c % 2][:, k, j * P:(j + 1) * P], q1[:, k, c * P:(c + 1) * P],
                                      start=(k == 0), stop=False)
                        ins = pe.matmul(o, vn[:, c, j * P:(j + 1) * P], sd[:, c * P:(c + 1) * P],
                                        start=(c == 0), stop=True)
                    ins.then_inc(num_done, 1)
                update(0)
                for c in range(8):
                    if c < 7:
                        update(c + 1)
                    numerators(c)
                for j in range(3):
                    ins = pe.matmul(ps[:, 1, j * TS:(j + 1) * TS], vn[0:TS, 8, j * P:(j + 1) * P],
                                    sd[0:TS, SEQ:SEQ + TS], start=True, stop=True)
                ins.then_inc(intra_done, 1)
                for b in range(NB):
                    pe.wait_ge(cs_loaded[b % 2], 16 * (NB // 2 * h + b // 2 + 1))
                    pe.wait_ge(nc_ready, NB * h + b + 1)
                    for j in range(3):
                        for k in range(2):
                            ins = pe.matmul(ps[:, 2, j * TS + NS * b:j * TS + NS * b + NS],
                                            cs[b % 2][:, k, j * P:(j + 1) * P],
                                            q1[:, k, SEQ + NS * b:SEQ + NS * b + NS], start=(k == 0), stop=(k == 1))
                    ins.then_inc(inter_done, 1)
                    pe.wait_ge(wkb_ready, NB * h + b + 1)
                    if b < 2:
                        pe.wait_ge(state_ready, 8 * h + 7 + b)
                    else:
                        pe.wait_ge(cs_ready, NB * h + b - 1)
                    for k in range(2):
                        ins = pe.matmul(ps[:, 3 + 2 * (b % 2) + k, 0:384], wk_b[b % 2][:, k * P:(k + 1) * P],
                                        vn[0:TS, 8, :], start=True, stop=True)
                    ins.then_inc(ups_done, 1)
                pe.wait_ge(n_made, h + 1)
                for k in range(2):
                    ins = pe.transpose(ps[0:1 + NB, 7, k * P:(k + 1) * P], n_new[:, k, :], ident[:, :])
                ins.then_inc(n_t, 1)
                pe.wait_ge(hc_ready, h + 1)
                for g in range(3):
                    for k in range(2):
                        ins = pe.matmul(ps[:, g, 0:GW], ones[:, :], hcell[:, k, g * GW:(g + 1) * GW],
                                        start=(k == 0), stop=(k == 1))
                ins.then_inc(mean_done, 1)
                pe.wait_ge(hsq_ready, h + 1)
                pe_roots(pe, ML_Q + h, ML_D + 9 * h, [k1[:, 0, :], k1[:, 1, :]], i_bc, T, 3)

        def dve_mlstm(dve, chain):
            per = 42
            with dve.Fori(0, HEADS) as h:
                chain.enter(h, per)
                dve.wait_ge(hn_done, h)
                dve.tensor_copy(sel_h[:, :].rearrange("p (a n) -> p a n", a=1), sel[:, ds(h, 1), :])
                dve.tensor_copy(a_h[:, :, :], acol[:, :, :, ds(h, 1)].rearrange("p k c a -> p k (c a)"))
                dve.tensor_copy(g_h[:, :], gains[:, ds(GM + 2 * h, 2)])
                dve.tensor_copy(n_h[:, :, :], nT[:, :, ds(h, 1), :].rearrange("p b a k -> p (b a) k")).then_inc(
                    selh_ready, 1)
                for m in range(8):
                    c, r_ = QKVO + m, 4 * h
                    split_lo(dve, c + 1, r_, KD)
                    if m in (2, 3):
                        dve.wait_ge(mm_done, at(c, r_))
                        dve.tensor_scalar(by3(k1[:, m % 2, :]), group(3 * (c % 2)), MLD ** -0.5 / WS, None,
                                          ALU.mult).then_inc(evac[c % 2], 1)
                dve.wait_ge(selh_ready, h + 1)
                dve.wait_ge(bc_t, 4 * h + 2)
                dve.tensor_copy(by3(i_bc), group(3)).then_inc(bc_dve, 1)
                dve.wait_ge(bc_t, 4 * h + 4)
                dve.tensor_copy(d_h[:, :], ps[:, 6, 0:16]).then_inc(bc_dve, 1)
                dve.wait_ge(bc_dve, 2 * h + 2)
                for t in range(5):
                    dve.wait_ge(kn_t, 5 * h + t + 1)
                    for tt in range(2 * t, min(2 * t + 2, NTT)):
                        w = P if tt < NTT - 1 else TS
                        ins = dve.tensor_scalar(wk[0:w, tt, :], ps[0:w, 6, (tt % 2) * MLD:(tt % 2 + 1) * MLD],
                                                a_h[0:w, 1, tt:tt + 1], None, ALU.mult)
                    ins.then_inc(kn_ev, 1)
                dve.wait_ge(bc_act, 2 * h + 1)
                dve.wait_ge(vn_t, 5 * h + 5)
                for c in range(8):
                    dve.scalar_tensor_tensor(dec[:, c * P:(c + 1) * P], m_bc[:, c * P:(c + 1) * P], a_h[:, 0, c:c + 1],
                                             dmask[:, :], ALU.subtract, ALU.max)
                dve.scalar_tensor_tensor(dec[0:TS, SEQ:SEQ + TS], m_bc[0:TS, SEQ:T], a_h[0:TS, 0, 8:9],
                                         dmask_s[:, :], ALU.subtract, ALU.max).then_inc(dx_ready, 1)
                dve.wait_ge(st_done, h + 1)
                for k in range(2):
                    ins = dve.tensor_tensor(q1[:, k, :], q1[:, k, :], i_bc, ALU.mult)
                ins.then_inc(qi_ready, 1)
                dve.wait_ge(dec_ready, h + 1)
                dve.wait_ge(kn_t, 5 * h + 5)
                dve.tensor_tensor(sd[:, 0:SEQ], flat(0, 1024), dec[:, 0:SEQ], ALU.mult)
                dve.tensor_tensor(sd[0:TS, SEQ:SEQ + TS], ps[0:TS, 2, 0:TS], dec[0:TS, SEQ:SEQ + TS],
                                  ALU.mult).then_inc(sd_ready, 1)

                def ratio(den, num, ecol, out, done):
                    w = ecol.shape[1]
                    chain.link(dve.tensor_tensor(den_[:, 0:w], den, ecol, ALU.max))
                    chain.link(dve.scalar_tensor_tensor(den_[:, 0:w], den, -1.0, den_[:, 0:w], ALU.mult, ALU.max))
                    chain.link(dve.reciprocal(rec_[:, 0:w], den_[:, 0:w]))
                    ins = dve.tensor_tensor(out, num, one(rec_[:, 0:w]).to_broadcast([P, 2, w]), ALU.mult)
                    ins.then_inc(done, 1) if done else chain.mark(ins)

                def next_state(c):
                    dve.wait_ge(up_done, 8 * h + c + 1)
                    up = ps[:, 3 + 2 * (c % 2):5 + 2 * (c % 2), 0:384]
                    if c >= 2:
                        dve.wait_ge(num_done, 8 * h + c)
                    if c == 0:
                        dve.wait_ge(state_stored, 16 * h)
                        dve.tensor_copy(state[1], up).then_inc(state_ready, 1)
                    else:
                        dve.wait_ge(state_ready, 8 * h + c)
                        dve.scalar_tensor_tensor(state[(c + 1) % 2], state[c % 2], d_h[:, c:c + 1], up, ALU.mult,
                                                 ALU.add).then_inc(state_ready, 1)
                for c in range(8):
                    next_state(c)
                    dve.wait_ge(num_done, 8 * h + c + 1)
                    bank = 7 if c % 2 == 0 else 0
                    ratio(ps[:, bank, 256:384], ps[:, bank, 0:256].rearrange("p (a t) -> p a t", a=2),
                          e_bc[:, c * P:(c + 1) * P], hcell[:, :, c * P:(c + 1) * P], num_ev)
                dve.wait_ge(state_ready, 8 * h + 8)
                dve.wait_ge(n_t, h)
                chain.mark(dve.tensor_copy(n_new[:, :, 0:1], state[0][:, :, MLD:MLD + 1]))
                dve.wait_ge(intra_done, h + 1)
                chain.mark(dve.tensor_copy(intra, ps[:, 1, 0:96]))
                for b in range(NB):
                    if b >= 2:
                        dve.wait_ge(ups_done, NB * h + b - 1)
                    dve.wait_ge(kn_ev, 5 * h + 5)
                    dve.tensor_scalar(wk_b[b % 2], wk[0:TS, 8, :], bmask[:, b:b + 1], None, ALU.mult).then_inc(
                        wkb_ready, 1)
                    dve.wait_ge(ups_done, NB * h + b + 1)
                    dve.wait_ge(cs_stored[b % 2], 16 * (NB // 2 * h + b // 2))
                    dve.scalar_tensor_tensor(cs_new[b % 2], cs[b % 2], d_h[:, 8 + b:9 + b],
                                             ps[:, 3 + 2 * (b % 2):5 + 2 * (b % 2), 0:384], ALU.mult,
                                             ALU.add).then_inc(cs_ready, 1)
                    dve.wait_ge(cs_ready, NB * h + b + 1)
                    ins = dve.tensor_copy(n_new[:, :, 1 + b:2 + b], cs_new[b % 2][:, :, MLD:MLD + 1])
                    ins.then_inc(n_made, 1) if b == NB - 1 else chain.mark(ins)
                chain.sync()
                dve.wait_ge(inter_done, NB * h + NB)
                chain.link(dve.tensor_tensor(intra, intra, ps[:, 2, 0:96], ALU.add))
                ratio(intra[:, 64:96], intra[:, 0:64].rearrange("p (a t) -> p a t", a=2), e_bc[:, SEQ:T],
                      hcell[:, :, SEQ:T], None)
                dve.wait_ge(n_t, h + 1)
                dve.wait_ge(n_stored, 32 * h)
                dve.tensor_copy(n_nat, ps[0:1 + NB, 7, 0:MLD]).then_inc(n_ev, 1)
                chain.sync()
                dve.wait_ge(num_ev, 8 * h + 8)
                dve.tensor_tensor(hcell[:, :, :], hcell[:, :, :], o1[:, :, :], ALU.mult).then_inc(hc_ready, 1)
                dve.wait_ge(hc_ready, h + 1)
                dve.wait_ge(mean_done, h + 1)
                for k in range(2):
                    ins = dve.scalar_tensor_tensor(by3(hcell[:, k, :]), group(0), -1.0 / MLD, by3(hcell[:, k, :]),
                                                   ALU.mult, ALU.add)
                ins.then_inc(hd_ready, 1)
                dve.wait_ge(hd_ready, h + 1)
                dve_roots(dve, chain, ML_Q + h, ML_D + 9 * h, i_bc, T, MLD * EPS)
                for k in range(2):
                    dve.tensor_tensor(q1[:, k, :], hcell[:, k, :], flat(3, T), ALU.mult).then_inc(hn_ready, 1)
                for k in range(2):
                    dve.wait_ge(hn_hi, 2 * h + k + 1)
                    ins = dve.scalar_tensor_tensor(hn[:, 1, ds(2 * h + k, 1), :], q1[:, k:k + 1, :], g_h[:, k:k + 1],
                                                   hn[:, 0, ds(2 * h + k, 1), :], ALU.mult, ALU.subtract)
                ins.then_inc(hn_done, 1)
            chain.leave(HEADS)

        nat = arena[:, 27, :]
        gains_nat, sc_nat, n_rows = nat[0:85, 0:P], nat[0:2 * NB, 128:128 + CH], nat[0:64, 640:768]
        conv_nat = arena[0:2 + 2 * NB, 26, 0:CH]
        conv_t, conv_ev, own_stored = sem("conv_t"), sem("conv_ev"), sem("own_stored")

        block = ctx.enter_context(nc.Block())

        @block.sync
        def _(sp):
            for tt in range(NTT):
                w = P if tt < NTT - 1 else TS
                src = x_p[0, tt * P:tt * P + w, :] if tt < NTT - 1 else x_s.rearrange("b t d -> (b t) d")
                sp.dma_start(arena[0:w, tt, 0:D], src).then_inc(x_loaded[tt], 16)
                if tt == 1:
                    sp.dma_start(gains_nat[0:64, :], norms.rearrange("l n (k p) -> (l n k) p", p=P)).then_inc(
                        gain_loaded, 16)
                    sp.dma_start(gains_nat[64:72, :], mh_g1.rearrange("a (k p) -> (a k) p", p=P)).then_inc(
                        gain_loaded, 16)
                    sp.dma_start(gains_nat[72:73, :], subln_g0).then_inc(gain_loaded, 16)
                    sp.dma_start(gains_nat[73:85, :], conv_w0.rearrange("a w (k p) -> (a w k) p", p=P)).then_inc(
                        gain_loaded, 16)
                    sp.dma_start(sc_nat, state_conv.rearrange("a b t c -> (a b t) c")).then_inc(gain_loaded, 16)
                    sp.dma_start(n_rows, state_n.rearrange("a b h (k p) -> (a b h k) p", p=P)).then_inc(
                        gain_loaded, 16)
            sp.dma_start(lam_rows, lam0.rearrange("a f d -> a (f d)").partition_broadcast(P)).then_inc(lam_loaded, 16)
            sp.dma_start(page_ids[:, :], page_table.rearrange("(a b) n -> a (b n)", a=1)).then_inc(ids_loaded, 16)
            sp.dma_start(b_if[:, :], b_if1.rearrange("a (g h) -> h (a g)", g=2),
                         allow_slow_non_contiguous=True).then_inc(bif_loaded, 16)
            sp.dma_start(m_prev[:, 8:16], state_m.rearrange("a b h -> h (a b)"),
                         allow_slow_non_contiguous=True).then_inc(m0_loaded, 16)
            q_k = lambda i, j: w_cols(w_in0[0], ds(3 * CH + j * CH + i * P, P))
            load_tile(sp, QK, 0, q_k(0, 0), KD, wait=False)
            load_tile(sp, QK + 1, 0, q_k(0, 1), KD, wait=False)
            with sp.Fori(1, HEADS) as i:
                for j in range(2):
                    load_tile(sp, QK + j, i, q_k(i, j), KD)
            with sp.Fori(0, 2) as i:
                for j in range(2):
                    load_tile(sp, V + j, i, w_cols(w_in0[0], ds(5 * CH + (2 * i + j) * P, P)), KD)
            with sp.Fori(0, 2) as i:
                for m in range(6):
                    first = (CH, 2 * CH, 0)[m % 3] + m // 3 * P
                    load_tile(sp, CXB + m, 3 * i, w_cols(w_in0[0], ds(first + 2 * i * P, P)), KD)
            load_tile(sp, WO0, 0, w_cols(w_out0[0], ds(0, P)), KD)
            load_tile(sp, WO0 + 1, 0, w_cols(w_out0[0], ds(P, P)), KD)
            load_pages(sp)
            with sp.Fori(1, 4) as i:
                for j in range(2):
                    load_tile(sp, WO0 + j, i, w_cols(w_out0[0], ds((2 * i + j) * P, P)), KD)
            load_ffn(sp, FF0, 0)
            load_tile(sp, GATES, 0, w_cols(w_in1[0], slice(4 * D, 4 * D + 8)), KD, n=8)
            with sp.Fori(0, HEADS) as h:
                for m in range(8):
                    load_tile(sp, QKVO + m, 4 * h, head_src(h, m), KD)
            with sp.Fori(0, 4) as i:
                for j in range(2):
                    load_tile(sp, WO1 + j, i, w_cols(w_out1[0], ds((2 * i + j) * P, P)), KD)
            load_ffn(sp, FF1, 1)
            for tt in range(NTT):
                w = P if tt < NTT - 1 else TS
                sp.wait_ge(y_ev[tt % 2], tt // 2 + 1)
                dst = y_p[0, tt * P:tt * P + w, :] if tt < NTT - 1 else y_s.rearrange("b t d -> (b t) d")
                sp.dma_start(dst, arena[0:w, tt, 0:D]).then_inc(out_done, 16)
            sp.wait_ge(out_done, 16 * NTT)

        @block.gpsimd
        def _(pool):
            chain = Chain(pool, pool_c)
            for t, v in ((ident, 0.0), (ones, 1.0), (causal, 0.0), (dmask, 0.0), (dmask_s, 0.0), (smask, 0.0),
                         (bmask, 1.0), (sel, 1.0)):
                chain.mark(pool.memset(t[:], v))
            chain.sync()

            def where(t, op, fill, base, pattern, by):
                chain.link(pool.affine_select(out=t, in_=t, compare_op=op, fill=fill, base=base, pattern=pattern,
                                              channel_multiplier=by))
            where(ident[:, :], ALU.not_equal, 1.0, 0, [[-1, P]], 1)
            where(causal[:, :], ALU.is_ge, -BIG, 0, [[-1, P]], 1)
            where(dmask[:, :], ALU.is_ge, BIG, 0, [[1, P]], -1)
            where(dmask_s[:, :], ALU.is_ge, BIG, 0, [[1, TS]], -1)
            s4 = dmask_s[:, :].rearrange("p (b t) -> p b t", b=NB)
            where(s4, ALU.is_ge, BIG, 0, [[-NS, NB], [0, NS]], 1)
            m4 = smask[:, :].rearrange("p (b c t) -> p b c t", b=NB, c=2)
            where(m4, ALU.is_ge, -BIG, 0, [[NS, NB], [0, 2], [1, NS]], -1)
            where(m4, ALU.is_ge, -BIG, 0, [[-NS, NB], [0, 2], [0, NS]], 1)
            where(bmask[:, :], ALU.is_ge, 0.0, 0, [[-NS, NB]], 1)
            where(bmask[:, :], ALU.is_ge, 0.0, NS - 1, [[NS, NB]], -1)
            where(sel[:, :, :], ALU.is_ge, 0.0, 0, [[-1, HEADS], [0, P]], 1)
            where(sel[:, :, :], ALU.is_ge, 0.0, 0, [[1, HEADS], [0, P]], -1)
            pool.memset(conv_in[:, 0:2], 0.0).then_inc(const_ready, 1)
            add_squares(pool, 0)
            pool.wait_ge(mix_ready, HEADS)
            pool.wait_ge(conv_ev, 1)
            pool.dma_start(conv_p[0, 0], conv_nat[0:2, :]).then_inc(conv_saved, 16)
            pool.dma_start(conv_s[0].rearrange("b t c -> (b t) c"), conv_nat[2:2 + 2 * NB, :]).then_inc(conv_saved, 16)
            pool.wait_ge(conv_saved, 32)
            with pool.Fori(0, HEADS) as h:
                pool.wait_ge(head_done, h)
                pool.wait_ge(kv_stored, 32 * h)
                pool.tensor_copy(one(v_h), vT[:, ds(h, 1), :]).then_inc(cur_ready, 1)
                pool.tensor_copy(one(k_h), kT[:, ds(h, 1), :]).then_inc(cur_ready, 1)
                pool.tensor_copy(one(q_h), qT[:, ds(h, 1), 0:SEQ]).then_inc(cur_ready, 1)
                for ev, src, dst in ((v_ev, v_nat, v_p), (k_ev, k_nat, k_p)):
                    pool.wait_ge(ev, h + 1)
                    alone(pool)
                    pool.dma_start(dst[0, 0].rearrange("(c p) h e -> p c h e", p=P)[:, :, ds(h, 1), :],
                                   src.rearrange("p (c a e) -> p c a e", c=8, a=1)).then_inc(kv_stored, 16)
            pool.dma_start(k_s[0].rearrange("b t h e -> (b t) h e"), kv_s_nat[:, 0, :, :]).then_inc(own_stored, 16)
            pool.dma_start(v_s[0].rearrange("b t h e -> (b t) h e"), kv_s_nat[:, 1, :, :]).then_inc(own_stored, 16)
            for n in (1, 2, 3, 4):
                add_squares(pool, n)
            pool.wait_ge(h_ready, 2 * KD)
            pool.dma_start(spill, hT[:, :, :]).then_inc(spilled, 16)
            pool.wait_ge(r_dve, 2)
            pool.dma_start(m_p.rearrange("a b h -> h (a b)"), m_out[:, 0:1],
                           allow_slow_non_contiguous=True).then_inc(m_stored, 16)
            pool.dma_start(m_s.rearrange("a b h -> h (a b)"), m_out[:, 1:1 + NB],
                           allow_slow_non_contiguous=True).then_inc(m_stored, 16)
            pool.wait_ge(rows_ready, 1)
            with pool.Fori(0, HEADS) as h:
                def state_of(a, b):
                    return a[0, b, ds(h, 1), :, :].rearrange("a (k p) e -> p (a k) e", p=P)

                def load(b):
                    pool.wait_ge(cs_ready, NB * h + b - 1) if b >= 2 else pool.wait_ge(cs_ready, NB * h)
                    alone(pool)
                    pool.dma_start(cs[b % 2][:, :, 0:MLD], state_of(state_C, b)).then_inc(cs_loaded[b % 2], 16)
                load(0)
                load(1)
                pool.wait_ge(state_ready, 8 * h + 8)
                alone(pool)
                pool.dma_start(state_of(C_p, 0), state[0][:, :, 0:MLD]).then_inc(state_stored, 16)
                for b in range(NB):
                    pool.wait_ge(cs_ready, NB * h + b + 1)
                    alone(pool)
                    pool.dma_start(state_of(C_s, b), cs_new[b % 2][:, :, 0:MLD]).then_inc(cs_stored[b % 2], 16)
                    if b + 2 < NB:
                        load(b + 2)
                pool.wait_ge(n_ev, h + 1)
                alone(pool)
                pool.dma_start(n_p[0, :, ds(h, 1), :].rearrange("b a d -> b (a d)"), n_nat[0:1, :]).then_inc(n_stored, 16)
                pool.dma_start(n_s[0, :, ds(h, 1), :].rearrange("b a d -> b (a d)"), n_nat[1:1 + NB, :]).then_inc(
                    n_stored, 16)
            pool.wait_ge(hn_done, HEADS)
            pool.wait_ge(n_stored, 32 * HEADS)
            for b in range(2):
                pool.wait_ge(cs_stored[b], 16 * HEADS * NB // 2)
            pool.dma_start(hT[:, :, :], spill).then_inc(restored, 16)
            for n in (5, 6, 7):
                add_squares(pool, n)
            pool.wait_ge(kv_stored, 32 * HEADS)
            pool.wait_ge(own_stored, 32)
            pool.wait_ge(conv_saved, 32)
            pool.wait_ge(m_stored, 32)
            pool.wait_ge(state_stored, 16 * HEADS)

        @block.scalar
        def _(act):
            chain = Chain(act, act_c)
            act.wait_ge(lam_ready, 1)
            act.activation(lam_e, lam_e, ACT.Exp).then_inc(misc_ev, 1)
            split_hi(act, QK, 0, KD, first=True)
            for tt in range(0, NTT, 2):
                w = P if tt < NTT - 1 else TS
                act.wait_ge(x_t, tt + 1)
                act.activation(hT[:, :, tt * P:tt * P + w],
                               flat(2 * (tt % 3), 1024).rearrange("p (k t) -> p k t", t=P)[:, :, 0:w],
                               ACT.Copy).then_inc(x_ev[0], 1)
            act.wait_ge(x_ev[0], 5)
            act.wait_ge(x_ev[1], 4)
            act_before(act, 0, 0, 0)
            act_proj0(act, chain)
            act_heads(act)
            act_samples(act)
            act_project(act, WO0, 1, KD)
            act_roots(act, norm_q(1), NTT)
            act_before(act, 2, 0, 1)
            act_ffn(act, FF0, 0, 3, True)
            act_roots(act, norm_q(3), NTT)
            act_before(act, 4, KD, 2)
            act_gates(act, chain)
            act_mlstm(act)
            act_project(act, WO1, 5, KD)
            act_roots(act, norm_q(5), NTT)
            act_before(act, 6, 2 * KD, 3)
            act_ffn(act, FF1, 1, 7, False)
            act_roots(act, norm_q(7), NTT)
            for tt in range(0, NTT, 2):
                w = P if tt < NTT - 1 else TS
                act.wait_ge(y_t, tt + 1)
                act.activation(arena[0:w, tt, 0:D], flat(2 * (tt % 3), 1024)[0:w, :], ACT.Copy).then_inc(y_ev[0], 1)

        @block.vector
        def _(dve):
            chain = Chain(dve, dve_c)
            chain.link(dve.memset(roots[:, :, :], 1.0))
            dve.wait_ge(lam_loaded, 16)
            l4 = lam_rows.rearrange("p (f d) -> p f d", f=4)
            chain.link(dve.tensor_tensor(lam_prod.rearrange("p (f d) -> p f d", f=2), l4[:, 0:4:2, :], l4[:, 1:4:2, :],
                                         ALU.mult))
            dve.tensor_reduce(lam_e, lam_prod.rearrange("p (f d) -> p f d", f=2), AX.X, ALU.add).then_inc(lam_ready, 1)
            dve.wait_ge(misc_t, 1)
            t = ps[:, 7, :]
            dve.tensor_scalar(gains[:, 0:64], t[:, 0:64], math.sqrt(D), None, ALU.mult)
            dve.tensor_scalar(gains[:, GM:GM + 8], t[:, 64:72], math.sqrt(MLD), None, ALU.mult)
            dve.tensor_scalar(gains[:, GS:GS + 1], t[:, 72:73], math.sqrt(P) * (1 - LAM_INIT), None, ALU.mult)
            dve.tensor_copy(gains[:, GC:GC + 12], t[:, 73:85])
            dve.tensor_copy(nT[:, :, :, :].rearrange("p b h k -> p (b h k)"), t[:, 128:192])
            chain.link(dve.tensor_copy(stT[:, :, :].rearrange("p k n -> p (k n)"), t[:, 256:320]))
            dve.wait_ge(misc_ev, 1)
            chain.link(dve.scalar_tensor_tensor(neg_lam, lam_e[:, 1:2], -LAM_INIT, lam_e[:, 0:1], ALU.add,
                                                ALU.subtract))
            split_lo(dve, QK, 0, KD)
            for tt in range(1, NTT, 2):
                dve.wait_ge(x_t, tt + 1)
                dve.tensor_copy(hT[:, :, tt * P:(tt + 1) * P],
                                flat(2 * (tt % 3), 1024).rearrange("p (k t) -> p k t", t=P)).then_inc(x_ev[1], 1)
            dve_before(dve, chain, 0, 0, 0, 0)
            dve.wait_ge(const_ready, 1)
            dve_proj0(dve, chain)
            dve.wait_ge(conv_t, 1)
            dve.tensor_copy(conv_nat[:, :], ps[0:2 + 2 * NB, 7, :]).then_inc(conv_ev, 1)
            dve_heads(dve, chain)
            dve_samples(dve, chain)
            dve_splits(dve, WO0, 8, KD)
            dve_after(dve, chain, 1, 0, 1, 0)
            dve_before(dve, chain, 2, 0, 2, 1)
            dve_ffn(dve, FF0, 0, True)
            dve_after(dve, chain, 3, 0, 3, 1)
            dve_before(dve, chain, 4, 1, 0, 2)
            dve_gates(dve, chain)
            dve_mlstm(dve, chain)
            dve_splits(dve, WO1, 8, KD)
            dve.wait_ge(restored, 16)
            dve_after(dve, chain, 5, 1, 1, 2)
            dve_before(dve, chain, 6, 1, 2, 3)
            dve_ffn(dve, FF1, 1, False)
            dve_after(dve, chain, 7, 1, 3, 3)
            for tt in range(1, NTT, 2):
                dve.wait_ge(y_t, tt + 1)
                dve.tensor_copy(arena[:, tt, 0:D], flat(2 * (tt % 3), 1024)).then_inc(y_ev[1], 1)

        @block.tensor
        def _(pe):
            pe.wait_ge(const_ready, 1)
            pe.wait_ge(gain_loaded, 96)
            pe.transpose(ps[:, 7, 0:85], gains_nat, ident[0:85, 0:85])
            pe.transpose(ps[:, 7, 128:192], n_rows, ident[0:64, 0:64])
            for k in range(HC):
                ins = pe.transpose(ps[:, 7, 256 + 2 * NB * k:256 + 2 * NB * (k + 1)], sc_nat[:, k * P:(k + 1) * P],
                                   ident[0:2 * NB, 0:2 * NB])
            ins.then_inc(misc_t, 1)
            for tt in range(NTT):
                w = P if tt < NTT - 1 else TS
                pe.wait_ge(x_loaded[tt], 16)
                if tt >= 3:
                    pe.wait_ge(x_ev[(tt - 3) % 2], (tt - 3) // 2 + 1)
                for k in range(KD):
                    ins = pe.transpose(flat(2 * (tt % 3), 1024)[:, k * P:k * P + w],
                                       arena[0:w, tt, k * P:(k + 1) * P], ident[0:w, 0:w])
                ins.then_inc(x_t, 1)
            pe_norm(pe, 0, 3)
            pe.wait_ge(u_ready, KD)
            over_pairs(pe, 8, lambda i, j, last: products(pe, QK + j, i, u, KD))
            over_pairs(pe, 4, lambda i, j, last: products(pe, V + j, i, u, KD))
            with pe.Fori(0, 2) as i:
                for m in range(6):
                    products(pe, CXB + m, 3 * i, u, KD)
            pe.wait_ge(evac[0], WO0 // 2)
            pe.wait_ge(evac[1], WO0 // 2)
            pe.wait_ge(mix_ready, HEADS)
            for k in range(HC):
                ins = pe.transpose(ps[0:2 + 2 * NB, 7, k * P:(k + 1) * P], conv_new[:, k, :], ident[:, :])
            ins.then_inc(conv_t, 1)
            pe.wait_ge(conv_ev, 1)
            pe_heads(pe)
            pe_samples(pe)
            pe.wait_ge(mix_ready, HEADS + 1)
            over_pairs(pe, 8, lambda i, j, last: products(pe, WO0 + j, i, mix, KD))
            pe_norm(pe, 1, 0)
            pe_norm(pe, 2, 3)
            pe_ffn(pe, FF0, 0, 1)
            pe_norm(pe, 3, 0)
            pe_norm(pe, 4, 3)
            pe_gates(pe)
            pe_mlstm(pe)
            pe.wait_ge(hn_done, HEADS)
            over_pairs(pe, 8, lambda i, j, last: products(pe, WO1 + j, i, hn, KD))
            pe_norm(pe, 5, 0)
            pe_norm(pe, 6, 3)
            pe_ffn(pe, FF1, 1, 3)
            pe_norm(pe, 7, 0)
            pe.wait_ge(h_ready, 4 * KD)
            for tt in range(NTT):
                w = P if tt < NTT - 1 else TS
                if tt >= 3:
                    pe.wait_ge(y_ev[(tt - 3) % 2], (tt - 3) // 2 + 1)
                for k in range(KD):
                    ins = pe.transpose(flat(2 * (tt % 3), 1024)[0:w, k * P:(k + 1) * P], hT[:, k, tt * P:tt * P + w],
                                       ident[:, :])
                ins.then_inc(y_t, 1)


INS = ["x_prompt", "x_sample", "cache_k", "cache_v", "state_conv", "state_C", "state_n", "state_m", "page_table",
       "norms", "w_in0", "conv_w0", "lam0", "subln_g0", "w_out0", "w_in1", "b_if1", "mh_g1", "w_out1", "w_gu", "w_down"]
OUTS = [(1, SEQ, D), (NB, NS, D), (1, 1, SEQ, HEADS, P), (1, 1, SEQ, HEADS, P), (1, 1, 2, CH),
        (1, 1, HEADS, MLD, MLD), (1, 1, HEADS, MLD), (1, 1, HEADS), (1, NB, NS, HEADS, P), (1, NB, NS, HEADS, P),
        (1, NB, 2, CH), (1, NB, HEADS, MLD, MLD), (1, NB, HEADS, MLD), (1, NB, HEADS)]


def kernel(**inputs):
    import numpy as np
    import concourse.bacc as bacc
    from concourse.bass_utils import run_bass_kernel_spmd

    nc = bacc.Bacc("TRN2", target_bir_lowering=False, num_devices=1,
                   dynamic_dma_scratch_size=4096)
    arrays, args = {}, []
    for name in INS:
        a = np.ascontiguousarray(inputs[name])
        arrays[f"in_{name}"] = a
        args.append(nc.dram_tensor(f"in_{name}", a.shape, mybir.dt.from_np(a.dtype), kind="ExternalInput").ap())
    for i, shape in enumerate(OUTS):
        args.append(nc.dram_tensor(f"out_{i}", shape, F32, kind="ExternalOutput").ap())
    build(nc, *args)
    r = run_bass_kernel_spmd(nc, [arrays], core_ids=[0])
    return tuple(r.results[0][f"out_{i}"] for i in range(len(OUTS)))
```

```python
import math
from contextlib import ExitStack

import concourse.bass as bass
from concourse import mybir

F32 = mybir.dt.float32
F16 = mybir.dt.float16
I32 = mybir.dt.int32
ALU = mybir.AluOpType
ACT = mybir.ActivationFunctionType
AX = mybir.AxisListType
ds = bass.ds

P = 128
D = 1024
KD = D // P
SEQ = 1024
NB, NS = 8, 4
TS = NB * NS
T = SEQ + TS
GW = T // 3
NTT = SEQ // P + 1
CH = D // 2
HEADS = 4
HC = CH // P
PAGE = 128
NPG = 16
DFF = 2816
KF = 11
WS = 64.0
EPS = 1e-6
LAM_INIT = 0.8 - 0.6 * math.exp(0.0)
BIG = 1e30
MLD = 256
SCALE_DA = 64 ** -0.5
RING = 8


class Chain:

    def __init__(self, eng, sem):
        self.eng, self.sem, self.base, self.n = eng, sem, 0, 0

    def link(self, ins):
        self.mark(ins)
        self.sync()

    def mark(self, ins):
        self.n += 1
        ins.then_inc(self.sem, 1)

    def sync(self):
        self.eng.wait_ge(self.sem, self.base + self.n)

    def enter(self, i, per):
        self.start, self.per = self.base + self.n, per
        self.base, self.n = i * per + self.start, 0

    def leave(self, times):
        assert self.n == self.per, (self.sem, "marks in the body:", self.n, "declared:", self.per)
        self.base, self.n = self.start + self.per * times, 0


def build(nc, x_p, x_s, cache_k, cache_v, state_conv, state_C, state_n, state_m, page_table, norms, w_in0,
          conv_w0, lam0, subln_g0, w_out0, w_in1, b_if1, mh_g1, w_out1, w_gu, w_down, y_p, y_s, k_p, v_p,
          conv_p, C_p, n_p, m_p, k_s, v_s, conv_s, C_s, n_s, m_s):
    ctx = ExitStack()
    with ctx:
        def sb(name, shape, dt=F32):
            return ctx.enter_context(nc.sbuf_tensor(name, shape, dt))

        def sem(name):
            return ctx.enter_context(nc.semaphore(name))

        hT = sb("hT", [P, KD, T])
        u = sb("u", [P, 2, KD, T], F16)
        w_raw = sb("w_raw", [P, 2, KF * P])
        w_split = sb("w_split", [P, 2, 2, KF * P], F16)
        arena = sb("arena", [P, 28, T])
        ident = sb("ident", [P, P])
        ones = sb("ones", [P, P])
        gains = sb("gains", [P, 88])
        causal = sb("causal", [P, P])
        dmask = sb("dmask", [P, P])
        dmask_s = sb("dmask_s", [TS, TS])
        smask = sb("smask", [TS, NB * 2 * HEADS * NS])
        bmask = sb("bmask", [TS, NB])
        sel = sb("sel", [HEADS, HEADS, P])
        small = sb("small", [P, 400])
        roots = sb("roots", [P, 3, NTT])
        ps = ctx.enter_context(nc.psum_tensor("ps", [P, 8, 512], F32))

        GN = lambda layer, which: (layer * 4 + which) * KD
        GM, GS, GC = 64, 72, 73

        def rows(a, n):
            return arena[:, a:a + n, :]

        def half(region, tiles):
            return region.rearrange("p a t -> p (a t)").bitcast(F16).rearrange(
                "p (l k t) -> p l k t", l=2, k=tiles)

        def group(bank):
            return ps[:, bank:bank + 3, 0:GW]

        def flat(bank, n):
            return ps[:, bank:bank + -(-n // 512), :].rearrange("p b w -> p (b w)")[:, 0:n]

        def alone(eng):
            eng.sem_inc(passed[eng.engine], 1)

        def by3(row):
            return row.rearrange("p (g t) -> p g t", g=3)

        mix = half(rows(0, 8), KD)
        hid = half(rows(0, KF), KF)
        ybuf = rows(11, 8)
        tmp = [arena[:, 19, :], arena[:, 20, :]]
        hidf = arena[:, 21, :]
        gate = arena[:, 22, :]
        sq = [arena[:, 23, :], arena[:, 24, :]]
        ssq = arena[:, 25, :]
        diag_row = arena[:, 26, :]

        w_loaded = [sem("w_loaded0"), sem("w_loaded1")]
        w_hi = sem("w_hi")
        w_ready = sem("w_ready")
        mm_done = sem("mm_done")
        evac = [sem("evac0"), sem("evac1")]
        passed = {e.engine: sem(f"passed{i}") for i, e in enumerate((nc.sync, nc.scalar, nc.gpsimd, nc.tensor))}
        const_ready = sem("const_ready")
        gain_loaded = sem("gain_loaded")
        gain_t = sem("gain_t")
        x_loaded = [sem(f"x_loaded{i}") for i in range(NTT)]
        x_t = sem("x_t")
        x_ev = [sem("x_ev0"), sem("x_ev1")]
        sq_ready = sem("sq_ready")
        ssq_added = sem("ssq_added")
        root_sum = sem("root_sum")
        root_in, root_out = sem("root_in"), sem("root_out")
        root_diag = sem("root_diag")
        root_done = sem("root_done")
        h_ready = sem("h_ready")
        t_ready = sem("t_ready")
        u_hi = sem("u_hi")
        u_ready = sem("u_ready")
        hid_hi = sem("hid_hi")
        hid_ready = sem("hid_ready")
        y_t = sem("y_t")
        y_ev = [sem("y_ev0"), sem("y_ev1")]
        out_done = sem("out_done")
        act_c, dve_c, pool_c = sem("act_c"), sem("dve_c"), sem("pool_c")
        outs = [0]

        def over_pairs(eng, n, body, chain=None, per=0):
            if n > 2:
                with eng.Fori(0, n // 2 - 1) as i:
                    if chain:
                        chain.enter(i, per)
                    body(i, 0, False)
                    body(i, 1, False)
                if chain:
                    chain.leave(n // 2 - 1)
            body(n // 2 - 1, 0, False)
            body(n // 2 - 1, 1, True)

        def load_tile(sp, c, r, src, kt, n=P, wait=True):
            s = c % 2
            if wait:
                sp.wait_ge(w_ready, c - 1 + 2 * r)
            alone(sp)
            sp.dma_start(w_raw[:, s, 0:kt * n].rearrange("p (k n) -> p k n", k=kt), src).then_inc(w_loaded[s], 16)

        def split_hi(act, c, r, kt, n=P, first=False):
            s = c % 2
            act.wait_ge(w_loaded[s], 16 * (c // 2 + 1) + 16 * r)
            if not first:
                act.wait_ge(mm_done, c - 1 + 2 * r)
            act.activation(w_split[:, s, 0, 0:kt * n], w_raw[:, s, 0:kt * n], ACT.Copy, scale=WS).then_inc(w_hi, 1)

        def split_lo(dve, c, r, kt, n=P):
            s = c % 2
            dve.wait_ge(w_hi, c + 1 + 2 * r)
            dve.scalar_tensor_tensor(w_split[:, s, 1, 0:kt * n], w_raw[:, s, 0:kt * n], WS,
                                     w_split[:, s, 0, 0:kt * n], ALU.mult, ALU.subtract).then_inc(w_ready, 1)

        def products(pe, c, r, x, kt, m=P, n=P, col=0, bank=None, signal=True):
            s = c % 2
            pe.wait_ge(w_ready, c + 1 + 2 * r)
            pe.wait_ge(evac[s], c // 2 + r)
            b = 3 * s if bank is None else bank
            for k in range(kt):
                for q, (wp, xp) in enumerate(((0, 0), (0, 1), (1, 0))):
                    for g in range(3):
                        ins = pe.matmul(ps[0:m, b + g, 0:GW], w_split[:, s, wp, k * n + col:k * n + col + m],
                                        x[:, xp, k, g * GW:(g + 1) * GW],
                                        start=(k == 0 and q == 0), stop=(k == kt - 1 and q == 2))
            if signal:
                ins.then_inc(mm_done, 1)

        QK, V, CXB, WO0 = 0, 8, 12, 24
        FF0 = 32
        GATES, QKVO, WO1 = FF0 + 60, FF0 + 61, FF0 + 93
        FF1 = WO1 + 8
        END = FF1 + 60

        def at(c, r):
            return c + 1 + 2 * r

        def out_of_banks(c, r):
            return c // 2 + 1 + r

        def w_cols(w, col):
            return w.rearrange("(k p) n -> p k n", p=P)[:, :, col]

        def one(ap):
            return ap.rearrange("p (a t) -> p a t", a=1)

        def add_squares(pool, n):
            for k in range(KD):
                pool.wait_ge(sq_ready, KD * n + k + 1)
                if k == 0:
                    if n:
                        pool.wait_ge(root_sum, norm_q(n - 1) + 1)
                    pool.tensor_copy(ssq, sq[k % 2]).then_inc(ssq_added, 1)
                else:
                    pool.wait_ge(ssq_added, KD * n + k)
                    pool.tensor_tensor(ssq, ssq, sq[k % 2], ALU.add).then_inc(ssq_added, 1)

        def square(act, n, k, r, src):
            if not (n == 0 and k < 2 and isinstance(r, int) and r == 0):
                act.wait_ge(ssq_added, KD * n + k - 1 + 2 * r)
            act.activation(sq[k % 2], src, ACT.Square).then_inc(sq_ready, 1)

        def tiles_of(width):
            return [(t, min(P, width - t * P)) for t in range(-(-width // P))]

        def pe_roots(pe, q, d, srcs, diag, width, bank):
            for t, w in tiles_of(width):
                for k, src in enumerate(srcs):
                    ins = pe.matmul(ps[0:w, 6, t:t + 1], src[:, t * P:t * P + w], ones[:, 0:1], start=(k == 0),
                                    stop=(k == len(srcs) - 1))
            ins.then_inc(root_sum, 1)
            for t, w in tiles_of(width):
                pe.wait_ge(root_diag, d + t + 1)
                ins = pe.matmul(flat(bank, width)[:, t * P:t * P + w], ones[0:w, :], diag[0:w, t * P:t * P + w],
                                start=True, stop=True)
            ins.then_inc(root_done, 1)

        def act_roots(act, q, n):
            act.wait_ge(root_in, q + 1)
            act.activation(roots[:, 1, 0:n], roots[:, 0, 0:n], ACT.Abs_reciprocal_sqrt).then_inc(root_out, 1)

        def newton(dve, chain, x, y, z):
            chain.link(dve.tensor_tensor(z, x, y, ALU.mult))
            chain.link(dve.tensor_tensor(z, z, y, ALU.mult))
            chain.link(dve.tensor_scalar(z, z, -0.5, 1.5, ALU.mult, ALU.add))
            chain.link(dve.tensor_tensor(z, z, y, ALU.mult))

        def dve_roots(dve, chain, q, d, diag, width, eps):
            ts = tiles_of(width)
            dve.wait_ge(root_sum, q + 1)
            full = sum(w == P for _, w in ts)
            x, y, z = (roots[:, i, 0:len(ts)] for i in range(3))
            ins = dve.tensor_scalar(roots[:, 0, 0:full], ps[:, 6, 0:full], eps, None, ALU.add)
            if full < len(ts):
                w = ts[-1][1]
                ins = dve.tensor_scalar(roots[0:w, 0, full:full + 1], ps[0:w, 6, full:full + 1], eps, None, ALU.add)
            ins.then_inc(root_in, 1)
            dve.wait_ge(root_in, q + 1)
            dve.wait_ge(root_out, q + 1)
            newton(dve, chain, x, y, z)
            for t, w in ts:
                dve.tensor_scalar(diag[0:w, t * P:t * P + w], ident[0:w, 0:w], z[0:w, t:t + 1], None,
                                  ALU.mult).then_inc(root_diag, 1)
            dve.wait_ge(root_done, q + 1)

        def norm_q(n):
            return HEADS + 1 + n if n else 0

        HEAD_Q, HEAD_D, SAMPLE_Q, SAMPLE_D = 1, NTT, 1 + HEADS, NTT + 8 * HEADS

        def norm_d(n):
            return SAMPLE_D + 1 + NTT * (n - 1) if n else 0

        def pe_norm(pe, n, bank):
            pe.wait_ge(ssq_added, KD * (n + 1))
            pe_roots(pe, norm_q(n), norm_d(n), [ssq], diag_row, T, bank)

        def dve_after(dve, chain, n, layer, which, m):
            dve_roots(dve, chain, norm_q(n), norm_d(n), diag_row, T, D * EPS)
            rs = flat(0, T)
            col = GN(layer, which)
            for k in range(KD):
                chain.link(dve.tensor_tensor(tmp[k % 2], ybuf[:, k, :], rs, ALU.mult))
                dve.scalar_tensor_tensor(hT[:, k, :], tmp[k % 2], gains[:, col + k:col + k + 1], hT[:, k, :],
                                         ALU.mult, ALU.add).then_inc(h_ready, 1)

        def act_before(act, n, h0, m):
            for k in range(KD):
                if n:
                    act.wait_ge(h_ready, h0 + k + 1)
                square(act, n, k, 0, hT[:, k, :])
            act_roots(act, norm_q(n), NTT)
            for k in range(KD):
                act.wait_ge(t_ready, KD * m + k + 1)
                act.activation(u[:, 0, k, :], tmp[k % 2], ACT.Copy).then_inc(u_hi, 1)

        def dve_before(dve, chain, n, layer, which, m):
            dve_roots(dve, chain, norm_q(n), norm_d(n), diag_row, T, D * EPS)
            rs = flat(3, T)
            col = GN(layer, which)
            def lo(k):
                dve.wait_ge(u_hi, KD * m + k + 1)
                dve.tensor_tensor(u[:, 1, k, :], tmp[k % 2], u[:, 0, k, :], ALU.subtract).then_inc(u_ready, 1)
            for k in range(KD):
                if k >= 2:
                    dve.wait_ge(u_ready, KD * m + k - 1)
                dve.scalar_tensor_tensor(tmp[k % 2], hT[:, k, :], gains[:, col + k:col + k + 1], rs,
                                         ALU.mult, ALU.mult).then_inc(t_ready, 1)
                if k:
                    lo(k - 1)
            lo(KD - 1)

        def act_project(act, c0, stage, kt_next):
            def tile(i, j, last):
                split_hi(act, c0 + j + 1, i, kt_next if last else KD)
                act.wait_ge(mm_done, at(c0 + j, i))
                alone(act)
                yt = ybuf[:, ds(2 * i + j, 1), :] if not isinstance(i, int) else ybuf[:, 2 * i + j:2 * i + j + 1, :]
                yt = yt.rearrange("p a (g t) -> p (a g) t", g=3)
                act.activation(yt, group(3 * ((c0 + j) % 2)), ACT.Copy,
                               scale=1 / WS).then_inc(evac[(c0 + j) % 2], 1)
                act.wait_ge(evac[(c0 + j) % 2], out_of_banks(c0 + j, i))
                act.wait_ge(ssq_added, KD * stage + j - 1 + 2 * i)
                alone(act)
                act.activation(by3(sq[j]), yt, ACT.Square).then_inc(sq_ready, 1)
            over_pairs(act, 8, tile)

        def dve_splits(dve, c0, n, kt_next):
            over_pairs(dve, n, lambda i, j, last: split_lo(dve, c0 + j + 1, i, kt_next if last else KD))

        def load_ffn(sp, c0, layer):
            for half_ in range(2):
                c = c0 + 30 * half_
                r0 = half_ * KF * P
                over_pairs(sp, 22, lambda i, j, last: load_tile(
                    sp, c + j, i, w_cols(w_gu[layer], ds(r0 + j * DFF + i * P, P)), KD))
                over_pairs(sp, 8, lambda i, j, last: load_tile(
                    sp, c + 22 + j, i, w_cols(w_down[layer, r0:r0 + KF * P, :], ds((2 * i + j) * P, P)), KF))

        def pe_ffn(pe, c0, layer, m):
            pe.wait_ge(u_ready, KD * (m + 1))
            for half_ in range(2):
                c = c0 + 30 * half_
                over_pairs(pe, 22, lambda i, j, last: products(pe, c + j, i, u, KD))
                pe.wait_ge(hid_ready, 22 * layer + 11 * (half_ + 1))
                over_pairs(pe, 8, lambda i, j, last: products(pe, c + 22 + j, i, hid, KF))

        def act_ffn(act, c0, layer, stage, more):
            for half_ in range(2):
                c, n0 = c0 + 30 * half_, 22 * layer + 11 * half_
                a, b = c % 2, (c + 1) % 2

                def gate_up(i, j, last):
                    split_hi(act, c + j + 1, i, KF if last else KD)
                    if j == 0:
                        act.wait_ge(mm_done, at(c, i))
                        act.wait_ge(evac[b], (c + 1) // 2 + i)
                        act.activation(by3(gate), group(3 * a), ACT.Silu, scale=1 / WS).then_inc(evac[a], 1)
                    else:
                        act.wait_ge(evac[b], out_of_banks(c + 1, i))
                        alone(act)
                        act.activation(hid[:, 0, ds(i, 1), :], one(hidf), ACT.Copy).then_inc(hid_hi, 1)
                over_pairs(act, 22, gate_up)

                def down(i, j, last):
                    e = c + 22 + j
                    if not last or more or half_ == 0:
                        split_hi(act, e + 1, i, KD if last else KF, n=8 if last and half_ else P)
                    yt = ybuf[:, ds(2 * i + j, 1), :].rearrange("p a (g t) -> p (a g) t", g=3)
                    if half_ == 0:
                        act.wait_ge(mm_done, at(e, i))
                        alone(act)
                        act.activation(yt, group(3 * (e % 2)), ACT.Copy, scale=1 / WS).then_inc(evac[e % 2], 1)
                    else:
                        act.wait_ge(evac[e % 2], out_of_banks(e, i))
                        act.wait_ge(ssq_added, KD * stage + j - 1 + 2 * i)
                        alone(act)
                        act.activation(by3(sq[j]), yt, ACT.Square).then_inc(sq_ready, 1)
                over_pairs(act, 8, down)

        def dve_ffn(dve, c0, layer, more):
            for half_ in range(2):
                c, n0 = c0 + 30 * half_, 22 * layer + 11 * half_
                a, b = c % 2, (c + 1) % 2

                def gate_up(i, j, last):
                    split_lo(dve, c + j + 1, i, KF if last else KD)
                    if j == 0:
                        return
                    dve.wait_ge(mm_done, at(c + 1, i))
                    dve.wait_ge(evac[a], out_of_banks(c, i))
                    dve.wait_ge(hid_hi, n0 + i)
                    dve.wait_ge(hid_ready, n0 + i)
                    dve.scalar_tensor_tensor(by3(hidf), group(3 * b), 1 / WS, by3(gate),
                                             ALU.mult, ALU.mult).then_inc(evac[b], 1)
                    dve.wait_ge(evac[b], out_of_banks(c + 1, i))
                    dve.wait_ge(hid_hi, n0 + i + 1)
                    dve.tensor_tensor(hid[:, 1, ds(i, 1), :], one(hidf), hid[:, 0, ds(i, 1), :],
                                      ALU.subtract).then_inc(hid_ready, 1)
                over_pairs(dve, 22, gate_up)

                def down(i, j, last):
                    e = c + 22 + j
                    if not last or more or half_ == 0:
                        split_lo(dve, e + 1, i, KD if last else KF, n=8 if last and half_ else P)
                    if half_ == 0:
                        return
                    yt = ybuf[:, ds(2 * i + j, 1), :].rearrange("p a (g t) -> p (a g) t", g=3)
                    dve.wait_ge(mm_done, at(e, i))
                    dve.scalar_tensor_tensor(yt, group(3 * (e % 2)), 1 / WS, yt,
                                             ALU.mult, ALU.add).then_inc(evac[e % 2], 1)
                over_pairs(dve, 8, down)

        qT, kT, vT = rows(8, 4), rows(12, 4), rows(16, 4)
        gate_c = arena[:, 20, :]
        conv_in = rows(21, 2).rearrange("p a t -> p (a t)")
        conv_p_in = conv_in[:, 0:SEQ + 2]
        conv_s_in = conv_in[:, SEQ + 2:SEQ + 2 + NB * 6].rearrange("p (b t) -> p b t", b=NB)
        conv_y, y_b = arena[:, 23, :], arena[:, 24, :]
        u_row = u.rearrange("p l k t -> p (l k t)").bitcast(F32).rearrange("p (a t) -> p a t", t=T)
        prob = [u_row[:, i, 0:SEQ] for i in range(4)]
        ring = u_row[:, 4:8, :].rearrange("p a t -> p (a t)")[:, 0:RING * CH].rearrange("p (r c) -> p r c", r=RING)
        q_h, k_h, v_h = arena[:, 20, 0:SEQ], arena[:, 21, :], arena[:, 22, :]
        v_nat, k_nat, att = arena[:, 23, 0:SEQ], arena[:, 27, 0:SEQ], arena[:, 24, 0:SEQ]
        squares_h, diag_h, normed_h = prob[0], prob[1], prob[2]
        prob_t = [arena[:, 25, 0:SEQ], arena[:, 26, 0:SEQ]]
        kv_s_nat = sb("kv_s_nat", [TS, 2, HEADS, P])
        stT = sb("stT", [P, HC, 2 * NB])
        conv_new = sb("conv_new", [P, HC, 2 + 2 * NB])
        lam_rows = small[:, 0:256]
        lam_prod = small[:, 256:384]
        lam_e = small[:, 384:386]
        neg_lam = small[:, 386:387]
        mx, neg_mx = small[:, 388:390], small[:, 390:394]
        lsum, rl = small[:, 394:398], small[:, 398:400]
        flat2 = lambda a: rows(a, 2).rearrange("p a t -> p (a t)")
        q_cur = [arena[:, 16, 160 * b:160 * (b + 1)] for b in range(2)]
        o_nat = arena[0:TS, 16, 512:1024]
        own_s = [arena[0:TS, 17, 32 * b:32 * (b + 1)] for b in range(2)]
        smask_n = arena[0:TS, 17, 64:320].rearrange("p (b t) -> p b t", b=NB)
        sm_max = [arena[0:TS, 17, 320 + 8 * b:325 + 8 * b] for b in range(2)]
        sm_neg = [arena[0:TS, 17, 336 + b:337 + b] for b in range(2)]
        sm_sum = [arena[0:TS, 17, 340 + 8 * b:345 + 8 * b] for b in range(2)]
        sm_rl = [arena[0:TS, 17, 356 + b:357 + b] for b in range(2)]
        sm_t = arena[:, 17, 384:544]
        k_page_t = [arena[:, 25, 0:CH], arena[:, 25, CH:2 * CH]]
        probs_s = [flat2(20)[0:TS, 0:2 * SEQ + TS], flat2(22)[0:TS, 0:2 * SEQ + TS]]
        probs_t = [arena[:, 26 + b, 0:(NPG + 1) * TS] for b in range(2)]
        att_s = arena[:, 24, 0:P].rearrange("p (h t) -> p h t", h=HEADS)
        page_ids = sb("page_ids", [1, NB * NPG], I32)

        lam_loaded, misc_t, misc_ev = sem("lam_loaded"), sem("misc_t"), sem("misc_ev")
        lam_ready = sem("lam_ready")
        gate_c_used = sem("gate_c_used")
        yb_hi, mix_ready = sem("yb_hi"), sem("mix_ready")
        conv_saved = sem("conv_saved")
        cur_ready = sem("cur_ready")
        vk_t = sem("vk_t")
        v_ev, k_ev = sem("v_ev"), sem("k_ev")
        kv_stored = sem("kv_stored")
        s_done = sem("s_done")
        nm_ready = sem("nm_ready")
        p_ready = sem("p_ready")
        w_comb = sem("w_comb")
        pt_t = sem("pt_t")
        pt_ev = sem("pt_ev")
        pv_done = sem("pv_done")
        pv_ev = sem("pv_ev")
        asq_ready = sem("asq_ready")
        at_ready, mix_hi = sem("at_ready"), sem("mix_hi")
        head_done = sem("head_done")
        page_loaded = [sem(f"page_loaded{i}") for i in range(RING)]
        page_used = sem("page_used")
        ids_loaded = sem("ids_loaded")
        kp_t = sem("kp_t")
        kp_ev = [sem("kp_ev0"), sem("kp_ev1")]
        kp_used = sem("kp_used")
        qc_ready = sem("qc_ready")
        misc7_t, misc7_ev = sem("misc7_t"), sem("misc7_ev")
        max_ready = sem("max_ready")
        exps = sem("exps")
        o_done, o_ev = sem("o_done"), sem("o_ev")
        att_ready = sem("att_ready")
        mask_t = sem("mask_t")
        spilled, restored = sem("spilled"), sem("restored")

        def act_proj0(act, chain):
            def qk(i, j, last):
                split_hi(act, QK + j + 1, i, KD)
                if j == 0:
                    act.wait_ge(mm_done, at(QK, i))
                    alone(act)
                    act.activation(qT[:, ds(i, 1), :].rearrange("p a (g t) -> p (a g) t", g=3), group(0), ACT.Copy,
                                   scale=1 / WS).then_inc(evac[0], 1)
            over_pairs(act, 8, qk)

            def v(i, j, last):
                split_hi(act, V + j + 1, i, KD)
                if j == 0:
                    act.wait_ge(mm_done, at(V, i))
                    alone(act)
                    act.activation(vT[:, ds(2 * i, 1), :].rearrange("p a (g t) -> p (a g) t", g=3), group(0),
                                   ACT.Copy, scale=1 / WS).then_inc(evac[0], 1)
            over_pairs(act, 4, v)
            with act.Fori(0, 2) as i:
                for m in range(6):
                    c, r = CXB + m, 3 * i
                    split_hi(act, c + 1, r, KD)
                    if m % 3 == 0:
                        act.wait_ge(mm_done, at(c, r))
                        act.wait_ge(gate_c_used, 2 * i + m // 3)
                        act.activation(by3(gate_c), group(3 * (c % 2)), ACT.Copy,
                                       scale=1 / WS).then_inc(evac[c % 2], 1)
                    if m % 3 == 2:
                        act.wait_ge(evac[c % 2], out_of_banks(c, r))
                        alone(act)
                        act.activation(mix[:, 0, ds(2 * i + m // 3, 1), :], one(y_b), ACT.Copy).then_inc(yb_hi, 1)

        def dve_proj0(dve, chain):
            def qk(i, j, last):
                split_lo(dve, QK + j + 1, i, KD)
                if j:
                    dve.wait_ge(mm_done, at(QK + 1, i))
                    dve.tensor_scalar(kT[:, ds(i, 1), :].rearrange("p a (g t) -> p (a g) t", g=3), group(3), 1 / WS,
                                      None, ALU.mult).then_inc(evac[1], 1)
            over_pairs(dve, 8, qk)

            def v(i, j, last):
                split_lo(dve, V + j + 1, i, KD)
                if j:
                    dve.wait_ge(mm_done, at(V + 1, i))
                    dve.tensor_scalar(vT[:, ds(2 * i + 1, 1), :].rearrange("p a (g t) -> p (a g) t", g=3), group(3),
                                      1 / WS, None, ALU.mult).then_inc(evac[1], 1)
            over_pairs(dve, 4, v)
            per = 2 * 7
            with dve.Fori(0, 2) as i:
                chain.enter(i, per)
                for m in range(6):
                    c, r = CXB + m, 3 * i
                    h = 2 * i + m // 3
                    b = 3 * (c % 2)
                    split_lo(dve, c + 1, r, KD)
                    if m % 3 == 1:
                        chain.mark(dve.tensor_copy(conv_s_in[:, :, 0:2], stT[:, ds(h, 1), :].rearrange(
                            "p a (b t) -> p (a b) t", b=NB)))
                        dve.wait_ge(mm_done, at(c, r))
                        dve.wait_ge(evac[(c - 1) % 2], out_of_banks(c - 1, r))
                        dve.scalar_tensor_tensor(
                            conv_p_in[:, 2:2 + 2 * GW].rearrange("p (g t) -> p g t", g=2), ps[:, b:b + 2, 0:GW],
                            1 / WS, gate_c[:, 0:2 * GW].rearrange("p (g t) -> p g t", g=2), ALU.mult, ALU.mult)
                        chain.mark(dve.scalar_tensor_tensor(
                            conv_p_in[:, 2 + 2 * GW:2 + SEQ], ps[:, b + 2, 0:SEQ - 2 * GW], 1 / WS,
                            gate_c[:, 2 * GW:SEQ], ALU.mult, ALU.mult))
                        dve.scalar_tensor_tensor(
                            conv_s_in[:, :, 2:6], ps[:, b + 2, SEQ - 2 * GW:GW].rearrange("p (b t) -> p b t", b=NB),
                            1 / WS, gate_c[:, SEQ:T].rearrange("p (b t) -> p b t", b=NB),
                            ALU.mult, ALU.mult).then_inc(evac[c % 2], 1)
                        dve.wait_ge(evac[c % 2], out_of_banks(c, r))
                        chain.sync()
                        chain.mark(dve.tensor_copy(conv_new[:, ds(h, 1), 0:2], one(conv_p_in[:, SEQ:SEQ + 2])))
                        chain.mark(dve.tensor_copy(
                            conv_new[:, ds(h, 1), 2:2 + 2 * NB].rearrange("p a (b t) -> p (a b) t", b=NB),
                            conv_s_in[:, :, 4:6]))
                        for k in range(3):
                            w = gains[:, ds(GC + k * HC + h, 1)]
                            yp, ys = conv_y[:, 0:SEQ], conv_y[:, SEQ:T].rearrange("p (b t) -> p b t", b=NB)
                            xp, xs = conv_p_in[:, k:k + SEQ], conv_s_in[:, :, k:k + NS]
                            if k == 0:
                                dve.tensor_scalar(yp, xp, w, None, ALU.mult)
                                chain.link(dve.tensor_scalar(ys, xs, w, None, ALU.mult))
                            elif k == 1:
                                dve.scalar_tensor_tensor(yp, xp, w, yp, ALU.mult, ALU.add)
                                chain.link(dve.scalar_tensor_tensor(ys, xs, w, ys, ALU.mult, ALU.add))
                            else:
                                chain.mark(dve.scalar_tensor_tensor(yp, xp, w, yp, ALU.mult, ALU.add))
                                dve.scalar_tensor_tensor(ys, xs, w, ys, ALU.mult, ALU.add).then_inc(gate_c_used, 1)
                    if m % 3 == 2:
                        dve.wait_ge(mm_done, at(c, r))
                        dve.wait_ge(gate_c_used, 2 * i + m // 3 + 1)
                        chain.sync()
                        dve.wait_ge(yb_hi, 2 * i + m // 3)
                        dve.wait_ge(mix_ready, 2 * i + m // 3)
                        dve.scalar_tensor_tensor(by3(y_b), group(b), 1 / WS, by3(conv_y), ALU.mult,
                                                 ALU.mult).then_inc(evac[c % 2], 1)
                        dve.wait_ge(evac[c % 2], out_of_banks(c, r))
                        dve.wait_ge(yb_hi, 2 * i + m // 3 + 1)
                        dve.tensor_tensor(mix[:, 1, ds(h, 1), :], one(y_b), mix[:, 0, ds(h, 1), :],
                                          ALU.subtract).then_inc(mix_ready, 1)
            chain.leave(2)

        def pe_heads(pe):
            with pe.Fori(0, HEADS) as h:
                def transposes(src, n):
                    for tt in range(NTT):
                        w = P if tt < NTT - 1 else TS
                        ins = pe.transpose(ps[0:w, 4 + tt // 4, (tt % 4) * P:(tt % 4 + 1) * P],
                                           src[:, tt * P:tt * P + w], ident[:, :])
                    ins.then_inc(vk_t, 1)
                pe.wait_ge(cur_ready, 3 * h + 1)
                pe.wait_ge(head_done, h)
                transposes(v_h, 0)
                pe.wait_ge(cur_ready, 3 * h + 2)
                pe.wait_ge(v_ev, h + 1)
                transposes(k_h, 1)
                pe.wait_ge(cur_ready, 3 * h + 3)

                def scores(n):
                    i, c = n // 2, n % 2
                    if n < 2:
                        pe.wait_ge(p_ready, 16 * h)
                    else:
                        pe.wait_ge(p_ready, 16 * h + n - 1)
                    w = (i + 1) * P
                    for j in range(0, w, 512):
                        ins = pe.matmul(ps[:, 2 * (n % 2) + j // 512, 0:min(512, w - j)],
                                        q_h[64 * c:64 * c + 64, i * P:(i + 1) * P],
                                        k_h[64 * c:64 * c + 64, j:min(j + 512, w)], start=True, stop=True)
                    ins.then_inc(s_done, 1)

                def values(i):
                    pe.wait_ge(pt_ev, 8 * h + i + 1)
                    if i < 2:
                        pe.wait_ge(pv_ev, 8 * h)
                    else:
                        pe.wait_ge(pv_ev, 8 * h + i - 1)
                    for j in range(i + 1):
                        ins = pe.matmul(ps[:, 6 + i % 2, 0:P], v_nat[:, j * P:(j + 1) * P],
                                        prob_t[i % 2][:, j * P:(j + 1) * P], start=(j == 0), stop=(j == i))
                    ins.then_inc(pv_done, 1)
                scores(0)
                scores(1)
                pe.wait_ge(k_ev, h + 1)
                for i in range(8):
                    if i < 7:
                        scores(2 * i + 2)
                        scores(2 * i + 3)
                    pe.wait_ge(w_comb, 8 * h + i + 1)
                    pe.wait_ge(pt_ev, 8 * h + i)
                    for j in range(i + 1):
                        ins = pe.transpose(flat(4, 1024)[:, j * P:(j + 1) * P], prob[2 * (i % 2)][:, j * P:(j + 1) * P],
                                           ident[:, :])
                    ins.then_inc(pt_t, 1)
                    if i:
                        values(i - 1)
                values(7)
                pe.wait_ge(asq_ready, h + 1)
                pe_roots(pe, HEAD_Q + h, HEAD_D + 8 * h, [squares_h], diag_h, SEQ, 4)

        def act_heads(act):
            with act.Fori(0, HEADS) as h:
                act.wait_ge(vk_t, 2 * h + 1)
                act.activation(v_nat, flat(4, 1024), ACT.Copy)
                act.activation(kv_s_nat[:, 1, ds(h, 1), :], ps[0:TS, 6:7, 0:P], ACT.Copy).then_inc(v_ev, 1)

                def exp(n):
                    i, w = n // 2, (n // 2 + 1) * P
                    act.wait_ge(nm_ready, 16 * h + n + 1)
                    if i >= 2:
                        act.wait_ge(pt_t, 8 * h + i - 1)
                    act.activation(prob[n % 4][:, 0:w], flat(2 * (n % 2), 1024)[:, 0:w], ACT.Exp,
                                   bias=neg_mx[:, n % 4:n % 4 + 1], scale=SCALE_DA,
                                   accum_out=lsum[:, n % 4:n % 4 + 1]).then_inc(p_ready, 1)
                exp(0)
                exp(1)

                def out(i):
                    act.wait_ge(pv_done, 8 * h + i + 1)
                    act.activation(att[:, i * P:(i + 1) * P], ps[:, 6 + i % 2, 0:P], ACT.Copy).then_inc(pv_ev, 1)
                for i in range(8):
                    if i < 7:
                        exp(2 * i + 2)
                        exp(2 * i + 3)
                    act.wait_ge(pt_t, 8 * h + i + 1)
                    if i >= 2:
                        act.wait_ge(pv_done, 8 * h + i - 1)
                    act.activation(prob_t[i % 2][:, 0:(i + 1) * P], flat(4, 1024)[:, 0:(i + 1) * P],
                                   ACT.Copy).then_inc(pt_ev, 1)
                    if i:
                        out(i - 1)
                out(7)
                act.wait_ge(pv_ev, 8 * h + 8)
                act.activation(squares_h, att, ACT.Square).then_inc(asq_ready, 1)
                act_roots(act, HEAD_Q + h, 8)
                act.wait_ge(at_ready, h + 1)
                alone(act)
                act.activation(mix[:, 0, ds(HC + h, 1), 0:SEQ], one(normed_h), ACT.Copy,
                               scale=gains[:, GS:GS + 1]).then_inc(mix_hi, 1)

        def dve_heads(dve, chain):
            per = 16 * 2 + 8 * 3 + 4
            with dve.Fori(0, HEADS) as h:
                chain.enter(h, per)

                def maxima(n):
                    i, w = n // 2, (n // 2 + 1) * P
                    s = flat(2 * (n % 2), 1024)
                    dve.wait_ge(s_done, 16 * h + n + 1)
                    chain.link(dve.tensor_tensor(s[:, i * P:w], s[:, i * P:w], causal[:, :], ALU.add))
                    chain.link(dve.tensor_reduce(mx[:, n % 2:n % 2 + 1], s[:, 0:w], AX.X, ALU.max))
                    dve.tensor_scalar(neg_mx[:, n % 4:n % 4 + 1], mx[:, n % 2:n % 2 + 1], -SCALE_DA, None,
                                      ALU.mult).then_inc(nm_ready, 1)
                maxima(0)
                maxima(1)
                dve.wait_ge(vk_t, 2 * h + 2)
                dve.tensor_copy(k_nat, flat(4, 1024))
                dve.tensor_copy(kv_s_nat[:, 0, ds(h, 1), :], ps[0:TS, 6:7, 0:P]).then_inc(k_ev, 1)
                for i in range(8):
                    a, w = 2 * (i % 2), (i + 1) * P
                    dve.wait_ge(p_ready, 16 * h + 2 * i + 2)
                    dve.wait_ge(w_comb, 8 * h + i)
                    chain.link(dve.reciprocal(rl, lsum[:, a:a + 2]))
                    chain.link(dve.tensor_scalar(rl[:, 1:2], rl[:, 1:2], neg_lam, None, ALU.mult))
                    chain.link(dve.tensor_scalar(prob[a + 1][:, 0:w], prob[a + 1][:, 0:w], rl[:, 1:2], None, ALU.mult))
                    dve.scalar_tensor_tensor(prob[a][:, 0:w], prob[a][:, 0:w], rl[:, 0:1], prob[a + 1][:, 0:w],
                                             ALU.mult, ALU.add).then_inc(w_comb, 1)
                    if i < 7:
                        maxima(2 * i + 2)
                        maxima(2 * i + 3)
                dve_roots(dve, chain, HEAD_Q + h, HEAD_D + 8 * h, diag_h, SEQ, P * EPS)
                dve.tensor_tensor(normed_h, att, flat(4, SEQ), ALU.mult).then_inc(at_ready, 1)
                dve.wait_ge(mix_hi, h + 1)
                dve.scalar_tensor_tensor(mix[:, 1, ds(HC + h, 1), 0:SEQ], one(normed_h), gains[:, GS:GS + 1],
                                         mix[:, 0, ds(HC + h, 1), 0:SEQ], ALU.mult,
                                         ALU.subtract).then_inc(head_done, 1)
            chain.leave(HEADS)

        def load_pages(sp):
            sp.wait_ge(ids_loaded, 16)
            sp.wait_ge(mm_done, CXB + 12)
            with sp.Fori(0, NB // 2) as i:
                for f in range(4 * NPG):
                    b, cache = (f // NPG) % 2, cache_k if f < 2 * NPG else cache_v
                    n = (2 * i + b) * NPG + f % NPG
                    page = sp.value_load(page_ids[0:1, ds(n, 1)], min_val=0, max_val=cache_k.shape[1] - 1)
                    if f >= RING:
                        sp.wait_ge(page_used, 4 * NPG * i + f - RING + 1)
                    else:
                        sp.wait_ge(page_used, 4 * NPG * i)
                    alone(sp)
                    sp.dma_start(ring[:, f % RING, :],
                                 cache[0, ds(page, 1), :, :, :].rearrange("a t h e -> (a t) (h e)")
                                 ).then_inc(page_loaded[f % RING], 16)

        PT_A, PT_B = 8, NPG + 1 - 8

        def pe_samples(pe):
            pe.wait_ge(kv_stored, 32 * HEADS)
            for b in range(NB):
                ins = pe.transpose(ps[0:TS, 7, 32 * b:32 * b + 32], smask[:, 32 * b:32 * b + 32], ident[0:TS, 0:TS])
            ins.then_inc(mask_t, 1)
            with pe.Fori(0, NB // 2) as i:
                def page_ready(f):
                    pe.wait_ge(page_loaded[f % RING], 16 * (4 * NPG // RING * i + f // RING + 1))

                def bank7(n):
                    pe.wait_ge(misc7_ev, 8 * i + n + 1)

                def own(b):
                    pe.wait_ge(qc_ready, 2 * i + b + 1)
                    bank7(b)
                    for h in range(HEADS):
                        ins = pe.matmul(ps[0:TS, 7, 0:TS], q_cur[b][:, 32 * h:32 * h + 32], kT[:, h, SEQ:T],
                                        start=(h == 0), stop=(h == HEADS - 1))
                    ins.then_inc(misc7_t, 1)

                def key_page(f):
                    page_ready(f)
                    pe.wait_ge(kp_ev[f % 2], NPG * i + f // 2)
                    for h in range(HEADS):
                        ins = pe.transpose(ps[:, f % 2, h * P:(h + 1) * P], ring[:, f % RING, h * P:(h + 1) * P],
                                           ident[:, :])
                    ins.then_inc(page_used, 1)

                def key_scores(f):
                    pe.wait_ge(kp_ev[f % 2], NPG * i + f // 2 + 1)
                    b, p = f // NPG, f % NPG
                    if p % 4 == 0:
                        if b:
                            pe.wait_ge(exps, 10 * i + p // 4 + 2)
                        else:
                            pe.wait_ge(exps, 10 * i)
                    for h in range(HEADS):
                        ins = pe.matmul(ps[0:TS, 2 + p // 4, (p % 4) * P:(p % 4 + 1) * P],
                                        q_cur[b][:, 32 * h:32 * h + 32], k_page_t[f % 2][:, h * P:(h + 1) * P],
                                        start=(h == 0), stop=(h == HEADS - 1))
                    ins.then_inc(kp_used, 1)

                def weights_t(b, half_):
                    pe.wait_ge(exps, 10 * i + 5 * (b + 1))
                    bank7(2 + 2 * b + half_)
                    alone(pe)
                    for q in range(PT_B if half_ else PT_A):
                        p = q + PT_A * half_
                        w = P if p < NPG else TS
                        ins = pe.transpose(ps[0:w, 7, q * TS:(q + 1) * TS], probs_s[b][:, p * P:p * P + w],
                                           ident[0:TS, 0:TS])
                    ins.then_inc(misc7_t, 1)

                def outputs_t(b):
                    bank7(6 + b)
                    pe.wait_ge(o_ev, 2 * i + b + 1)
                    alone(pe)
                    for h in range(HEADS):
                        ins = pe.transpose(ps[:, 7, 32 * h:32 * h + 32], o_nat[:, h * P:(h + 1) * P],
                                           ident[0:TS, 0:TS])
                    ins.then_inc(misc7_t, 1)

                def values(b, between):
                    pe.wait_ge(misc7_ev, 8 * i + 5 + 2 * b)
                    pe.wait_ge(o_ev, 2 * i + b)
                    for p in range(NPG):
                        f = (2 + b) * NPG + p
                        page_ready(f)
                        pe.matmul(ps[0:TS, 6, :], probs_t[b][:, p * TS:(p + 1) * TS], ring[:, f % RING, :],
                                  start=(p == 0), stop=False).then_inc(page_used, 1)
                        if p in between:
                            between[p]()
                    pe.matmul(ps[0:TS, 6, :], probs_t[b][0:TS, NPG * TS:(NPG + 1) * TS],
                              kv_s_nat[:, 1, :, :].rearrange("p h e -> p (h e)"), start=False,
                              stop=True).then_inc(o_done, 1)

                for b in range(2):
                    own(b)
                    for p in range(NPG):
                        f = b * NPG + p
                        key_page(f)
                        if p:
                            key_scores(f - 1)
                        if b and p == 7:
                            weights_t(0, 0)
                        if b and p == 9:
                            weights_t(0, 1)
                    key_scores(b * NPG + NPG - 1)
                values(0, {6: lambda: weights_t(1, 0), 8: lambda: weights_t(1, 1)})
                values(1, {3: lambda: outputs_t(0)})
                outputs_t(1)
            pe.wait_ge(asq_ready, HEADS + 1)
            pe_roots(pe, SAMPLE_Q, SAMPLE_D, [arena[:, 26, 0:P]], arena[:, 26, P:2 * P], P, 4)

        def evac_page(eng, i, f):
            eng.wait_ge(kp_used, 2 * NPG * i + f - 1) if f >= 2 else eng.wait_ge(kp_used, 2 * NPG * i)
            eng.wait_ge(page_used, 4 * NPG * i + f + 1)

        def act_samples(act):
            with act.Fori(0, NB // 2) as i:
                def exp(b):
                    act.wait_ge(max_ready, 2 * i + b + 1)
                    act.activation(probs_s[b][:, 2 * SEQ:2 * SEQ + TS], own_s[b], ACT.Exp, scale=SCALE_DA,
                                   bias=sm_neg[b], accum_out=sm_sum[b][:, 4:5]).then_inc(exps, 1)
                    for j in range(4):
                        act.activation(probs_s[b][:, 512 * j:512 * (j + 1)], ps[0:TS, 2 + j, :], ACT.Exp,
                                       scale=SCALE_DA, bias=sm_neg[b],
                                       accum_out=sm_sum[b][:, j:j + 1]).then_inc(exps, 1)
                for f in range(0, 2 * NPG, 2):
                    evac_page(act, i, f)
                    act.activation(k_page_t[0], ps[:, 0, :], ACT.Copy).then_inc(kp_ev[0], 1)
                    if f == NPG:
                        exp(0)
                exp(1)
            act.wait_ge(att_ready, NB)
            act.activation(arena[:, 26, 0:P], arena[:, 24, 0:P], ACT.Square).then_inc(asq_ready, 1)
            act_roots(act, SAMPLE_Q, 1)
            act.wait_ge(at_ready, HEADS + 1)
            act.activation(mix[:, 0, HC:KD, SEQ:T], arena[:, 27, 0:P].rearrange("p (h t) -> p h t", h=HEADS), ACT.Copy,
                           scale=gains[:, GS:GS + 1]).then_inc(mix_hi, 1)

        def dve_samples(dve, chain):
            dve.wait_ge(kv_stored, 32 * HEADS)
            for b in range(2):
                chain.mark(dve.memset(q_cur[b], 0.0))
            dve.wait_ge(mask_t, 1)
            dve.tensor_copy(smask_n.rearrange("p b t -> p (b t)"), ps[0:TS, 7, 0:256]).then_inc(misc7_ev, 1)
            chain.sync()
            dve.wait_ge(misc7_ev, 1)
            per = 2 * 4
            with dve.Fori(0, NB // 2) as i:
                chain.enter(i, per)

                def bank7_done(n):
                    dve.wait_ge(misc7_t, 8 * i + n + 1)

                def bank_max(b, j):
                    dve.wait_ge(kp_used, 2 * NPG * i + NPG * b + 4 * j + 4)
                    ins = dve.tensor_reduce(sm_max[b][:, j:j + 1], ps[0:TS, 2 + j, :], AX.X, ALU.max)
                    if j == 3:
                        chain.link(ins)
                        chain.link(dve.tensor_reduce(sm_max[b][:, 0:1], sm_max[b], AX.X, ALU.max))
                        dve.tensor_scalar(sm_neg[b], sm_max[b][:, 0:1], -SCALE_DA, None, ALU.mult).then_inc(
                            max_ready, 1)

                def weights_t(b, half_):
                    bank7_done(2 + 2 * b + half_)
                    if half_ == 0:
                        dve.tensor_copy(probs_t[b][:, 0:PT_A * TS], ps[:, 7, 0:PT_A * TS]).then_inc(misc7_ev, 1)
                    else:
                        n = (PT_B - 1) * TS
                        dve.tensor_copy(probs_t[b][:, PT_A * TS:NPG * TS], ps[:, 7, 0:n])
                        dve.tensor_copy(probs_t[b][0:TS, NPG * TS:(NPG + 1) * TS], ps[0:TS, 7, n:n + TS]).then_inc(
                            misc7_ev, 1)

                def out(b):
                    dve.wait_ge(exps, 10 * i + 5 * (b + 1))
                    chain.link(dve.tensor_reduce(sm_rl[b], sm_sum[b], AX.X, ALU.add))
                    chain.link(dve.reciprocal(sm_rl[b], sm_rl[b]))
                    dve.wait_ge(o_done, 2 * i + b + 1)
                    if b:
                        bank7_done(6)
                    else:
                        dve.wait_ge(misc7_t, 8 * i)
                    dve.tensor_scalar(o_nat, ps[0:TS, 6, :], sm_rl[b], None, ALU.mult).then_inc(o_ev, 1)

                def out_t(b):
                    bank7_done(6 + b)
                    dve.tensor_copy(sm_t[:, 0:P], ps[:, 7, 0:P]).then_inc(misc7_ev, 1)
                    dve.wait_ge(misc7_ev, 8 * i + 8 + b)
                    o = sm_t.rearrange("p (h n) -> p h n", n=40)
                    dve.scalar_tensor_tensor(att_s[:, :, ds(8 * i + 4 * b, 4)], o[:, :, 4:8], neg_lam,
                                             o[:, :, 0:4], ALU.mult, ALU.add).then_inc(att_ready, 1)

                dve.wait_ge(kp_used, 2 * NPG * i)
                for b in range(2):
                    for c in range(2):
                        ins = dve.tensor_copy(
                            q_cur[b][64 * c:64 * c + 64, :].rearrange("p (h n) -> p h n", n=40)[:, :, 4 * c:4 * c + 4],
                            qT[64 * c:64 * c + 64, :, ds(8 * i + SEQ + 4 * b, NS)])
                    ins.then_inc(qc_ready, 1)
                for b in range(2):
                    bank7_done(b)
                    dve.tensor_tensor(own_s[b].rearrange("p (a t) -> p a t", a=1),
                                      ps[0:TS, 7, 0:TS].rearrange("p (a t) -> p a t", a=1),
                                      smask_n[:, ds(2 * i + b, 1), :], ALU.add).then_inc(misc7_ev, 1)
                    dve.wait_ge(misc7_ev, 8 * i + 2 + b)
                    dve.tensor_reduce(sm_max[b][:, 4:5], own_s[b], AX.X, ALU.max)
                    for p in range(1, NPG, 2):
                        if b and p == 1:
                            bank_max(0, 3)
                        evac_page(dve, i, NPG * b + p)
                        dve.tensor_copy(k_page_t[1], ps[:, 1, :]).then_inc(kp_ev[1], 1)
                        if p % 4 == 1 and p > 1:
                            bank_max(b, p // 4 - 1)
                        if b and p == 7:
                            weights_t(0, 0)
                        if b and p == 9:
                            weights_t(0, 1)
                bank_max(1, 3)
                weights_t(1, 0)
                weights_t(1, 1)
                out(0)
                out_t(0)
                out(1)
                out_t(1)
            chain.leave(NB // 2)
            dve_roots(dve, chain, SAMPLE_Q, SAMPLE_D, arena[:, 26, P:2 * P], P, P * EPS)
            dve.wait_ge(att_ready, NB)
            t = arena[:, 27, 0:P]
            dve.tensor_tensor(t, arena[:, 24, 0:P], flat(4, P), ALU.mult).then_inc(at_ready, 1)
            dve.wait_ge(mix_hi, HEADS + 1)
            dve.scalar_tensor_tensor(mix[:, 1, HC:KD, SEQ:T], t.rearrange("p (h t) -> p h t", h=HEADS),
                                     gains[:, GS:GS + 1], mix[:, 0, HC:KD, SEQ:T], ALU.mult,
                                     ALU.subtract).then_inc(mix_ready, 1)

        hn = mix
        q1, k1, v1, o1 = rows(8, 2), rows(10, 2), rows(12, 2), rows(14, 2)
        flat_rows = lambda a, n: rows(a, n).rearrange("p a t -> p (a t)")
        wk = flat_rows(16, 3)[:, 0:NTT * MLD].rearrange("p (c d) -> p c d", c=NTT)
        ML1 = MLD + 1
        vn = flat_rows(19, 3)[:, 0:NTT * ML1].rearrange("p (c e) -> p c e", c=NTT)
        hc = flat_rows(22, 3)[:, 0:NTT * MLD].rearrange("p (c e) -> p c e", c=NTT)
        m_bc, i_bc = arena[:, 25, :], arena[:, 27, :]
        state = [arena[:, 26, 2 * ML1 * i:2 * ML1 * (i + 1)].rearrange("p (k e) -> p k e", k=2) for i in range(2)]
        spare = flat_rows(16, 3)[:, NTT * MLD:]
        den_ = spare[:, 0:1]
        rec_ = [spare[:, 1 + i:2 + i] for i in range(2)]
        sums, neg_mean, sqs = (spare[:, 16 * i:16 * i + NTT] for i in (1, 2, 3))
        junk = spare[:, 64:64 + MLD]
        sd = flat_rows(10, 2)[:, 0:NTT * P]
        dec = flat_rows(12, 2)[:, 0:NTT * P]
        m_row, i_row, e_row = (hT[0:HEADS, k, :] for k in range(3))
        cs = [hT[:, 3, 2 * ML1 * i:2 * ML1 * (i + 1)].rearrange("p (k e) -> p k e", k=2) for i in range(2)]
        cs_new = [hT[:, 5, 2 * ML1 * i:2 * ML1 * (i + 1)].rearrange("p (k e) -> p k e", k=2) for i in range(2)]
        q_pad = hT[:, 6, 0:2 * 288].rearrange("p (k n) -> p k n", k=2)
        wk_b = [hT[0:TS, 7, MLD * i:MLD * (i + 1)] for i in range(2)]
        n_nat = hT[0:1 + NB, 7, 640:896]
        r = lambda k: arena[0:HEADS, k, :]
        li, fx, fa, fe, fl, bc, aa, we, mt = (r(16 + k) for k in range(9))
        acol = sb("acol", [P, 3, NTT, HEADS])
        a_h = sb("a_h", [P, 3, NTT])
        sel_h = sb("sel_h", [HEADS, P])
        reset = hT[0:HEADS, 4, :]
        m_prev = sb("m_prev", [HEADS, 16])
        m_last = sb("m_last", [HEADS, 16])
        m_out = sb("m_out", [HEADS, 1 + NB])
        decay = sb("decay", [HEADS, 16])
        d_h = sb("d_h", [P, 16])
        b_if = sb("b_if", [HEADS, 2])
        nT = sb("nT", [P, NB, HEADS, 2])
        n_h = sb("n_h", [P, NB, 2])
        n_new = sb("n_new", [P, 2, 1 + NB])
        g_h = sb("g_h", [P, 2])
        spill = nc.dram_tensor("h_spill", (P, KD, T), F32, kind="Internal").ap()

        bif_loaded, m0_loaded = sem("bif_loaded"), sem("m0_loaded")
        r_act, r_dve = sem("r_act"), sem("r_dve")
        col_t, col_ev = sem("col_t"), sem("col_ev")
        rows_ready = sem("rows_ready")
        m_stored = sem("m_stored")
        selh_ready = sem("selh_ready")
        bc_t, bc_act, bc_dve = sem("bc_t"), sem("bc_act"), sem("bc_dve")
        kn_t, kn_ev, vn_t, vn_ev = sem("kn_t"), sem("kn_ev"), sem("vn_t"), sem("vn_ev")
        st_done, dx_ready, dec_ready, sd_ready, qi_ready = (sem(n) for n in ("st_done", "dx_ready", "dec_ready",
                                                                             "sd_ready", "qi_ready"))
        up_done, state_ready, num_done = sem("up_done"), sem("state_ready"), sem("num_done")
        cs_loaded, nc_ready, wkb_ready = [sem("cs_loaded0"), sem("cs_loaded1")], sem("nc_ready"), sem("wkb_ready")
        inter_done = sem("inter_done")
        ups_done, cs_ready, cs_stored = sem("ups_done"), sem("cs_ready"), [sem("cs_stored0"), sem("cs_stored1")]
        state_stored, n_made, n_t = sem("state_stored"), sem("n_made"), sem("n_t")
        n_ev, n_stored = sem("n_ev"), sem("n_stored")
        hc_ready = sem("hc_ready")
        stat_ready = sem("stat_ready")
        mr_in, mr_out = sem("mr_in"), sem("mr_out")
        hs_ready = sem("hs_ready")
        hs_t = sem("hs_t")
        hn_hi, hn_done = sem("hn_hi"), sem("hn_done")

        def chunks(row):
            return row[:, 0:SEQ].rearrange("p (c t) -> p c t", t=P)

        def samples(row):
            return row[:, SEQ:T].rearrange("p (b t) -> p b t", b=NB)

        def pe_gates(pe):
            pe.wait_ge(u_ready, KD * 3)
            pe.wait_ge(evac[1], GATES // 2)
            products(pe, GATES, 0, u, KD, m=HEADS, n=8, col=0, bank=0, signal=False)
            products(pe, GATES, 0, u, KD, m=HEADS, n=8, col=HEADS, bank=3)
            pe.wait_ge(evac[0], GATES // 2 + 1)
            pe.wait_ge(rows_ready, 1)
            for k, src in enumerate((aa, we, e_row)):
                for c in range(NTT):
                    w = P if c < NTT - 1 else TS
                    ins = pe.transpose(ps[0:w, 6, (k * NTT + c) * HEADS:(k * NTT + c + 1) * HEADS],
                                       src[:, c * P:c * P + w], ident[0:HEADS, 0:HEADS])
            ins.then_inc(col_t, 1)

        def act_gates(act, chain):
            split_hi(act, QKVO, 0, KD)
            act.wait_ge(mm_done, GATES + 1)
            act.wait_ge(bif_loaded, 16)
            act.activation(by3(li), ps[0:HEADS, 0:3, 0:GW], ACT.Identity, scale=1 / WS, bias=b_if[:, 0:1])
            act.activation(by3(fx), ps[0:HEADS, 3:6, 0:GW], ACT.Identity, scale=1 / WS,
                           bias=b_if[:, 1:2]).then_inc(evac[0], 1)
            act.wait_ge(r_dve, 1)
            chain.link(act.activation(fe, fa, ACT.Exp, scale=-1.0))
            act.activation(fl, fe, ACT.Ln, bias=1.0).then_inc(r_act, 1)
            act.wait_ge(r_dve, 2)
            act.activation(we, we, ACT.Exp)
            act.activation(i_row, i_row, ACT.Exp)
            act.activation(decay[:, :], decay[:, :], ACT.Exp)
            act.activation(e_row, mt, ACT.Exp, scale=-1.0).then_inc(rows_ready, 1)

        def dve_gates(dve, chain):
            split_lo(dve, QKVO, 0, KD)
            dve.wait_ge(spilled, 16)
            chain.link(dve.memset(reset, 1.0))
            dve.memset(chunks(reset)[:, :, 0:1], 0.0)
            chain.mark(dve.memset(samples(reset)[:, :, 0:1], 0.0))
            chain.mark(dve.memset(m_prev[:, 0:1], 0.0))
            chain.mark(dve.memset(acol[:, :, :, :], 0.0))
            chain.mark(dve.memset(hT[:, 6, 0:2 * 288], 0.0))
            dve.wait_ge(evac[0], GATES // 2 + 1)
            dve.scalar_tensor_tensor(fa, fx, -1.0, fx, ALU.mult, ALU.max).then_inc(r_dve, 1)
            chain.link(dve.tensor_scalar(mt, fx, 0.0, None, ALU.min))
            dve.wait_ge(r_act, 1)
            chain.link(dve.tensor_tensor(fl, mt, fl, ALU.subtract))
            chain.link(dve.tensor_tensor_scan(bc, reset, fl, 0.0, ALU.mult, ALU.add))
            chain.link(dve.tensor_tensor(aa, li, bc, ALU.subtract))
            dve.wait_ge(m0_loaded, 16)
            for c in range(8):
                m_c, a_c = m_row[:, c * P:(c + 1) * P], aa[:, c * P:(c + 1) * P]
                chain.link(dve.tensor_tensor_scan(m_c, a_c, a_c, m_prev[:, c:c + 1], ALU.max, ALU.max))
                if c < 7:
                    chain.link(dve.tensor_tensor(m_prev[:, c + 1:c + 2], bc[:, c * P + P - 1:c * P + P],
                                                 m_row[:, c * P + P - 1:c * P + P], ALU.add))
            for t in range(NS):
                before = m_prev[:, 8:16] if t == 0 else samples(m_row)[:, :, t - 1]
                chain.link(dve.tensor_tensor(samples(m_row)[:, :, t], before, samples(aa)[:, :, t], ALU.max))
            chain.mark(dve.tensor_copy(m_last[:, 0:8], chunks(m_row)[:, :, P - 1]))
            chain.link(dve.tensor_copy(m_last[:, 8:16], samples(m_row)[:, :, NS - 1]))
            dve.tensor_tensor(chunks(we), chunks(aa), m_last[:, 0:8].rearrange("p (c a) -> p c a", a=1).to_broadcast(
                [HEADS, 8, P]), ALU.subtract)
            dve.tensor_tensor(samples(we), samples(aa), m_last[:, 8:16].rearrange("p (c a) -> p c a", a=1)
                              .to_broadcast([HEADS, NB, NS]), ALU.subtract)
            dve.tensor_tensor(chunks(i_row), m_prev[:, 0:8].rearrange("p (c a) -> p c a", a=1).to_broadcast(
                [HEADS, 8, P]), chunks(m_row), ALU.subtract)
            dve.tensor_tensor(samples(i_row), m_prev[:, 8:16].rearrange("p (c a) -> p c a", a=1).to_broadcast(
                [HEADS, NB, NS]), samples(m_row), ALU.subtract)
            dve.tensor_tensor(decay[:, :], m_prev[:, :], m_last[:, :], ALU.subtract)
            chain.link(dve.tensor_tensor(mt, bc, m_row, ALU.add))
            dve.tensor_copy(m_out[:, 0:1], mt[:, SEQ - 1:SEQ])
            dve.tensor_copy(m_out[:, 1:1 + NB], samples(mt)[:, :, NS - 1]).then_inc(r_dve, 1)
            dve.wait_ge(col_t, 1)
            dve.tensor_copy(acol[:, :, 0:8, :], ps[:, 6, 0:3 * NTT * HEADS].rearrange(
                "p (k c h) -> p k c h", k=3, c=NTT)[:, :, 0:8, :])
            chain.mark(dve.tensor_copy(acol[0:TS, :, 8:9, :], ps[0:TS, 6, 0:3 * NTT * HEADS].rearrange(
                "p (k c h) -> p k c h", k=3, c=NTT)[:, :, 8:9, :]))
            chain.mark(dve.memset(vn[:, :, MLD:ML1], 1.0))
            chain.sync()

        def head_src(h, m):
            return w_cols(w_in1[0], ds((m // 2) * D + (m % 2) * P + h * MLD, P))

        def act_mlstm(act, chain):
            per = 2 * NTT
            with act.Fori(0, HEADS) as h:
                chain.enter(h, per)

                def tokens(t, out):
                    n = t if out is vn else 5 + t
                    act.wait_ge(vn_t, 10 * h + n + 1)
                    if t < 4:
                        act.activation(out[:, 2 * t:2 * t + 2, 0:MLD],
                                       ps[:, 7, :].rearrange("p (a e) -> p a e", a=2), ACT.Copy).then_inc(vn_ev, 1)
                    else:
                        act.activation(out[0:TS, 8, 0:MLD], ps[0:TS, 7, 0:MLD], ACT.Copy).then_inc(vn_ev, 1)

                def normaliser(b):
                    act.wait_ge(inter_done, NB * h + b - 1) if b >= 2 else act.wait_ge(inter_done, NB * h)
                    act.wait_ge(cs_ready, NB * h + b - 1) if b >= 2 else act.wait_ge(cs_ready, NB * h)
                    act.activation(cs[b % 2][:, :, MLD:ML1], n_h[:, b, :].rearrange("p (k a) -> p k a", a=1),
                                   ACT.Copy).then_inc(nc_ready, 1)

                def statistics(c):
                    w = P if c < NTT - 1 else TS
                    act.wait_ge(hc_ready, NTT * h + c + 1)
                    chain.link(act.activation(junk[0:w, :], hc[0:w, c, :], ACT.Copy, accum_out=sums[0:w, c:c + 1]))
                    chain.link(act.activation(neg_mean[0:w, c:c + 1], sums[0:w, c:c + 1], ACT.Copy, scale=-1 / MLD))
                    act.activation(junk[0:w, :], hc[0:w, c, :], ACT.Square, bias=neg_mean[0:w, c:c + 1],
                                   accum_out=sqs[0:w, c:c + 1]).then_inc(stat_ready, 1)
                    act.wait_ge(stat_ready, NTT * h + c + 1)
                for m in range(8):
                    c, r_ = QKVO + m, 4 * h
                    split_hi(act, c + 1, r_, KD)
                    if m in (2, 3):
                        continue
                    act.wait_ge(mm_done, at(c, r_))
                    if m == 0:
                        act.wait_ge(hn_done, h)
                    dst = {0: q1, 4: v1, 6: o1}[m - m % 2][:, m % 2, :]
                    act.activation(by3(dst), group(3 * (c % 2)), ACT.Sigmoid if m >= 6 else ACT.Copy,
                                   scale=1 / WS).then_inc(evac[c % 2], 1)
                act.wait_ge(bc_t, 3 * h + 1)
                act.activation(by3(m_bc), group(0), ACT.Copy).then_inc(bc_act, 1)
                for t in range(5):
                    tokens(t, vn)
                act.wait_ge(dx_ready, h + 1)
                act.activation(dec[:, 0:SEQ], dec[:, 0:SEQ], ACT.Exp, scale=-1.0)
                act.activation(dec[0:TS, SEQ:SEQ + TS], dec[0:TS, SEQ:SEQ + TS], ACT.Exp,
                               scale=-1.0).then_inc(dec_ready, 1)
                for t in range(5):
                    tokens(t, hc)
                act.wait_ge(selh_ready, h + 1)
                normaliser(0)
                normaliser(1)
                for c in range(8):
                    statistics(c)
                act.wait_ge(mr_in, 2 * h + 1)
                act.activation(roots[:, 1, 0:8], roots[:, 0, 0:8], ACT.Abs_reciprocal_sqrt).then_inc(mr_out, 1)
                for b in range(2, NB):
                    normaliser(b)
                statistics(8)
                act.wait_ge(mr_in, 2 * h + 2)
                act.activation(roots[0:TS, 1, 8:9], roots[0:TS, 0, 8:9], ACT.Abs_reciprocal_sqrt).then_inc(mr_out, 1)
                for k in range(2):
                    act.wait_ge(hs_t, 2 * h + k + 1)
                    alone(act)
                    act.activation(hn[:, 0, ds(2 * h + k, 1), :], one(flat(3 * k, T)), ACT.Copy,
                                   scale=g_h[:, k:k + 1]).then_inc(hn_hi, 1)
            chain.leave(HEADS)

        def pe_mlstm(pe):
            with pe.Fori(0, HEADS) as h:
                for m in range(8):
                    if m == 0:
                        pe.wait_ge(hn_done, h)
                    products(pe, QKVO + m, 4 * h, u, KD)
                pe.wait_ge(selh_ready, h + 1)
                pe.wait_ge(evac[0], out_of_banks(QKVO + 7, 4 * h))
                pe.wait_ge(evac[1], out_of_banks(QKVO + 6, 4 * h))
                for src, bank in ((m_row, 0), (i_row, 3)):
                    for g in range(3):
                        ins = pe.matmul(ps[:, bank + g, 0:GW], sel_h[:, :], src[:, g * GW:(g + 1) * GW],
                                        start=True, stop=True)
                    ins.then_inc(bc_t, 1)
                pe.matmul(ps[:, 6, 0:16], sel_h[:, :], decay[:, :], start=True, stop=True).then_inc(bc_t, 1)
                def tokens(t, src, bank, done):
                    for tt in range(2 * t, min(2 * t + 2, NTT)):
                        w = P if tt < NTT - 1 else TS
                        for k in range(2):
                            o = (tt % 2) * MLD + k * P
                            ins = pe.transpose(ps[0:w, bank, o:o + P], src[:, k, tt * P:tt * P + w], ident[:, :])
                    ins.then_inc(done, 1)
                for t in range(5):
                    if t == 0:
                        pe.wait_ge(bc_dve, 2 * h + 2)
                    else:
                        pe.wait_ge(kn_ev, 5 * h + t)
                    tokens(t, k1, 6, kn_t)
                    pe.wait_ge(vn_ev, 10 * h + t)
                    tokens(t, v1, 7, vn_t)
                pe.wait_ge(bc_act, h + 1)
                for c in range(NTT):
                    w = P if c < NTT - 1 else TS
                    for k in range(2):
                        ins = pe.matmul(ps[0:w, c // 4, (c % 4) * P:(c % 4) * P + w], k1[:, k, c * P:c * P + w],
                                        q1[:, k, c * P:c * P + w], start=(k == 0), stop=(k == 1))
                ins.then_inc(st_done, 1)
                for t in range(5):
                    pe.wait_ge(vn_ev, 10 * h + 5 + t)
                    tokens(t, o1, 7, vn_t)
                pe.wait_ge(kn_ev, 5 * h + 5)
                pe.wait_ge(vn_ev, 10 * h + 5)
                pe.wait_ge(bc_dve, 2 * h + 1)

                def update(c):
                    if c >= 2:
                        pe.wait_ge(state_ready, 8 * h + c - 1)
                    for k in range(2):
                        ins = pe.matmul(ps[:, 3 + 2 * (c % 2) + k, 0:ML1], wk[:, c, k * P:(k + 1) * P], vn[:, c, :],
                                        start=True, stop=True)
                    ins.then_inc(up_done, 1)

                def numerators(c):
                    if c == 0:
                        pe.wait_ge(sd_ready, h + 1)
                        pe.wait_ge(qi_ready, h + 1)
                        pe.wait_ge(vn_ev, 10 * h + 10)
                    else:
                        pe.wait_ge(state_ready, 8 * h + c)
                    if c >= 2:
                        pe.wait_ge(hc_ready, NTT * h + c - 1)
                    o = ps[:, 7 if c % 2 == 0 else 0, 0:ML1]
                    for k in range(2 if c else 0):
                        pe.matmul(o, q1[:, k, c * P:(c + 1) * P], state[c % 2][:, k, :], start=(k == 0), stop=False)
                    pe.matmul(o, sd[:, c * P:(c + 1) * P], vn[:, c, :], start=(c == 0), stop=True).then_inc(
                        num_done, 1)
                update(0)
                for c in range(8):
                    if c < 7:
                        update(c + 1)
                    numerators(c)
                pe.matmul(ps[0:TS, 2, 0:ML1], sd[0:TS, SEQ:SEQ + TS], vn[0:TS, 8, :], start=True, stop=False)
                for b in range(NB):
                    pe.wait_ge(cs_loaded[b % 2], 16 * (NB // 2 * h + b // 2 + 1))
                    pe.wait_ge(nc_ready, NB * h + b + 1)
                    for k in range(2):
                        ins = pe.matmul(ps[0:TS, 2, 0:ML1], q_pad[:, k, TS * b:TS * (b + 1)], cs[b % 2][:, k, :],
                                        start=False, stop=(b == NB - 1 and k == 1))
                    ins.then_inc(inter_done, 1)
                    pe.wait_ge(wkb_ready, NB * h + b + 1)
                    if b < 2:
                        pe.wait_ge(state_ready, 8 * h + 7 + b)
                    else:
                        pe.wait_ge(cs_ready, NB * h + b - 1)
                    for k in range(2):
                        ins = pe.matmul(ps[:, 3 + 2 * (b % 2) + k, 0:ML1], wk_b[b % 2][:, k * P:(k + 1) * P],
                                        vn[0:TS, 8, :], start=True, stop=True)
                    ins.then_inc(ups_done, 1)
                pe.wait_ge(hs_ready, 2 * h + 1)
                pe.wait_ge(n_made, h + 1)
                for k in range(2):
                    ins = pe.transpose(ps[0:1 + NB, 7, k * P:(k + 1) * P], n_new[:, k, :], ident[:, :])
                ins.then_inc(n_t, 1)
                for k in range(2):
                    for c in range(8):
                        pe.transpose(flat(3 * k, T)[:, c * P:(c + 1) * P], hc[:, c, k * P:(k + 1) * P], ident[:, :])
                pe.wait_ge(hs_ready, 2 * h + 2)
                alone(pe)
                for k in range(2):
                    pe.transpose(ps[:, 3 * k + 2, 0:TS], hc[0:TS, 8, k * P:(k + 1) * P],
                                 ident[0:TS, 0:TS]).then_inc(hs_t, 1)

        def dve_mlstm(dve, chain):
            per = 3 * NTT + 2 * 4 + NB + 1
            with dve.Fori(0, HEADS) as h:
                chain.enter(h, per)
                dve.wait_ge(hn_done, h)
                dve.tensor_copy(sel_h[:, :].rearrange("p (a n) -> p a n", a=1), sel[:, ds(h, 1), :])
                dve.tensor_copy(a_h[:, :, :], acol[:, :, :, ds(h, 1)].rearrange("p k c a -> p k (c a)"))
                dve.tensor_copy(g_h[:, :], gains[:, ds(GM + 2 * h, 2)])
                dve.tensor_copy(n_h[:, :, :], nT[:, :, ds(h, 1), :].rearrange("p b a k -> p (b a) k")).then_inc(
                    selh_ready, 1)
                for m in range(8):
                    c, r_ = QKVO + m, 4 * h
                    split_lo(dve, c + 1, r_, KD)
                    if m in (2, 3):
                        dve.wait_ge(mm_done, at(c, r_))
                        dve.tensor_scalar(by3(k1[:, m % 2, :]), group(3 * (c % 2)), MLD ** -0.5 / WS, None,
                                          ALU.mult).then_inc(evac[c % 2], 1)
                dve.wait_ge(selh_ready, h + 1)
                dve.wait_ge(bc_t, 3 * h + 2)
                dve.tensor_copy(by3(i_bc), group(3)).then_inc(bc_dve, 1)
                dve.wait_ge(bc_t, 3 * h + 3)
                dve.tensor_copy(d_h[:, :], ps[:, 6, 0:16]).then_inc(bc_dve, 1)
                dve.wait_ge(bc_dve, 2 * h + 2)
                for t in range(5):
                    dve.wait_ge(kn_t, 5 * h + t + 1)
                    for tt in range(2 * t, min(2 * t + 2, NTT)):
                        w = P if tt < NTT - 1 else TS
                        ins = dve.tensor_scalar(wk[0:w, tt, :], ps[0:w, 6, (tt % 2) * MLD:(tt % 2 + 1) * MLD],
                                                a_h[0:w, 1, tt:tt + 1], None, ALU.mult)
                    ins.then_inc(kn_ev, 1)
                dve.wait_ge(bc_act, h + 1)
                dve.wait_ge(vn_t, 10 * h + 5)
                for c in range(8):
                    dve.scalar_tensor_tensor(dec[:, c * P:(c + 1) * P], m_bc[:, c * P:(c + 1) * P], a_h[:, 0, c:c + 1],
                                             dmask[:, :], ALU.subtract, ALU.max)
                dve.scalar_tensor_tensor(dec[0:TS, SEQ:SEQ + TS], m_bc[0:TS, SEQ:T], a_h[0:TS, 0, 8:9],
                                         dmask_s[:, :], ALU.subtract, ALU.max).then_inc(dx_ready, 1)
                dve.wait_ge(st_done, h + 1)
                for k in range(2):
                    ins = dve.tensor_tensor(q1[:, k, :], q1[:, k, :], i_bc, ALU.mult)
                chain.link(ins)
                dve.tensor_copy(q_pad.rearrange("p k (b n) -> p k b n", n=36)[:, :, :, 0:NS],
                                q1[:, :, SEQ:T].rearrange("p k (b t) -> p k b t", b=NB)).then_inc(qi_ready, 1)
                dve.wait_ge(dec_ready, h + 1)
                dve.wait_ge(kn_t, 5 * h + 5)
                dve.tensor_tensor(sd[:, 0:SEQ], flat(0, 1024), dec[:, 0:SEQ], ALU.mult)
                dve.tensor_tensor(sd[0:TS, SEQ:SEQ + TS], ps[0:TS, 2, 0:TS], dec[0:TS, SEQ:SEQ + TS],
                                  ALU.mult).then_inc(sd_ready, 1)

                def outputs(c, bank):
                    w = P if c < NTT - 1 else TS
                    den, d_, r_ = ps[0:w, bank, MLD:ML1], den_[0:w, :], rec_[c % 2][0:w, :]
                    chain.link(dve.tensor_tensor(d_, den, a_h[0:w, 2, c:c + 1], ALU.max))
                    chain.link(dve.scalar_tensor_tensor(d_, den, -1.0, d_, ALU.mult, ALU.max))
                    chain.link(dve.reciprocal(r_, d_))
                    dve.scalar_tensor_tensor(hc[0:w, c, :], ps[0:w, bank, 0:MLD], r_, hc[0:w, c, :], ALU.mult,
                                             ALU.mult).then_inc(hc_ready, 1)

                def normed(c0, c1, w, n):
                    dve.wait_ge(stat_ready, NTT * h + c1)
                    x, y, z = (roots[0:w, i, c0:c1] for i in range(3))
                    dve.tensor_scalar(x, sqs[0:w, c0:c1], MLD * EPS, None, ALU.add).then_inc(mr_in, 1)
                    dve.wait_ge(mr_in, 2 * h + n + 1)
                    dve.wait_ge(mr_out, 2 * h + n + 1)
                    newton(dve, chain, x, y, z)
                    for c in range(c0, c1):
                        ins = dve.tensor_scalar(hc[0:w, c, :], hc[0:w, c, :], neg_mean[0:w, c:c + 1],
                                                roots[0:w, 2, c:c + 1], ALU.add, ALU.mult)
                    ins.then_inc(hs_ready, 1)

                def next_state(c):
                    dve.wait_ge(up_done, 8 * h + c + 1)
                    up = ps[:, 3 + 2 * (c % 2):5 + 2 * (c % 2), 0:ML1]
                    if c >= 2:
                        dve.wait_ge(num_done, 8 * h + c)
                    if c == 0:
                        dve.wait_ge(state_stored, 16 * h)
                        dve.tensor_copy(state[1], up).then_inc(state_ready, 1)
                    else:
                        dve.wait_ge(state_ready, 8 * h + c)
                        dve.scalar_tensor_tensor(state[(c + 1) % 2], state[c % 2], d_h[:, c:c + 1], up, ALU.mult,
                                                 ALU.add).then_inc(state_ready, 1)
                for c in range(8):
                    next_state(c)
                    dve.wait_ge(num_done, 8 * h + c + 1)
                    outputs(c, 7 if c % 2 == 0 else 0)
                dve.wait_ge(state_ready, 8 * h + 8)
                dve.wait_ge(n_t, h)
                chain.mark(dve.tensor_copy(n_new[:, :, 0:1], state[0][:, :, MLD:MLD + 1]))
                normed(0, 8, P, 0)
                for b in range(NB):
                    if b >= 2:
                        dve.wait_ge(ups_done, NB * h + b - 1)
                    dve.wait_ge(kn_ev, 5 * h + 5)
                    dve.tensor_scalar(wk_b[b % 2], wk[0:TS, 8, :], bmask[:, b:b + 1], None, ALU.mult).then_inc(
                        wkb_ready, 1)
                    dve.wait_ge(ups_done, NB * h + b + 1)
                    dve.wait_ge(cs_stored[b % 2], 16 * (NB // 2 * h + b // 2))
                    dve.scalar_tensor_tensor(cs_new[b % 2], cs[b % 2], d_h[:, 8 + b:9 + b],
                                             ps[:, 3 + 2 * (b % 2):5 + 2 * (b % 2), 0:ML1], ALU.mult,
                                             ALU.add).then_inc(cs_ready, 1)
                    dve.wait_ge(cs_ready, NB * h + b + 1)
                    ins = dve.tensor_copy(n_new[:, :, 1 + b:2 + b], cs_new[b % 2][:, :, MLD:MLD + 1])
                    ins.then_inc(n_made, 1) if b == NB - 1 else chain.mark(ins)
                dve.wait_ge(inter_done, NB * h + NB)
                outputs(8, 2)
                dve.wait_ge(n_t, h + 1)
                dve.wait_ge(n_stored, 32 * h)
                dve.tensor_copy(n_nat, ps[0:1 + NB, 7, 0:MLD]).then_inc(n_ev, 1)
                normed(8, 9, TS, 1)
                for k in range(2):
                    dve.wait_ge(hn_hi, 2 * h + k + 1)
                    ins = dve.scalar_tensor_tensor(hn[:, 1, ds(2 * h + k, 1), :], one(flat(3 * k, T)), g_h[:, k:k + 1],
                                                   hn[:, 0, ds(2 * h + k, 1), :], ALU.mult, ALU.subtract)
                ins.then_inc(hn_done, 1)
            chain.leave(HEADS)

        nat = arena[:, 27, :]
        gains_nat, sc_nat, n_rows = nat[0:85, 0:P], nat[0:2 * NB, 128:128 + CH], nat[0:64, 640:768]
        conv_nat = arena[0:2 + 2 * NB, 26, 0:CH]
        conv_t, conv_ev, own_stored = sem("conv_t"), sem("conv_ev"), sem("own_stored")

        block = ctx.enter_context(nc.Block())

        @block.sync
        def _(sp):
            for tt in range(NTT):
                w = P if tt < NTT - 1 else TS
                src = x_p[0, tt * P:tt * P + w, :] if tt < NTT - 1 else x_s.rearrange("b t d -> (b t) d")
                sp.dma_start(arena[0:w, tt, 0:D], src).then_inc(x_loaded[tt], 16)
                if tt == 1:
                    sp.dma_start(gains_nat[0:64, :], norms.rearrange("l n (k p) -> (l n k) p", p=P)).then_inc(
                        gain_loaded, 16)
                    sp.dma_start(gains_nat[64:72, :], mh_g1.rearrange("a (k p) -> (a k) p", p=P)).then_inc(
                        gain_loaded, 16)
                    sp.dma_start(gains_nat[72:73, :], subln_g0).then_inc(gain_loaded, 16)
                    sp.dma_start(gains_nat[73:85, :], conv_w0.rearrange("a w (k p) -> (a w k) p", p=P)).then_inc(
                        gain_loaded, 16)
                    sp.dma_start(sc_nat, state_conv.rearrange("a b t c -> (a b t) c")).then_inc(gain_loaded, 16)
                    sp.dma_start(n_rows, state_n.rearrange("a b h (k p) -> (a b h k) p", p=P)).then_inc(
                        gain_loaded, 16)
            sp.dma_start(lam_rows, lam0.rearrange("a f d -> a (f d)").partition_broadcast(P)).then_inc(lam_loaded, 16)
            sp.dma_start(page_ids[:, :], page_table.rearrange("(a b) n -> a (b n)", a=1)).then_inc(ids_loaded, 16)
            sp.dma_start(b_if[:, :], b_if1.rearrange("a (g h) -> h (a g)", g=2),
                         allow_slow_non_contiguous=True).then_inc(bif_loaded, 16)
            sp.dma_start(m_prev[:, 8:16], state_m.rearrange("a b h -> h (a b)"),
                         allow_slow_non_contiguous=True).then_inc(m0_loaded, 16)
            q_k = lambda i, j: w_cols(w_in0[0], ds(3 * CH + j * CH + i * P, P))
            load_tile(sp, QK, 0, q_k(0, 0), KD, wait=False)
            load_tile(sp, QK + 1, 0, q_k(0, 1), KD, wait=False)
            with sp.Fori(1, HEADS) as i:
                for j in range(2):
                    load_tile(sp, QK + j, i, q_k(i, j), KD)
            with sp.Fori(0, 2) as i:
                for j in range(2):
                    load_tile(sp, V + j, i, w_cols(w_in0[0], ds(5 * CH + (2 * i + j) * P, P)), KD)
            with sp.Fori(0, 2) as i:
                for m in range(6):
                    first = (CH, 2 * CH, 0)[m % 3] + m // 3 * P
                    load_tile(sp, CXB + m, 3 * i, w_cols(w_in0[0], ds(first + 2 * i * P, P)), KD)
            load_tile(sp, WO0, 0, w_cols(w_out0[0], ds(0, P)), KD)
            load_tile(sp, WO0 + 1, 0, w_cols(w_out0[0], ds(P, P)), KD)
            load_pages(sp)
            with sp.Fori(1, 4) as i:
                for j in range(2):
                    load_tile(sp, WO0 + j, i, w_cols(w_out0[0], ds((2 * i + j) * P, P)), KD)
            load_ffn(sp, FF0, 0)
            load_tile(sp, GATES, 0, w_cols(w_in1[0], slice(4 * D, 4 * D + 8)), KD, n=8)
            with sp.Fori(0, HEADS) as h:
                for m in range(8):
                    load_tile(sp, QKVO + m, 4 * h, head_src(h, m), KD)
            with sp.Fori(0, 4) as i:
                for j in range(2):
                    load_tile(sp, WO1 + j, i, w_cols(w_out1[0], ds((2 * i + j) * P, P)), KD)
            load_ffn(sp, FF1, 1)
            for tt in range(NTT):
                w = P if tt < NTT - 1 else TS
                sp.wait_ge(y_ev[tt % 2], tt // 2 + 1)
                dst = y_p[0, tt * P:tt * P + w, :] if tt < NTT - 1 else y_s.rearrange("b t d -> (b t) d")
                sp.dma_start(dst, arena[0:w, tt, 0:D]).then_inc(out_done, 16)
            sp.wait_ge(out_done, 16 * NTT)

        @block.gpsimd
        def _(pool):
            chain = Chain(pool, pool_c)
            for t, v in ((ident, 0.0), (ones, 1.0), (causal, 0.0), (dmask, 0.0), (dmask_s, 0.0), (smask, 0.0),
                         (bmask, 1.0), (sel, 1.0)):
                chain.mark(pool.memset(t[:], v))
            chain.sync()

            def where(t, op, fill, base, pattern, by):
                chain.link(pool.affine_select(out=t, in_=t, compare_op=op, fill=fill, base=base, pattern=pattern,
                                              channel_multiplier=by))
            where(ident[:, :], ALU.not_equal, 1.0, 0, [[-1, P]], 1)
            where(causal[:, :], ALU.is_ge, -BIG, 0, [[-1, P]], 1)
            where(dmask[:, :], ALU.is_ge, BIG, 0, [[1, P]], -1)
            where(dmask_s[:, :], ALU.is_ge, BIG, 0, [[1, TS]], -1)
            s4 = dmask_s[:, :].rearrange("p (b t) -> p b t", b=NB)
            where(s4, ALU.is_ge, BIG, 0, [[-NS, NB], [0, NS]], 1)
            m4 = smask[:, :].rearrange("p (b c t) -> p b c t", b=NB, c=2 * HEADS)
            where(m4, ALU.is_ge, -BIG, 0, [[NS, NB], [0, 2 * HEADS], [1, NS]], -1)
            where(m4, ALU.is_ge, -BIG, 0, [[-NS, NB], [0, 2 * HEADS], [0, NS]], 1)
            where(bmask[:, :], ALU.is_ge, 0.0, 0, [[-NS, NB]], 1)
            where(bmask[:, :], ALU.is_ge, 0.0, NS - 1, [[NS, NB]], -1)
            where(sel[:, :, :], ALU.is_ge, 0.0, 0, [[-1, HEADS], [0, P]], 1)
            where(sel[:, :, :], ALU.is_ge, 0.0, 0, [[1, HEADS], [0, P]], -1)
            pool.memset(conv_in[:, 0:2], 0.0).then_inc(const_ready, 1)
            add_squares(pool, 0)
            pool.wait_ge(mix_ready, HEADS)
            pool.wait_ge(conv_ev, 1)
            pool.dma_start(conv_p[0, 0], conv_nat[0:2, :]).then_inc(conv_saved, 16)
            pool.dma_start(conv_s[0].rearrange("b t c -> (b t) c"), conv_nat[2:2 + 2 * NB, :]).then_inc(conv_saved, 16)
            pool.wait_ge(conv_saved, 32)
            def copy_head(h):
                pool.tensor_copy(one(v_h), vT[:, ds(h, 1), :]).then_inc(cur_ready, 1)
                pool.tensor_copy(one(k_h), kT[:, ds(h, 1), :]).then_inc(cur_ready, 1)
                pool.tensor_copy(one(q_h), qT[:, ds(h, 1), 0:SEQ]).then_inc(cur_ready, 1)

            def store_head(h):
                for ev, src, dst in ((v_ev, v_nat, v_p), (k_ev, k_nat, k_p)):
                    pool.wait_ge(ev, h + 1)
                    alone(pool)
                    pool.dma_start(dst[0, 0].rearrange("(c p) h e -> p c h e", p=P)[:, :, ds(h, 1), :],
                                   src.rearrange("p (c a e) -> p c a e", c=8, a=1)).then_inc(kv_stored, 16)
            copy_head(0)
            with pool.Fori(0, HEADS - 1) as h:
                store_head(h)
                pool.wait_ge(kv_stored, 32 * h + 32)
                pool.wait_ge(s_done, 16 * h + 16)
                copy_head(h + 1)
            store_head(HEADS - 1)
            pool.dma_start(k_s[0].rearrange("b t h e -> (b t) h e"), kv_s_nat[:, 0, :, :]).then_inc(own_stored, 16)
            pool.dma_start(v_s[0].rearrange("b t h e -> (b t) h e"), kv_s_nat[:, 1, :, :]).then_inc(own_stored, 16)
            for n in (1, 2, 3, 4):
                add_squares(pool, n)
            pool.wait_ge(h_ready, 2 * KD)
            pool.dma_start(spill, hT[:, :, :]).then_inc(spilled, 16)
            pool.wait_ge(r_dve, 2)
            pool.dma_start(m_p.rearrange("a b h -> h (a b)"), m_out[:, 0:1],
                           allow_slow_non_contiguous=True).then_inc(m_stored, 16)
            pool.dma_start(m_s.rearrange("a b h -> h (a b)"), m_out[:, 1:1 + NB],
                           allow_slow_non_contiguous=True).then_inc(m_stored, 16)
            pool.wait_ge(rows_ready, 1)
            with pool.Fori(0, HEADS) as h:
                def state_of(a, b):
                    return a[0, b, ds(h, 1), :, :].rearrange("a (k p) e -> p (a k) e", p=P)

                def load(b):
                    pool.wait_ge(cs_ready, NB * h + b - 1) if b >= 2 else pool.wait_ge(cs_ready, NB * h)
                    alone(pool)
                    pool.dma_start(cs[b % 2][:, :, 0:MLD], state_of(state_C, b)).then_inc(cs_loaded[b % 2], 16)
                load(0)
                load(1)
                pool.wait_ge(state_ready, 8 * h + 8)
                alone(pool)
                pool.dma_start(state_of(C_p, 0), state[0][:, :, 0:MLD]).then_inc(state_stored, 16)
                for b in range(NB):
                    pool.wait_ge(cs_ready, NB * h + b + 1)
                    alone(pool)
                    pool.dma_start(state_of(C_s, b), cs_new[b % 2][:, :, 0:MLD]).then_inc(cs_stored[b % 2], 16)
                    if b + 2 < NB:
                        load(b + 2)
                pool.wait_ge(n_ev, h + 1)
                alone(pool)
                pool.dma_start(n_p[0, :, ds(h, 1), :].rearrange("b a d -> b (a d)"), n_nat[0:1, :]).then_inc(n_stored, 16)
                pool.dma_start(n_s[0, :, ds(h, 1), :].rearrange("b a d -> b (a d)"), n_nat[1:1 + NB, :]).then_inc(
                    n_stored, 16)
            pool.wait_ge(hn_done, HEADS)
            pool.wait_ge(n_stored, 32 * HEADS)
            for b in range(2):
                pool.wait_ge(cs_stored[b], 16 * HEADS * NB // 2)
            pool.dma_start(hT[:, :, :], spill).then_inc(restored, 16)
            for n in (5, 6, 7):
                add_squares(pool, n)
            pool.wait_ge(kv_stored, 32 * HEADS)
            pool.wait_ge(own_stored, 32)
            pool.wait_ge(conv_saved, 32)
            pool.wait_ge(m_stored, 32)
            pool.wait_ge(state_stored, 16 * HEADS)

        @block.scalar
        def _(act):
            chain = Chain(act, act_c)
            act.wait_ge(lam_ready, 1)
            act.activation(lam_e, lam_e, ACT.Exp).then_inc(misc_ev, 1)
            split_hi(act, QK, 0, KD, first=True)
            for tt in range(0, NTT, 2):
                w = P if tt < NTT - 1 else TS
                act.wait_ge(x_t, tt + 1)
                act.activation(hT[:, :, tt * P:tt * P + w],
                               flat(2 * (tt % 3), 1024).rearrange("p (k t) -> p k t", t=P)[:, :, 0:w],
                               ACT.Copy).then_inc(x_ev[0], 1)
            act.wait_ge(x_ev[0], 5)
            act.wait_ge(x_ev[1], 4)
            act_before(act, 0, 0, 0)
            act_proj0(act, chain)
            act_heads(act)
            act_samples(act)
            act_project(act, WO0, 1, KD)
            act_roots(act, norm_q(1), NTT)
            act_before(act, 2, 0, 1)
            act_ffn(act, FF0, 0, 3, True)
            act_roots(act, norm_q(3), NTT)
            act_before(act, 4, KD, 2)
            act_gates(act, chain)
            act_mlstm(act, chain)
            act_project(act, WO1, 5, KD)
            act_roots(act, norm_q(5), NTT)
            act_before(act, 6, 2 * KD, 3)
            act_ffn(act, FF1, 1, 7, False)
            act_roots(act, norm_q(7), NTT)
            for tt in range(0, NTT, 2):
                w = P if tt < NTT - 1 else TS
                act.wait_ge(y_t, tt + 1)
                act.activation(arena[0:w, tt, 0:D], flat(2 * (tt % 3), 1024)[0:w, :], ACT.Copy).then_inc(y_ev[0], 1)

        @block.vector
        def _(dve):
            chain = Chain(dve, dve_c)
            chain.link(dve.memset(roots[:, :, :], 1.0))
            dve.wait_ge(lam_loaded, 16)
            l4 = lam_rows.rearrange("p (f d) -> p f d", f=4)
            chain.link(dve.tensor_tensor(lam_prod.rearrange("p (f d) -> p f d", f=2), l4[:, 0:4:2, :], l4[:, 1:4:2, :],
                                         ALU.mult))
            dve.tensor_reduce(lam_e, lam_prod.rearrange("p (f d) -> p f d", f=2), AX.X, ALU.add).then_inc(lam_ready, 1)
            dve.wait_ge(misc_t, 1)
            t = ps[:, 7, :]
            dve.tensor_scalar(gains[:, 0:64], t[:, 0:64], math.sqrt(D), None, ALU.mult)
            dve.tensor_scalar(gains[:, GM:GM + 8], t[:, 64:72], math.sqrt(MLD), None, ALU.mult)
            dve.tensor_scalar(gains[:, GS:GS + 1], t[:, 72:73], math.sqrt(P) * (1 - LAM_INIT), None, ALU.mult)
            dve.tensor_copy(gains[:, GC:GC + 12], t[:, 73:85])
            dve.tensor_copy(nT[:, :, :, :].rearrange("p b h k -> p (b h k)"), t[:, 128:192])
            chain.link(dve.tensor_copy(stT[:, :, :].rearrange("p k n -> p (k n)"), t[:, 256:320]))
            dve.wait_ge(misc_ev, 1)
            chain.link(dve.scalar_tensor_tensor(neg_lam, lam_e[:, 1:2], -LAM_INIT, lam_e[:, 0:1], ALU.add,
                                                ALU.subtract))
            split_lo(dve, QK, 0, KD)
            for tt in range(1, NTT, 2):
                dve.wait_ge(x_t, tt + 1)
                dve.tensor_copy(hT[:, :, tt * P:(tt + 1) * P],
                                flat(2 * (tt % 3), 1024).rearrange("p (k t) -> p k t", t=P)).then_inc(x_ev[1], 1)
            dve_before(dve, chain, 0, 0, 0, 0)
            dve.wait_ge(const_ready, 1)
            dve_proj0(dve, chain)
            dve.wait_ge(conv_t, 1)
            dve.tensor_copy(conv_nat[:, :], ps[0:2 + 2 * NB, 7, :]).then_inc(conv_ev, 1)
            dve_heads(dve, chain)
            dve_samples(dve, chain)
            dve_splits(dve, WO0, 8, KD)
            dve_after(dve, chain, 1, 0, 1, 0)
            dve_before(dve, chain, 2, 0, 2, 1)
            dve_ffn(dve, FF0, 0, True)
            dve_after(dve, chain, 3, 0, 3, 1)
            dve_before(dve, chain, 4, 1, 0, 2)
            dve_gates(dve, chain)
            dve_mlstm(dve, chain)
            dve_splits(dve, WO1, 8, KD)
            dve.wait_ge(restored, 16)
            dve_after(dve, chain, 5, 1, 1, 2)
            dve_before(dve, chain, 6, 1, 2, 3)
            dve_ffn(dve, FF1, 1, False)
            dve_after(dve, chain, 7, 1, 3, 3)
            for tt in range(1, NTT, 2):
                dve.wait_ge(y_t, tt + 1)
                dve.tensor_copy(arena[:, tt, 0:D], flat(2 * (tt % 3), 1024)).then_inc(y_ev[1], 1)

        @block.tensor
        def _(pe):
            pe.wait_ge(const_ready, 1)
            pe.wait_ge(gain_loaded, 96)
            pe.transpose(ps[:, 7, 0:85], gains_nat, ident[0:85, 0:85])
            pe.transpose(ps[:, 7, 128:192], n_rows, ident[0:64, 0:64])
            for k in range(HC):
                ins = pe.transpose(ps[:, 7, 256 + 2 * NB * k:256 + 2 * NB * (k + 1)], sc_nat[:, k * P:(k + 1) * P],
                                   ident[0:2 * NB, 0:2 * NB])
            ins.then_inc(misc_t, 1)
            for tt in range(NTT):
                w = P if tt < NTT - 1 else TS
                pe.wait_ge(x_loaded[tt], 16)
                if tt >= 3:
                    pe.wait_ge(x_ev[(tt - 3) % 2], (tt - 3) // 2 + 1)
                for k in range(KD):
                    ins = pe.transpose(flat(2 * (tt % 3), 1024)[:, k * P:k * P + w],
                                       arena[0:w, tt, k * P:(k + 1) * P], ident[0:w, 0:w])
                ins.then_inc(x_t, 1)
            pe_norm(pe, 0, 3)
            pe.wait_ge(u_ready, KD)
            over_pairs(pe, 8, lambda i, j, last: products(pe, QK + j, i, u, KD))
            over_pairs(pe, 4, lambda i, j, last: products(pe, V + j, i, u, KD))
            with pe.Fori(0, 2) as i:
                for m in range(6):
                    products(pe, CXB + m, 3 * i, u, KD)
            pe.wait_ge(evac[0], WO0 // 2)
            pe.wait_ge(evac[1], WO0 // 2)
            pe.wait_ge(mix_ready, HEADS)
            for k in range(HC):
                ins = pe.transpose(ps[0:2 + 2 * NB, 7, k * P:(k + 1) * P], conv_new[:, k, :], ident[:, :])
            ins.then_inc(conv_t, 1)
            pe.wait_ge(conv_ev, 1)
            pe_heads(pe)
            pe_samples(pe)
            pe.wait_ge(mix_ready, HEADS + 1)
            over_pairs(pe, 8, lambda i, j, last: products(pe, WO0 + j, i, mix, KD))
            pe_norm(pe, 1, 0)
            pe_norm(pe, 2, 3)
            pe_ffn(pe, FF0, 0, 1)
            pe_norm(pe, 3, 0)
            pe_norm(pe, 4, 3)
            pe_gates(pe)
            pe_mlstm(pe)
            pe.wait_ge(hn_done, HEADS)
            over_pairs(pe, 8, lambda i, j, last: products(pe, WO1 + j, i, hn, KD))
            pe_norm(pe, 5, 0)
            pe_norm(pe, 6, 3)
            pe_ffn(pe, FF1, 1, 3)
            pe_norm(pe, 7, 0)
            pe.wait_ge(h_ready, 4 * KD)
            for tt in range(NTT):
                w = P if tt < NTT - 1 else TS
                if tt >= 3:
                    pe.wait_ge(y_ev[(tt - 3) % 2], (tt - 3) // 2 + 1)
                for k in range(KD):
                    ins = pe.transpose(flat(2 * (tt % 3), 1024)[0:w, k * P:(k + 1) * P], hT[:, k, tt * P:tt * P + w],
                                       ident[:, :])
                ins.then_inc(y_t, 1)


INS = ["x_prompt", "x_sample", "cache_k", "cache_v", "state_conv", "state_C", "state_n", "state_m", "page_table",
       "norms", "w_in0", "conv_w0", "lam0", "subln_g0", "w_out0", "w_in1", "b_if1", "mh_g1", "w_out1", "w_gu", "w_down"]
OUTS = [(1, SEQ, D), (NB, NS, D), (1, 1, SEQ, HEADS, P), (1, 1, SEQ, HEADS, P), (1, 1, 2, CH),
        (1, 1, HEADS, MLD, MLD), (1, 1, HEADS, MLD), (1, 1, HEADS), (1, NB, NS, HEADS, P), (1, NB, NS, HEADS, P),
        (1, NB, 2, CH), (1, NB, HEADS, MLD, MLD), (1, NB, HEADS, MLD), (1, NB, HEADS)]


def kernel(**inputs):
    import numpy as np
    import concourse.bacc as bacc
    from concourse.bass_utils import run_bass_kernel_spmd

    nc = bacc.Bacc("TRN2", target_bir_lowering=False, num_devices=1,
                   dynamic_dma_scratch_size=4096)
    arrays, args = {}, []
    for name in INS:
        a = np.ascontiguousarray(inputs[name])
        arrays[f"in_{name}"] = a
        args.append(nc.dram_tensor(f"in_{name}", a.shape, mybir.dt.from_np(a.dtype), kind="ExternalInput").ap())
    for i, shape in enumerate(OUTS):
        args.append(nc.dram_tensor(f"out_{i}", shape, F32, kind="ExternalOutput").ap())
    build(nc, *args)
    r = run_bass_kernel_spmd(nc, [arrays], core_ids=[0])
    return tuple(r.results[0][f"out_{i}"] for i in range(len(OUTS)))
```

```python
import math
from contextlib import ExitStack

import concourse.bass as bass
from concourse import mybir

F32 = mybir.dt.float32
F16 = mybir.dt.float16
I32 = mybir.dt.int32
ALU = mybir.AluOpType
ACT = mybir.ActivationFunctionType
AX = mybir.AxisListType
ds = bass.ds

P = 128
D = 1024
KD = D // P
SEQ = 1024
NB, NS = 8, 4
TS = NB * NS
T = SEQ + TS
GW = T // 3
NTT = SEQ // P + 1
CH = D // 2
HEADS = 4
HC = CH // P
PAGE = 128
NPG = 16
DFF = 2816
KF = 11
WS = 64.0
EPS = 1e-6
LAM_INIT = 0.8 - 0.6 * math.exp(0.0)
BIG = 1e30
MLD = 256
SCALE_DA = 64 ** -0.5
RING = 8


class Chain:

    def __init__(self, eng, sem):
        self.eng, self.sem, self.base, self.n = eng, sem, 0, 0

    def link(self, ins):
        self.mark(ins)
        self.sync()

    def mark(self, ins):
        self.n += 1
        ins.then_inc(self.sem, 1)

    def sync(self):
        self.eng.wait_ge(self.sem, self.base + self.n)

    def enter(self, i, per):
        self.start, self.per = self.base + self.n, per
        self.base, self.n = i * per + self.start, 0

    def leave(self, times):
        assert self.n == self.per, (self.sem, "marks in the body:", self.n, "declared:", self.per)
        self.base, self.n = self.start + self.per * times, 0


def build(nc, x_p, x_s, cache_k, cache_v, state_conv, state_C, state_n, state_m, page_table, norms, w_in0,
          conv_w0, lam0, subln_g0, w_out0, w_in1, b_if1, mh_g1, w_out1, w_gu, w_down, y_p, y_s, k_p, v_p,
          conv_p, C_p, n_p, m_p, k_s, v_s, conv_s, C_s, n_s, m_s):
    ctx = ExitStack()
    with ctx:
        def sb(name, shape, dt=F32):
            return ctx.enter_context(nc.sbuf_tensor(name, shape, dt))

        def sem(name):
            return ctx.enter_context(nc.semaphore(name))

        hT = sb("hT", [P, KD, T])
        u = sb("u", [P, 2, KD, T], F16)
        w_raw = sb("w_raw", [P, 2, KF * P])
        w_split = sb("w_split", [P, 2, 2, KF * P], F16)
        arena = sb("arena", [P, 28, T])
        ident = sb("ident", [P, P])
        ones = sb("ones", [P, P])
        gains = sb("gains", [P, 88])
        causal = sb("causal", [P, P])
        dmask = sb("dmask", [P, P])
        dmask_s = sb("dmask_s", [TS, TS])
        smask = sb("smask", [TS, NB * 2 * HEADS * NS])
        bmask = sb("bmask", [TS, NB])
        sel = sb("sel", [HEADS, HEADS, P])
        small = sb("small", [P, 400])
        roots = sb("roots", [P, 4, NTT])
        eps_col = sb("eps_col", [P, 1])
        ps = ctx.enter_context(nc.psum_tensor("ps", [P, 8, 512], F32))

        GN = lambda layer, which: (layer * 4 + which) * KD
        GM, GS, GC = 64, 72, 73

        def rows(a, n):
            return arena[:, a:a + n, :]

        def half(region, tiles):
            return region.rearrange("p a t -> p (a t)").bitcast(F16).rearrange(
                "p (l k t) -> p l k t", l=2, k=tiles)

        def group(bank):
            return ps[:, bank:bank + 3, 0:GW]

        def flat(bank, n):
            return ps[:, bank:bank + -(-n // 512), :].rearrange("p b w -> p (b w)")[:, 0:n]

        def alone(eng):
            eng.sem_inc(passed[eng.engine], 1)

        def by3(row):
            return row.rearrange("p (g t) -> p g t", g=3)

        mix = half(rows(0, 8), KD)
        hid = half(rows(0, KF), KF)
        ybuf = rows(11, 8)
        tmp = [arena[:, 19 + i, :] for i in range(4)]
        hidf = arena[:, 21, :]
        gate = arena[:, 22, :]
        sq = [arena[:, 23, :], arena[:, 24, :]]
        ssq = arena[:, 25, :]
        diag_row = arena[:, 26, :]
        rs_table = ssq

        w_loaded = [sem("w_loaded0"), sem("w_loaded1")]
        w_hi = sem("w_hi")
        w_ready = sem("w_ready")
        mm_done = sem("mm_done")
        evac = [sem("evac0"), sem("evac1")]
        passed = {e.engine: sem(f"passed{i}") for i, e in enumerate((nc.sync, nc.scalar, nc.gpsimd, nc.tensor))}
        const_ready = sem("const_ready")
        gain_loaded = sem("gain_loaded")
        x_loaded = [sem(f"x_loaded{i}") for i in range(NTT)]
        x_t = sem("x_t")
        x_ev = [sem("x_ev0"), sem("x_ev1")]
        sq_ready = sem("sq_ready")
        ssq_added = sem("ssq_added")
        sq_summed = sem("sq_summed")
        rs_out, rs_made = sem("rs_out"), sem("rs_made")
        root_sum = sem("root_sum")
        root_in, root_out = sem("root_in"), sem("root_out")
        root_diag = sem("root_diag")
        root_done = sem("root_done")
        h_ready, h_pool = sem("h_ready"), sem("h_pool")
        hy_ready = sem("hy_ready")
        t_ready = sem("t_ready")
        u_hi = sem("u_hi")
        u_lo = {"dve": sem("u_lo_dve"), "pool": sem("u_lo_pool")}
        hid_hi = sem("hid_hi")
        hid_ready = sem("hid_ready")
        y_t = sem("y_t")
        y_ev = sem("y_ev")
        out_done = sem("out_done")
        act_c, dve_c, pool_c = sem("act_c"), sem("dve_c"), sem("pool_c")
        outs = [0]

        def over_pairs(eng, n, body, chain=None, per=0):
            if n > 2:
                with eng.Fori(0, n // 2 - 1) as i:
                    if chain:
                        chain.enter(i, per)
                    body(i, 0, False)
                    body(i, 1, False)
                if chain:
                    chain.leave(n // 2 - 1)
            body(n // 2 - 1, 0, False)
            body(n // 2 - 1, 1, True)

        def load_tile(sp, c, r, src, kt, n=P, wait=True):
            s = c % 2
            if wait:
                sp.wait_ge(w_ready, c - 1 + 2 * r)
            alone(sp)
            sp.dma_start(w_raw[:, s, 0:kt * n].rearrange("p (k n) -> p k n", k=kt), src).then_inc(w_loaded[s], 16)

        def split_hi(act, c, r, kt, n=P, first=False):
            s = c % 2
            act.wait_ge(w_loaded[s], 16 * (c // 2 + 1) + 16 * r)
            if not first:
                act.wait_ge(mm_done, c - 1 + 2 * r)
            act.activation(w_split[:, s, 0, 0:kt * n], w_raw[:, s, 0:kt * n], ACT.Copy, scale=WS).then_inc(w_hi, 1)

        def split_lo(dve, c, r, kt, n=P):
            s = c % 2
            dve.wait_ge(w_hi, c + 1 + 2 * r)
            dve.scalar_tensor_tensor(w_split[:, s, 1, 0:kt * n], w_raw[:, s, 0:kt * n], WS,
                                     w_split[:, s, 0, 0:kt * n], ALU.mult, ALU.subtract).then_inc(w_ready, 1)

        def products(pe, c, r, x, kt, m=P, n=P, col=0, bank=None, signal=True, made=None):
            s = c % 2
            pe.wait_ge(w_ready, c + 1 + 2 * r)
            pe.wait_ge(evac[s], c // 2 + r)
            b = 3 * s if bank is None else bank
            for k in range(kt):
                if made:
                    made(k)
                for q, (wp, xp) in enumerate(((0, 0), (0, 1), (1, 0))):
                    for g in range(3):
                        ins = pe.matmul(ps[0:m, b + g, 0:GW], w_split[:, s, wp, k * n + col:k * n + col + m],
                                        x[:, xp, k, g * GW:(g + 1) * GW],
                                        start=(k == 0 and q == 0), stop=(k == kt - 1 and q == 2))
            if signal:
                ins.then_inc(mm_done, 1)

        QK, V, CXB, WO0 = 0, 8, 12, 24
        FF0 = 32
        GATES, QKVO, WO1 = FF0 + 60, FF0 + 61, FF0 + 93
        FF1 = WO1 + 8
        END = FF1 + 60

        def at(c, r):
            return c + 1 + 2 * r

        def out_of_banks(c, r):
            return c // 2 + 1 + r

        def w_cols(w, col):
            return w.rearrange("(k p) n -> p k n", p=P)[:, :, col]

        def one(ap):
            return ap.rearrange("p (a t) -> p a t", a=1)

        def add_squares(pool, n):
            if n % 2 == 0:
                pool.wait_ge(sq_summed, KD * (n // 2))
                pool.sem_inc(ssq_added, KD)
                return
            for k in range(KD):
                pool.wait_ge(sq_ready, KD * n + k + 1)
                if k == 0:
                    if n > 1:
                        pool.wait_ge(rs_made, n // 2)
                    pool.tensor_copy(ssq, sq[k % 2]).then_inc(ssq_added, 1)
                else:
                    pool.wait_ge(ssq_added, KD * n + k)
                    pool.tensor_tensor(ssq, ssq, sq[k % 2], ALU.add).then_inc(ssq_added, 1)

        def square(act, n, k, src):
            if k < 2:
                act.wait_ge(ssq_added, KD * n + k - 1)
            else:
                act.wait_ge(sq_summed, KD * (n // 2 - 1) + k - 1)
            act.activation(sq[k % 2], src, ACT.Square).then_inc(sq_ready, 1)

        def tiles_of(width):
            return [(t, min(P, width - t * P)) for t in range(-(-width // P))]

        def pe_roots(pe, q, d, srcs, diag, width, bank):
            for t, w in tiles_of(width) if srcs else ():
                for k, src in enumerate(srcs):
                    ins = pe.matmul(ps[0:w, 6, t:t + 1], src[:, t * P:t * P + w], ones[:, 0:1], start=(k == 0),
                                    stop=(k == len(srcs) - 1))
            ins.then_inc(root_sum, 1) if srcs else pe.sem_inc(root_sum, 1)
            for t, w in tiles_of(width):
                pe.wait_ge(root_diag, d + t + 1)
                ins = pe.matmul(flat(bank, width)[:, t * P:t * P + w], ones[0:w, :], diag[0:w, t * P:t * P + w],
                                start=True, stop=True)
            ins.then_inc(root_done, 1)

        def act_roots(act, q, n):
            act.wait_ge(root_in, q + 1)
            act.activation(roots[:, 1, 0:n], roots[:, 0, 0:n], ACT.Abs_reciprocal_sqrt).then_inc(root_out, 1)

        def newton(dve, chain, x, y, z):
            chain.link(dve.tensor_tensor(z, x, y, ALU.mult))
            chain.link(dve.tensor_tensor(z, z, y, ALU.mult))
            chain.link(dve.tensor_scalar(z, z, -0.5, 1.5, ALU.mult, ALU.add))
            chain.link(dve.tensor_tensor(z, z, y, ALU.mult))

        def dve_roots(dve, chain, q, d, diag, width, eps):
            ts = tiles_of(width)
            dve.wait_ge(root_sum, q + 1)
            full = sum(w == P for _, w in ts)
            x, y, z = (roots[:, i, 0:len(ts)] for i in range(3))
            sums_ = roots[:, 3, :] if isinstance(q, int) and q == 0 else ps[:, 6, :]
            ins = dve.tensor_scalar(roots[:, 0, 0:full], sums_[:, 0:full], eps, None, ALU.add)
            if full < len(ts):
                w = ts[-1][1]
                ins = dve.tensor_scalar(roots[0:w, 0, full:full + 1], sums_[0:w, full:full + 1], eps, None, ALU.add)
            ins.then_inc(root_in, 1)
            dve.wait_ge(root_in, q + 1)
            dve.wait_ge(root_out, q + 1)
            newton(dve, chain, x, y, z)
            for t, w in ts:
                dve.tensor_scalar(diag[0:w, t * P:t * P + w], ident[0:w, 0:w], z[0:w, t:t + 1], None,
                                  ALU.mult).then_inc(root_diag, 1)
            dve.wait_ge(root_done, q + 1)

        def norm_q(n):
            return HEADS + 2 + n // 2 if n else 0

        HEAD_Q, HEAD_D, SAMPLE_Q, SAMPLE_D = 1, NTT, 1 + HEADS, NTT + 8 * HEADS

        def norm_d(n):
            return SAMPLE_D + 1 + NTT * (n // 2) if n else 0

        def pe_norm(pe, n):
            if n and n % 2 == 0:
                for k in range(KD):
                    pe.wait_ge(sq_ready, KD * n + k + 1)
                    for g in range(3):
                        ins = pe.matmul(ps[:, root_bank(n) + g, 0:GW], ones[:, :], sq[k % 2][:, g * GW:(g + 1) * GW],
                                        start=(k == 0), stop=(k == KD - 1))
                    ins.then_inc(sq_summed, 1)
                return
            if n:
                pe.wait_ge(ssq_added, KD * (n + 1))
            else:
                pe.wait_ge(sq_ready, KD)
            pe_roots(pe, norm_q(n), norm_d(n), [ssq] if n else [], diag_row, T, root_bank(n))

        def root_bank(n):
            return (3 if n % 2 == 0 else 0) if n < 5 else 3 if n == 5 else 0

        POOL_H = (1, 3, 5)

        def h_made(eng, m, k):
            if k in POOL_H:
                eng.wait_ge(h_pool, len(POOL_H) * m + POOL_H.index(k) + 1)
            else:
                others = [j for j in range(KD) if j not in POOL_H]
                eng.wait_ge(h_ready, len(others) * m + others.index(k) + 1)

        def pool_after(pool, m):
            for j, k in enumerate(POOL_H):
                pool.wait_ge(hy_ready, len(POOL_H) * m + j + 1)
                pool.tensor_tensor(hT[:, k, :], hT[:, k, :], tmp[k % 4], ALU.add).then_inc(h_pool, 1)

        def dve_after(dve, chain, n, layer, which):
            m = n // 2
            dve_roots(dve, chain, norm_q(n), norm_d(n), diag_row, T, D * EPS)
            rs = flat(root_bank(n), T)
            col = GN(layer, which)
            for k in range(KD):
                if k >= 4:
                    h_made(dve, m, k - 4)
                ins = dve.scalar_tensor_tensor(tmp[k % 4], ybuf[:, k, :], gains[:, col + k:col + k + 1], rs,
                                               ALU.mult, ALU.mult)
                if k in POOL_H:
                    ins.then_inc(hy_ready, 1)
                    continue
                chain.link(ins)
                dve.scalar_tensor_tensor(hT[:, k, :], tmp[k % 4], 1.0, hT[:, k, :],
                                         ALU.mult, ALU.add).then_inc(h_ready, 1)

        def dve_last(dve, chain):
            dve_roots(dve, chain, norm_q(7), norm_d(7), diag_row, T, D * EPS)
            rs = flat(root_bank(7), T).rearrange("p (a t) -> p a t", a=1)
            for a, b in ((0, 3 * P), (3 * P, 6 * P), (6 * P, T)):
                y = ybuf[:, :, a:b]
                chain.link(dve.tensor_tensor(y, y, rs[:, :, a:b].to_broadcast([P, KD, b - a]), ALU.mult))
                for k in range(KD):
                    g = gains[:, GN(1, 3) + k:GN(1, 3) + k + 1]
                    dve.scalar_tensor_tensor(hT[:, k, a:b], ybuf[:, k, a:b], g, hT[:, k, a:b], ALU.mult,
                                             ALU.add).then_inc(h_ready, 1)

        POOL_LO = (1, 3, 5)

        def lo_part(eng, who, m, k):
            eng.wait_ge(u_hi, KD * m + k + 1)
            eng.tensor_tensor(u[:, 1, k, :], tmp[k % 4], u[:, 0, k, :], ALU.subtract).then_inc(u_lo[who], 1)

        def u_made(eng, m, k):
            if k in POOL_LO:
                eng.wait_ge(u_lo["pool"], len(POOL_LO) * m + POOL_LO.index(k) + 1)
            else:
                others = [j for j in range(KD) if j not in POOL_LO]
                eng.wait_ge(u_lo["dve"], len(others) * m + others.index(k) + 1)

        def pool_lo(pool, m):
            for k in POOL_LO:
                lo_part(pool, "pool", m, k)

        def act_before(act, n, m):
            for k in range(KD if n else 0):
                h_made(act, n // 2 - 1, k)
                square(act, n, k, hT[:, k, :])
            if n:
                act.wait_ge(sq_summed, KD * (n // 2))
                act.activation(by3(rs_table), group(root_bank(n)), ACT.Abs_reciprocal_sqrt,
                               bias=eps_col[:, :]).then_inc(rs_out, 1)
            else:
                act_roots(act, 0, NTT)
            for k in range(KD):
                act.wait_ge(t_ready, KD * m + k + 1)
                act.activation(u[:, 0, k, :], tmp[k % 4], ACT.Copy).then_inc(u_hi, 1)

        def dve_before(dve, chain, n, layer, which, m):
            if n:
                dve.wait_ge(rs_out, n // 2)
                rs, y = diag_row, rs_table
                chain.link(dve.scalar_tensor_tensor(rs, y, 1.0, y, ALU.mult, ALU.mult))
                chain.link(dve.scalar_tensor_tensor(by3(rs), group(root_bank(n)), D * EPS, by3(rs), ALU.add, ALU.mult))
                chain.link(dve.tensor_scalar(rs, rs, -0.5, 1.5, ALU.mult, ALU.add))
                dve.scalar_tensor_tensor(rs, rs, 1.0, y, ALU.mult, ALU.mult).then_inc(rs_made, 1)
                dve.wait_ge(rs_made, n // 2)
            else:
                dve_roots(dve, chain, norm_q(n), norm_d(n), diag_row, T, D * EPS)
                rs = flat(root_bank(n), T)
            col = GN(layer, which)

            def lo(k):
                if k not in POOL_LO:
                    lo_part(dve, "dve", m, k)
            for k in range(KD):
                if k >= 4:
                    u_made(dve, m, k - 4)
                dve.scalar_tensor_tensor(tmp[k % 4], hT[:, k, :], gains[:, col + k:col + k + 1], rs,
                                         ALU.mult, ALU.mult).then_inc(t_ready, 1)
                if k:
                    lo(k - 1)
            lo(KD - 1)

        def act_project(act, c0, stage, kt_next):
            def tile(i, j, last):
                split_hi(act, c0 + j + 1, i, kt_next if last else KD)
                act.wait_ge(mm_done, at(c0 + j, i))
                alone(act)
                yt = ybuf[:, ds(2 * i + j, 1), :] if not isinstance(i, int) else ybuf[:, 2 * i + j:2 * i + j + 1, :]
                yt = yt.rearrange("p a (g t) -> p (a g) t", g=3)
                act.activation(yt, group(3 * ((c0 + j) % 2)), ACT.Copy,
                               scale=1 / WS).then_inc(evac[(c0 + j) % 2], 1)
                act.wait_ge(evac[(c0 + j) % 2], out_of_banks(c0 + j, i))
                act.wait_ge(ssq_added, KD * stage + j - 1 + 2 * i)
                alone(act)
                act.activation(by3(sq[j]), yt, ACT.Square).then_inc(sq_ready, 1)
            over_pairs(act, 8, tile)

        def dve_splits(dve, c0, n, kt_next):
            over_pairs(dve, n, lambda i, j, last: split_lo(dve, c0 + j + 1, i, kt_next if last else KD))

        def load_ffn(sp, c0, layer):
            for half_ in range(2):
                c = c0 + 30 * half_
                r0 = half_ * KF * P
                over_pairs(sp, 22, lambda i, j, last: load_tile(
                    sp, c + j, i, w_cols(w_gu[layer], ds(r0 + j * DFF + i * P, P)), KD))
                over_pairs(sp, 8, lambda i, j, last: load_tile(
                    sp, c + 22 + j, i, w_cols(w_down[layer, r0:r0 + KF * P, :], ds((2 * i + j) * P, P)), KF))

        def pe_ffn(pe, c0, layer, m):
            for half_ in range(2):
                c = c0 + 30 * half_
                over_pairs(pe, 22, lambda i, j, last: products(
                    pe, c + j, i, u, KD, made=(lambda k: u_made(pe, m, k)) if half_ == 0 and j == 0 else None))
                first = 22 * layer + 11 * half_
                over_pairs(pe, 8, lambda i, j, last: products(
                    pe, c + 22 + j, i, hid, KF,
                    made=(lambda k: pe.wait_ge(hid_ready, first + k + 1)) if j == 0 else None))

        def act_ffn(act, c0, layer, stage, more):
            for half_ in range(2):
                c, n0 = c0 + 30 * half_, 22 * layer + 11 * half_
                a, b = c % 2, (c + 1) % 2

                def gate_up(i, j, last):
                    split_hi(act, c + j + 1, i, KF if last else KD)
                    if j == 0:
                        act.wait_ge(mm_done, at(c, i))
                        act.wait_ge(evac[b], (c + 1) // 2 + i)
                        act.activation(by3(gate), group(3 * a), ACT.Silu, scale=1 / WS).then_inc(evac[a], 1)
                    else:
                        act.wait_ge(evac[b], out_of_banks(c + 1, i))
                        alone(act)
                        act.activation(hid[:, 0, ds(i, 1), :], one(hidf), ACT.Copy).then_inc(hid_hi, 1)
                over_pairs(act, 22, gate_up)

                def down(i, j, last):
                    e = c + 22 + j
                    if not last or more or half_ == 0:
                        split_hi(act, e + 1, i, KD if last else KF, n=8 if last and half_ else P)
                    yt = ybuf[:, ds(2 * i + j, 1), :].rearrange("p a (g t) -> p (a g) t", g=3)
                    if half_ == 0:
                        act.wait_ge(mm_done, at(e, i))
                        alone(act)
                        act.activation(yt, group(3 * (e % 2)), ACT.Copy, scale=1 / WS).then_inc(evac[e % 2], 1)
                    else:
                        act.wait_ge(evac[e % 2], out_of_banks(e, i))
                        act.wait_ge(ssq_added, KD * stage + j - 1 + 2 * i)
                        alone(act)
                        act.activation(by3(sq[j]), yt, ACT.Square).then_inc(sq_ready, 1)
                over_pairs(act, 8, down)

        def dve_ffn(dve, c0, layer, more):
            for half_ in range(2):
                c, n0 = c0 + 30 * half_, 22 * layer + 11 * half_
                a, b = c % 2, (c + 1) % 2

                def gate_up(i, j, last):
                    split_lo(dve, c + j + 1, i, KF if last else KD)
                    if j == 0:
                        return
                    dve.wait_ge(mm_done, at(c + 1, i))
                    dve.wait_ge(evac[a], out_of_banks(c, i))
                    dve.wait_ge(hid_hi, n0 + i)
                    dve.wait_ge(hid_ready, n0 + i)
                    dve.scalar_tensor_tensor(by3(hidf), group(3 * b), 1 / WS, by3(gate),
                                             ALU.mult, ALU.mult).then_inc(evac[b], 1)
                    dve.wait_ge(evac[b], out_of_banks(c + 1, i))
                    dve.wait_ge(hid_hi, n0 + i + 1)
                    dve.tensor_tensor(hid[:, 1, ds(i, 1), :], one(hidf), hid[:, 0, ds(i, 1), :],
                                      ALU.subtract).then_inc(hid_ready, 1)
                over_pairs(dve, 22, gate_up)

                def down(i, j, last):
                    e = c + 22 + j
                    if not last or more or half_ == 0:
                        split_lo(dve, e + 1, i, KD if last else KF, n=8 if last and half_ else P)
                    if half_ == 0:
                        return
                    yt = ybuf[:, ds(2 * i + j, 1), :].rearrange("p a (g t) -> p (a g) t", g=3)
                    dve.wait_ge(mm_done, at(e, i))
                    dve.scalar_tensor_tensor(yt, group(3 * (e % 2)), 1 / WS, yt,
                                             ALU.mult, ALU.add).then_inc(evac[e % 2], 1)
                over_pairs(dve, 8, down)

        qT, kT, vT = rows(8, 4), rows(12, 4), rows(16, 4)
        gate_c = arena[:, 20, :]
        conv_in = rows(21, 2).rearrange("p a t -> p (a t)")
        conv_p_in = conv_in[:, 0:SEQ + 2]
        conv_s_in = conv_in[:, SEQ + 2:SEQ + 2 + NB * 6].rearrange("p (b t) -> p b t", b=NB)
        conv_y, y_b = arena[:, 23, :], arena[:, 24, :]
        u_row = u.rearrange("p l k t -> p (l k t)").bitcast(F32).rearrange("p (a t) -> p a t", t=T)
        prob = [u_row[:, i, 0:SEQ] for i in range(4)]
        ring = u_row[:, 4:8, :].rearrange("p a t -> p (a t)")[:, 0:RING * CH].rearrange("p (r c) -> p r c", r=RING)
        q_h, k_h, v_h = arena[:, 20, 0:SEQ], arena[:, 21, :], arena[:, 22, :]
        v_nat, k_nat, att = arena[:, 23, 0:SEQ], arena[:, 27, 0:SEQ], arena[:, 24, 0:SEQ]
        squares_h, diag_h, normed_h = prob[0], prob[1], prob[2]
        prob_t = [arena[:, 25, 0:SEQ], arena[:, 26, 0:SEQ]]
        kv_s_nat = sb("kv_s_nat", [TS, 2, HEADS, P])
        stT = sb("stT", [P, HC, 2 * NB])
        conv_new = sb("conv_new", [P, HC, 2 + 2 * NB])
        lam_rows = small[:, 0:256]
        lam_prod = small[:, 256:384]
        lam_e = small[:, 384:386]
        neg_lam = small[:, 386:387]
        mx, neg_mx = small[:, 388:390], small[:, 390:394]
        lsum, rl = small[:, 394:398], small[:, 398:400]
        flat2 = lambda a: rows(a, 2).rearrange("p a t -> p (a t)")
        q_cur = [arena[:, 16, 160 * b:160 * (b + 1)] for b in range(2)]
        o_nat = arena[0:TS, 16, 512:1024]
        own_s = [arena[0:TS, 17, 32 * b:32 * (b + 1)] for b in range(2)]
        smask_n = arena[0:TS, 17, 64:320].rearrange("p (b t) -> p b t", b=NB)
        sm_max = [arena[0:TS, 17, 320 + 8 * b:325 + 8 * b] for b in range(2)]
        sm_neg = [arena[0:TS, 17, 336 + b:337 + b] for b in range(2)]
        sm_sum = [arena[0:TS, 17, 340 + 8 * b:345 + 8 * b] for b in range(2)]
        sm_rl = [arena[0:TS, 17, 356 + b:357 + b] for b in range(2)]
        sm_t = arena[:, 17, 384:544]
        k_page_t = [arena[:, 25, 0:CH], arena[:, 25, CH:2 * CH]]
        probs_s = [flat2(20)[0:TS, 0:2 * SEQ + TS], flat2(22)[0:TS, 0:2 * SEQ + TS]]
        probs_t = [arena[:, 26 + b, 0:(NPG + 1) * TS] for b in range(2)]
        att_s = arena[:, 24, 0:P].rearrange("p (h t) -> p h t", h=HEADS)
        page_ids = sb("page_ids", [1, NB * NPG], I32)

        lam_loaded, misc_t, misc_ev = sem("lam_loaded"), sem("misc_t"), sem("misc_ev")
        lam_ready = sem("lam_ready")
        gate_c_used = sem("gate_c_used")
        yb_hi, mix_ready = sem("yb_hi"), sem("mix_ready")
        conv_saved = sem("conv_saved")
        cur_ready = sem("cur_ready")
        vk_t = sem("vk_t")
        v_ev, k_ev = sem("v_ev"), sem("k_ev")
        kv_stored = sem("kv_stored")
        s_done = sem("s_done")
        nm_ready = sem("nm_ready")
        p_ready = sem("p_ready")
        w_comb = sem("w_comb")
        pt_t = sem("pt_t")
        pt_ev = sem("pt_ev")
        pv_done = sem("pv_done")
        pv_ev = sem("pv_ev")
        asq_ready = sem("asq_ready")
        at_ready, mix_hi = sem("at_ready"), sem("mix_hi")
        page_loaded = [sem(f"page_loaded{i}") for i in range(RING)]
        page_used = sem("page_used")
        ids_loaded = sem("ids_loaded")
        kp_ev = [sem("kp_ev0"), sem("kp_ev1")]
        kp_used = sem("kp_used")
        qc_ready = sem("qc_ready")
        misc7_t, misc7_ev = sem("misc7_t"), sem("misc7_ev")
        max_ready = sem("max_ready")
        exps = sem("exps")
        o_done, o_ev = sem("o_done"), sem("o_ev")
        att_ready = sem("att_ready")
        mask_t = sem("mask_t")
        spilled, restored = sem("spilled"), sem("restored")

        def act_proj0(act, chain):
            def qk(i, j, last):
                split_hi(act, QK + j + 1, i, KD)
                if j == 0:
                    act.wait_ge(mm_done, at(QK, i))
                    alone(act)
                    act.activation(qT[:, ds(i, 1), :].rearrange("p a (g t) -> p (a g) t", g=3), group(0), ACT.Copy,
                                   scale=1 / WS).then_inc(evac[0], 1)
            over_pairs(act, 8, qk)

            def v(i, j, last):
                split_hi(act, V + j + 1, i, KD)
                if j == 0:
                    act.wait_ge(mm_done, at(V, i))
                    alone(act)
                    act.activation(vT[:, ds(2 * i, 1), :].rearrange("p a (g t) -> p (a g) t", g=3), group(0),
                                   ACT.Copy, scale=1 / WS).then_inc(evac[0], 1)
            over_pairs(act, 4, v)
            with act.Fori(0, 2) as i:
                for m in range(6):
                    c, r = CXB + m, 3 * i
                    split_hi(act, c + 1, r, KD)
                    if m % 3 == 0:
                        act.wait_ge(mm_done, at(c, r))
                        act.wait_ge(gate_c_used, 2 * i + m // 3)
                        act.activation(by3(gate_c), group(3 * (c % 2)), ACT.Copy,
                                       scale=1 / WS).then_inc(evac[c % 2], 1)
                    if m % 3 == 2:
                        act.wait_ge(evac[c % 2], out_of_banks(c, r))
                        alone(act)
                        act.activation(mix[:, 0, ds(2 * i + m // 3, 1), :], one(y_b), ACT.Copy).then_inc(yb_hi, 1)

        def dve_proj0(dve, chain):
            def qk(i, j, last):
                split_lo(dve, QK + j + 1, i, KD)
                if j:
                    dve.wait_ge(mm_done, at(QK + 1, i))
                    dve.tensor_scalar(kT[:, ds(i, 1), :].rearrange("p a (g t) -> p (a g) t", g=3), group(3), 1 / WS,
                                      None, ALU.mult).then_inc(evac[1], 1)
            over_pairs(dve, 8, qk)

            def v(i, j, last):
                split_lo(dve, V + j + 1, i, KD)
                if j:
                    dve.wait_ge(mm_done, at(V + 1, i))
                    dve.tensor_scalar(vT[:, ds(2 * i + 1, 1), :].rearrange("p a (g t) -> p (a g) t", g=3), group(3),
                                      1 / WS, None, ALU.mult).then_inc(evac[1], 1)
            over_pairs(dve, 4, v)
            per = 2 * 7
            with dve.Fori(0, 2) as i:
                chain.enter(i, per)
                for m in range(6):
                    c, r = CXB + m, 3 * i
                    h = 2 * i + m // 3
                    b = 3 * (c % 2)
                    split_lo(dve, c + 1, r, KD)
                    if m % 3 == 1:
                        chain.mark(dve.tensor_copy(conv_s_in[:, :, 0:2], stT[:, ds(h, 1), :].rearrange(
                            "p a (b t) -> p (a b) t", b=NB)))
                        dve.wait_ge(mm_done, at(c, r))
                        dve.wait_ge(evac[(c - 1) % 2], out_of_banks(c - 1, r))
                        dve.scalar_tensor_tensor(
                            conv_p_in[:, 2:2 + 2 * GW].rearrange("p (g t) -> p g t", g=2), ps[:, b:b + 2, 0:GW],
                            1 / WS, gate_c[:, 0:2 * GW].rearrange("p (g t) -> p g t", g=2), ALU.mult, ALU.mult)
                        chain.mark(dve.scalar_tensor_tensor(
                            conv_p_in[:, 2 + 2 * GW:2 + SEQ], ps[:, b + 2, 0:SEQ - 2 * GW], 1 / WS,
                            gate_c[:, 2 * GW:SEQ], ALU.mult, ALU.mult))
                        dve.scalar_tensor_tensor(
                            conv_s_in[:, :, 2:6], ps[:, b + 2, SEQ - 2 * GW:GW].rearrange("p (b t) -> p b t", b=NB),
                            1 / WS, gate_c[:, SEQ:T].rearrange("p (b t) -> p b t", b=NB),
                            ALU.mult, ALU.mult).then_inc(evac[c % 2], 1)
                        dve.wait_ge(evac[c % 2], out_of_banks(c, r))
                        chain.sync()
                        chain.mark(dve.tensor_copy(conv_new[:, ds(h, 1), 0:2], one(conv_p_in[:, SEQ:SEQ + 2])))
                        chain.mark(dve.tensor_copy(
                            conv_new[:, ds(h, 1), 2:2 + 2 * NB].rearrange("p a (b t) -> p (a b) t", b=NB),
                            conv_s_in[:, :, 4:6]))
                        for k in range(3):
                            w = gains[:, ds(GC + k * HC + h, 1)]
                            yp, ys = conv_y[:, 0:SEQ], conv_y[:, SEQ:T].rearrange("p (b t) -> p b t", b=NB)
                            xp, xs = conv_p_in[:, k:k + SEQ], conv_s_in[:, :, k:k + NS]
                            if k == 0:
                                dve.tensor_scalar(yp, xp, w, None, ALU.mult)
                                chain.link(dve.tensor_scalar(ys, xs, w, None, ALU.mult))
                            elif k == 1:
                                dve.scalar_tensor_tensor(yp, xp, w, yp, ALU.mult, ALU.add)
                                chain.link(dve.scalar_tensor_tensor(ys, xs, w, ys, ALU.mult, ALU.add))
                            else:
                                chain.mark(dve.scalar_tensor_tensor(yp, xp, w, yp, ALU.mult, ALU.add))
                                dve.scalar_tensor_tensor(ys, xs, w, ys, ALU.mult, ALU.add).then_inc(gate_c_used, 1)
                    if m % 3 == 2:
                        dve.wait_ge(mm_done, at(c, r))
                        dve.wait_ge(gate_c_used, 2 * i + m // 3 + 1)
                        chain.sync()
                        dve.wait_ge(yb_hi, 2 * i + m // 3)
                        dve.wait_ge(mix_ready, 2 * i + m // 3)
                        dve.scalar_tensor_tensor(by3(y_b), group(b), 1 / WS, by3(conv_y), ALU.mult,
                                                 ALU.mult).then_inc(evac[c % 2], 1)
                        dve.wait_ge(evac[c % 2], out_of_banks(c, r))
                        dve.wait_ge(yb_hi, 2 * i + m // 3 + 1)
                        dve.tensor_tensor(mix[:, 1, ds(h, 1), :], one(y_b), mix[:, 0, ds(h, 1), :],
                                          ALU.subtract).then_inc(mix_ready, 1)
            chain.leave(2)

        def pe_heads(pe):
            with pe.Fori(0, HEADS) as h:
                def transposes(src, n):
                    for tt in range(NTT):
                        w = P if tt < NTT - 1 else TS
                        ins = pe.transpose(ps[0:w, 4 + tt // 4, (tt % 4) * P:(tt % 4 + 1) * P],
                                           src[:, tt * P:tt * P + w], ident[:, :])
                    ins.then_inc(vk_t, 1)
                pe.wait_ge(cur_ready, 3 * h + 1)
                pe.wait_ge(at_ready, h)
                transposes(v_h, 0)
                pe.wait_ge(cur_ready, 3 * h + 2)
                pe.wait_ge(v_ev, h + 1)
                transposes(k_h, 1)
                pe.wait_ge(cur_ready, 3 * h + 3)

                def scores(n):
                    i, c = n // 2, n % 2
                    if n < 2:
                        pe.wait_ge(p_ready, 16 * h)
                    else:
                        pe.wait_ge(p_ready, 16 * h + n - 1)
                    w = (i + 1) * P
                    for j in range(0, w, 512):
                        ins = pe.matmul(ps[:, 2 * (n % 2) + j // 512, 0:min(512, w - j)],
                                        q_h[64 * c:64 * c + 64, i * P:(i + 1) * P],
                                        k_h[64 * c:64 * c + 64, j:min(j + 512, w)], start=True, stop=True)
                    ins.then_inc(s_done, 1)

                def values(i):
                    pe.wait_ge(pt_ev, 8 * h + i + 1)
                    if i < 2:
                        pe.wait_ge(pv_ev, 8 * h)
                    else:
                        pe.wait_ge(pv_ev, 8 * h + i - 1)
                    for j in range(i + 1):
                        ins = pe.matmul(ps[:, 6 + i % 2, 0:P], v_nat[:, j * P:(j + 1) * P],
                                        prob_t[i % 2][:, j * P:(j + 1) * P], start=(j == 0), stop=(j == i))
                    ins.then_inc(pv_done, 1)
                scores(0)
                scores(1)
                for i in range(8):
                    if i < 7:
                        scores(2 * i + 2)
                        scores(2 * i + 3)
                    if i == 0:
                        pe.wait_ge(k_ev, h + 1)
                    if i == 7:
                        values(6)
                    pe.wait_ge(w_comb, 8 * h + i + 1)
                    pe.wait_ge(pt_ev, 8 * h + i)
                    for j in range(i + 1):
                        ins = pe.transpose(flat(4, 1024)[:, j * P:(j + 1) * P], prob[2 * (i % 2)][:, j * P:(j + 1) * P],
                                           ident[:, :])
                    ins.then_inc(pt_t, 1)
                    if 0 < i < 7:
                        values(i - 1)
                values(7)
                pe.wait_ge(asq_ready, h + 1)
                pe_roots(pe, HEAD_Q + h, HEAD_D + 8 * h, [squares_h], diag_h, SEQ, 4)

        def act_heads(act):
            with act.Fori(0, HEADS) as h:
                act.wait_ge(vk_t, 2 * h + 1)
                act.activation(v_nat, flat(4, 1024), ACT.Copy)
                act.activation(kv_s_nat[:, 1, ds(h, 1), :], ps[0:TS, 6:7, 0:P], ACT.Copy).then_inc(v_ev, 1)

                def exp(n):
                    i, w = n // 2, (n // 2 + 1) * P
                    act.wait_ge(nm_ready, 16 * h + n + 1)
                    if i >= 2:
                        act.wait_ge(pt_t, 8 * h + i - 1)
                    act.activation(prob[n % 4][:, 0:w], flat(2 * (n % 2), 1024)[:, 0:w], ACT.Exp,
                                   bias=neg_mx[:, n % 4:n % 4 + 1], scale=SCALE_DA,
                                   accum_out=lsum[:, n % 4:n % 4 + 1]).then_inc(p_ready, 1)
                exp(0)
                exp(1)

                def out(i):
                    act.wait_ge(pv_done, 8 * h + i + 1)
                    act.activation(att[:, i * P:(i + 1) * P], ps[:, 6 + i % 2, 0:P], ACT.Copy).then_inc(pv_ev, 1)
                for i in range(8):
                    if i < 7:
                        exp(2 * i + 2)
                        exp(2 * i + 3)
                    act.wait_ge(pt_t, 8 * h + i + 1)
                    if i >= 2:
                        act.wait_ge(pv_done, 8 * h + i - 1)
                    act.activation(prob_t[i % 2][:, 0:(i + 1) * P], flat(4, 1024)[:, 0:(i + 1) * P],
                                   ACT.Copy).then_inc(pt_ev, 1)
                    if i:
                        out(i - 1)
                out(7)
                act.wait_ge(pv_ev, 8 * h + 8)
                act.activation(squares_h, att, ACT.Square).then_inc(asq_ready, 1)
                act_roots(act, HEAD_Q + h, 8)
                act.wait_ge(at_ready, h + 1)
                alone(act)
                act.activation(mix[:, 0, ds(HC + h, 1), 0:SEQ], one(normed_h), ACT.Copy,
                               scale=gains[:, GS:GS + 1]).then_inc(mix_hi, 1)

        def dve_heads(dve, chain):
            per = 16 * 2 + 8 * 3 + 4
            with dve.Fori(0, HEADS) as h:
                chain.enter(h, per)

                def maxima(n):
                    i, w = n // 2, (n // 2 + 1) * P
                    s = flat(2 * (n % 2), 1024)
                    dve.wait_ge(s_done, 16 * h + n + 1)
                    chain.link(dve.tensor_tensor(s[:, i * P:w], s[:, i * P:w], causal[:, :], ALU.add))
                    chain.link(dve.tensor_reduce(mx[:, n % 2:n % 2 + 1], s[:, 0:w], AX.X, ALU.max))
                    dve.tensor_scalar(neg_mx[:, n % 4:n % 4 + 1], mx[:, n % 2:n % 2 + 1], -SCALE_DA, None,
                                      ALU.mult).then_inc(nm_ready, 1)
                maxima(0)
                maxima(1)
                dve.wait_ge(vk_t, 2 * h + 2)
                dve.tensor_copy(k_nat, flat(4, 1024))
                dve.tensor_copy(kv_s_nat[:, 0, ds(h, 1), :], ps[0:TS, 6:7, 0:P]).then_inc(k_ev, 1)
                for i in range(8):
                    a, w = 2 * (i % 2), (i + 1) * P
                    dve.wait_ge(p_ready, 16 * h + 2 * i + 2)
                    dve.wait_ge(w_comb, 8 * h + i)
                    chain.link(dve.reciprocal(rl, lsum[:, a:a + 2]))
                    chain.link(dve.tensor_scalar(rl[:, 1:2], rl[:, 1:2], neg_lam, None, ALU.mult))
                    chain.link(dve.tensor_scalar(prob[a + 1][:, 0:w], prob[a + 1][:, 0:w], rl[:, 1:2], None, ALU.mult))
                    dve.scalar_tensor_tensor(prob[a][:, 0:w], prob[a][:, 0:w], rl[:, 0:1], prob[a + 1][:, 0:w],
                                             ALU.mult, ALU.add).then_inc(w_comb, 1)
                    if i < 7:
                        maxima(2 * i + 2)
                        maxima(2 * i + 3)
                dve_roots(dve, chain, HEAD_Q + h, HEAD_D + 8 * h, diag_h, SEQ, P * EPS)
                dve.tensor_tensor(normed_h, att, flat(4, SEQ), ALU.mult).then_inc(at_ready, 1)
                dve.wait_ge(mix_hi, h + 1)
                dve.scalar_tensor_tensor(mix[:, 1, ds(HC + h, 1), 0:SEQ], one(normed_h), gains[:, GS:GS + 1],
                                         mix[:, 0, ds(HC + h, 1), 0:SEQ], ALU.mult,
                                         ALU.subtract)
            chain.leave(HEADS)

        def load_pages(sp):
            sp.wait_ge(ids_loaded, 16)
            sp.wait_ge(mm_done, CXB + 12)
            with sp.Fori(0, NB // 2) as i:
                for f in range(4 * NPG):
                    b, cache = (f // NPG) % 2, cache_k if f < 2 * NPG else cache_v
                    n = (2 * i + b) * NPG + f % NPG
                    page = sp.value_load(page_ids[0:1, ds(n, 1)], min_val=0, max_val=cache_k.shape[1] - 1)
                    if f >= RING:
                        sp.wait_ge(page_used, 4 * NPG * i + f - RING + 1)
                    else:
                        sp.wait_ge(page_used, 4 * NPG * i)
                    alone(sp)
                    sp.dma_start(ring[:, f % RING, :],
                                 cache[0, ds(page, 1), :, :, :].rearrange("a t h e -> (a t) (h e)")
                                 ).then_inc(page_loaded[f % RING], 16)

        PT_A, PT_B = 8, NPG + 1 - 8

        def pe_samples(pe):
            pe.wait_ge(kv_stored, 32 * HEADS)
            for b in range(NB):
                ins = pe.transpose(ps[0:TS, 7, 32 * b:32 * b + 32], smask[:, 32 * b:32 * b + 32], ident[0:TS, 0:TS])
            ins.then_inc(mask_t, 1)
            with pe.Fori(0, NB // 2) as i:
                def page_ready(f):
                    pe.wait_ge(page_loaded[f % RING], 16 * (4 * NPG // RING * i + f // RING + 1))

                def bank7(n):
                    pe.wait_ge(misc7_ev, 8 * i + n + 1)

                def own(b):
                    pe.wait_ge(qc_ready, 2 * i + b + 1)
                    bank7(b)
                    for h in range(HEADS):
                        ins = pe.matmul(ps[0:TS, 7, 0:TS], q_cur[b][:, 32 * h:32 * h + 32], kT[:, h, SEQ:T],
                                        start=(h == 0), stop=(h == HEADS - 1))
                    ins.then_inc(misc7_t, 1)

                def key_page(f):
                    page_ready(f)
                    pe.wait_ge(kp_ev[f % 2], NPG * i + f // 2)
                    for h in range(HEADS):
                        ins = pe.transpose(ps[:, f % 2, h * P:(h + 1) * P], ring[:, f % RING, h * P:(h + 1) * P],
                                           ident[:, :])
                    ins.then_inc(page_used, 1)

                def key_scores(f):
                    pe.wait_ge(kp_ev[f % 2], NPG * i + f // 2 + 1)
                    b, p = f // NPG, f % NPG
                    if p % 4 == 0:
                        if b:
                            pe.wait_ge(exps, 10 * i + (1, 3, 4, 5)[p // 4])
                        else:
                            pe.wait_ge(exps, 10 * i)
                    for h in range(HEADS):
                        ins = pe.matmul(ps[0:TS, 2 + p // 4, (p % 4) * P:(p % 4 + 1) * P],
                                        q_cur[b][:, 32 * h:32 * h + 32], k_page_t[f % 2][:, h * P:(h + 1) * P],
                                        start=(h == 0), stop=(h == HEADS - 1))
                    ins.then_inc(kp_used, 1)

                def weights_t(b, half_):
                    pe.wait_ge(exps, 10 * i + 5 * b + (5 if half_ else 3))
                    bank7(2 + 2 * b + half_)
                    alone(pe)
                    for q in range(PT_B if half_ else PT_A):
                        p = q + PT_A * half_
                        w = P if p < NPG else TS
                        ins = pe.transpose(ps[0:w, 7, q * TS:(q + 1) * TS], probs_s[b][:, p * P:p * P + w],
                                           ident[0:TS, 0:TS])
                    ins.then_inc(misc7_t, 1)

                def outputs_t(b):
                    bank7(6 + b)
                    pe.wait_ge(o_ev, 2 * i + b + 1)
                    alone(pe)
                    for h in range(HEADS):
                        ins = pe.transpose(ps[:, 7, 32 * h:32 * h + 32], o_nat[:, h * P:(h + 1) * P],
                                           ident[0:TS, 0:TS])
                    ins.then_inc(misc7_t, 1)

                def values(b, between):
                    pe.wait_ge(misc7_ev, 8 * i + 5 + 2 * b)
                    pe.wait_ge(o_ev, 2 * i + b)
                    for p in range(NPG):
                        f = (2 + b) * NPG + p
                        page_ready(f)
                        pe.matmul(ps[0:TS, 6, :], probs_t[b][:, p * TS:(p + 1) * TS], ring[:, f % RING, :],
                                  start=(p == 0), stop=False).then_inc(page_used, 1)
                        if p in between:
                            between[p]()
                    pe.matmul(ps[0:TS, 6, :], probs_t[b][0:TS, NPG * TS:(NPG + 1) * TS],
                              kv_s_nat[:, 1, :, :].rearrange("p h e -> p (h e)"), start=False,
                              stop=True).then_inc(o_done, 1)

                for b in range(2):
                    own(b)
                    for p in range(NPG):
                        f = b * NPG + p
                        key_page(f)
                        if p:
                            key_scores(f - 1)
                        if b and p == 7:
                            weights_t(0, 0)
                        if b and p == 9:
                            weights_t(0, 1)
                    key_scores(b * NPG + NPG - 1)
                values(0, {6: lambda: weights_t(1, 0), 8: lambda: weights_t(1, 1)})
                values(1, {3: lambda: outputs_t(0)})
                outputs_t(1)
            pe.wait_ge(asq_ready, HEADS + 1)
            pe_roots(pe, SAMPLE_Q, SAMPLE_D, [arena[:, 26, 0:P]], arena[:, 26, P:2 * P], P, 4)

        def evac_page(eng, i, f):
            eng.wait_ge(kp_used, 2 * NPG * i + f - 1) if f >= 2 else eng.wait_ge(kp_used, 2 * NPG * i)
            eng.wait_ge(page_used, 4 * NPG * i + f + 1)

        def act_samples(act):
            with act.Fori(0, NB // 2) as i:
                def exp(b, j):
                    if j == 0:
                        act.wait_ge(max_ready, 2 * i + b + 1)
                    act.activation(probs_s[b][:, 512 * j:512 * (j + 1)], ps[0:TS, 2 + j, :], ACT.Exp,
                                   scale=SCALE_DA, bias=sm_neg[b], accum_out=sm_sum[b][:, j:j + 1]).then_inc(exps, 1)
                    if j == 0:
                        act.activation(probs_s[b][:, 2 * SEQ:2 * SEQ + TS], own_s[b], ACT.Exp, scale=SCALE_DA,
                                       bias=sm_neg[b], accum_out=sm_sum[b][:, 4:5]).then_inc(exps, 1)
                for f in range(0, 2 * NPG, 2):
                    evac_page(act, i, f)
                    act.activation(k_page_t[0], ps[:, 0, :], ACT.Copy).then_inc(kp_ev[0], 1)
                    if 0 <= f - NPG < 8:
                        exp(0, (f - NPG) // 2)
                for j in range(4):
                    exp(1, j)
            act.wait_ge(att_ready, NB)
            act.activation(arena[:, 26, 0:P], arena[:, 24, 0:P], ACT.Square).then_inc(asq_ready, 1)
            act_roots(act, SAMPLE_Q, 1)
            act.wait_ge(at_ready, HEADS + 1)
            act.activation(mix[:, 0, HC:KD, SEQ:T], arena[:, 27, 0:P].rearrange("p (h t) -> p h t", h=HEADS), ACT.Copy,
                           scale=gains[:, GS:GS + 1]).then_inc(mix_hi, 1)

        def dve_samples(dve, chain):
            dve.wait_ge(kv_stored, 32 * HEADS)
            for b in range(2):
                chain.mark(dve.memset(q_cur[b], 0.0))
            dve.wait_ge(mask_t, 1)
            dve.tensor_copy(smask_n.rearrange("p b t -> p (b t)"), ps[0:TS, 7, 0:256]).then_inc(misc7_ev, 1)
            chain.sync()
            dve.wait_ge(misc7_ev, 1)
            per = 2 * 4
            with dve.Fori(0, NB // 2) as i:
                chain.enter(i, per)

                def bank7_done(n):
                    dve.wait_ge(misc7_t, 8 * i + n + 1)

                def bank_max(b, j):
                    dve.wait_ge(kp_used, 2 * NPG * i + NPG * b + 4 * j + 4)
                    ins = dve.tensor_reduce(sm_max[b][:, j:j + 1], ps[0:TS, 2 + j, :], AX.X, ALU.max)
                    if j == 3:
                        chain.link(ins)
                        chain.link(dve.tensor_reduce(sm_max[b][:, 0:1], sm_max[b], AX.X, ALU.max))
                        dve.tensor_scalar(sm_neg[b], sm_max[b][:, 0:1], -SCALE_DA, None, ALU.mult).then_inc(
                            max_ready, 1)

                def weights_t(b, half_):
                    bank7_done(2 + 2 * b + half_)
                    if half_ == 0:
                        dve.tensor_copy(probs_t[b][:, 0:PT_A * TS], ps[:, 7, 0:PT_A * TS]).then_inc(misc7_ev, 1)
                    else:
                        n = (PT_B - 1) * TS
                        dve.tensor_copy(probs_t[b][:, PT_A * TS:NPG * TS], ps[:, 7, 0:n])
                        dve.tensor_copy(probs_t[b][0:TS, NPG * TS:(NPG + 1) * TS], ps[0:TS, 7, n:n + TS]).then_inc(
                            misc7_ev, 1)

                def out(b):
                    dve.wait_ge(exps, 10 * i + 5 * (b + 1))
                    chain.link(dve.tensor_reduce(sm_rl[b], sm_sum[b], AX.X, ALU.add))
                    chain.link(dve.reciprocal(sm_rl[b], sm_rl[b]))
                    dve.wait_ge(o_done, 2 * i + b + 1)
                    if b:
                        bank7_done(6)
                    else:
                        dve.wait_ge(misc7_t, 8 * i)
                    dve.tensor_scalar(o_nat, ps[0:TS, 6, :], sm_rl[b], None, ALU.mult).then_inc(o_ev, 1)

                def out_t(b):
                    bank7_done(6 + b)
                    dve.tensor_copy(sm_t[:, 0:P], ps[:, 7, 0:P]).then_inc(misc7_ev, 1)
                    dve.wait_ge(misc7_ev, 8 * i + 8 + b)
                    o = sm_t.rearrange("p (h n) -> p h n", n=40)
                    dve.scalar_tensor_tensor(att_s[:, :, ds(8 * i + 4 * b, 4)], o[:, :, 4:8], neg_lam,
                                             o[:, :, 0:4], ALU.mult, ALU.add).then_inc(att_ready, 1)

                dve.wait_ge(kp_used, 2 * NPG * i)
                for b in range(2):
                    for c in range(2):
                        ins = dve.tensor_copy(
                            q_cur[b][64 * c:64 * c + 64, :].rearrange("p (h n) -> p h n", n=40)[:, :, 4 * c:4 * c + 4],
                            qT[64 * c:64 * c + 64, :, ds(8 * i + SEQ + 4 * b, NS)])
                    ins.then_inc(qc_ready, 1)
                for b in range(2):
                    bank7_done(b)
                    dve.tensor_tensor(own_s[b].rearrange("p (a t) -> p a t", a=1),
                                      ps[0:TS, 7, 0:TS].rearrange("p (a t) -> p a t", a=1),
                                      smask_n[:, ds(2 * i + b, 1), :], ALU.add).then_inc(misc7_ev, 1)
                    dve.wait_ge(misc7_ev, 8 * i + 2 + b)
                    dve.tensor_reduce(sm_max[b][:, 4:5], own_s[b], AX.X, ALU.max)
                    for p in range(1, NPG, 2):
                        if b and p == 1:
                            bank_max(0, 3)
                        evac_page(dve, i, NPG * b + p)
                        dve.tensor_copy(k_page_t[1], ps[:, 1, :]).then_inc(kp_ev[1], 1)
                        if p % 4 == 1 and p > 1:
                            bank_max(b, p // 4 - 1)
                        if b and p == 7:
                            weights_t(0, 0)
                        if b and p == 9:
                            weights_t(0, 1)
                bank_max(1, 3)
                weights_t(1, 0)
                weights_t(1, 1)
                out(0)
                out_t(0)
                out(1)
                out_t(1)
            chain.leave(NB // 2)
            dve_roots(dve, chain, SAMPLE_Q, SAMPLE_D, arena[:, 26, P:2 * P], P, P * EPS)
            dve.wait_ge(att_ready, NB)
            t = arena[:, 27, 0:P]
            dve.tensor_tensor(t, arena[:, 24, 0:P], flat(4, P), ALU.mult).then_inc(at_ready, 1)
            dve.wait_ge(mix_hi, HEADS + 1)
            dve.scalar_tensor_tensor(mix[:, 1, HC:KD, SEQ:T], t.rearrange("p (h t) -> p h t", h=HEADS),
                                     gains[:, GS:GS + 1], mix[:, 0, HC:KD, SEQ:T], ALU.mult,
                                     ALU.subtract).then_inc(mix_ready, 1)

        hn = mix
        q1, k1, v1, o1 = rows(8, 2), rows(10, 2), rows(12, 2), rows(14, 2)
        flat_rows = lambda a, n: rows(a, n).rearrange("p a t -> p (a t)")
        wk = flat_rows(16, 3)[:, 0:NTT * MLD].rearrange("p (c d) -> p c d", c=NTT)
        ML1 = MLD + 2
        vn = flat_rows(19, 3)[:, 0:NTT * ML1].rearrange("p (c e) -> p c e", c=NTT)
        hc = flat_rows(22, 3)[:, 0:NTT * MLD].rearrange("p (c e) -> p c e", c=NTT)
        m_bc, i_bc = arena[:, 25, :], arena[:, 27, :]
        state = [arena[:, 26, 2 * ML1 * i:2 * ML1 * (i + 1)].rearrange("p (k e) -> p k e", k=2) for i in range(2)]
        spare = flat_rows(16, 3)[:, NTT * MLD:]
        den_ = spare[:, 0:1]
        rec_ = [spare[:, 1 + i:2 + i] for i in range(2)]
        sums, neg_mean, sqs = (spare[:, 16 * i:16 * i + NTT] for i in (1, 2, 3))
        junk = spare[:, 64:64 + MLD]
        sd = flat_rows(10, 2)[:, 0:NTT * P]
        dec = flat_rows(12, 2)[:, 0:NTT * P]
        m_row, i_row, e_row = (hT[0:HEADS, k, :] for k in range(3))
        CSL = 4
        cs = [hT[:, 3 + i // 2, 2 * ML1 * (i % 2):2 * ML1 * (i % 2 + 1)].rearrange("p (k e) -> p k e", k=2)
              for i in range(CSL)]
        cs_new = [hT[:, 5, 2 * ML1 * i:2 * ML1 * (i + 1)].rearrange("p (k e) -> p k e", k=2) for i in range(2)]
        q_pad = hT[:, 6, 0:2 * 288].rearrange("p (k n) -> p k n", k=2)
        wk_b = [hT[0:TS, 7, MLD * i:MLD * (i + 1)] for i in range(2)]
        n_nat = hT[0:1 + NB, 7, 640:896]
        r = lambda k: arena[0:HEADS, k, :]
        li, fx, fa, fe, fl, bc, aa, we, mt = (r(16 + k) for k in range(9))
        acol = sb("acol", [P, 3, NTT, HEADS])
        a_h = sb("a_h", [P, 3, NTT])
        sel_h = sb("sel_h", [HEADS, P])
        reset = hT[0:HEADS, 4, :]
        m_prev = sb("m_prev", [HEADS, 16])
        m_last = sb("m_last", [HEADS, 16])
        m_out = sb("m_out", [HEADS, 1 + NB])
        decay = sb("decay", [HEADS, 16])
        d_h = sb("d_h", [P, 16])
        b_if = sb("b_if", [HEADS, 2])
        nT = sb("nT", [P, NB, HEADS, 2])
        n_h = sb("n_h", [P, NB, 2])
        n_new = sb("n_new", [P, 2, 1 + NB])
        g_h = sb("g_h", [P, 2])
        spill = nc.dram_tensor("h_spill", (P, KD, T), F32, kind="Internal").ap()

        bif_loaded, m0_loaded = sem("bif_loaded"), sem("m0_loaded")
        r_act, r_dve = sem("r_act"), sem("r_dve")
        col_t = sem("col_t")
        rows_ready = sem("rows_ready")
        m_stored = sem("m_stored")
        selh_ready = sem("selh_ready")
        bc_t, bc_act, bc_dve = sem("bc_t"), sem("bc_act"), sem("bc_dve")
        kn_t, kn_ev, vn_t, vn_ev = sem("kn_t"), sem("kn_ev"), sem("vn_t"), sem("vn_ev")
        st_done, dx_ready, dec_ready, sd_ready, qi_ready = (sem(n) for n in ("st_done", "dx_ready", "dec_ready",
                                                                             "sd_ready", "qi_ready"))
        up_done, state_ready, num_done = sem("up_done"), sem("state_ready"), sem("num_done")
        cs_loaded, nc_ready, wkb_ready = [sem(f"cs_loaded{i}") for i in range(CSL)], sem("nc_ready"), sem("wkb_ready")
        inter_done = sem("inter_done")
        ups_done, cs_ready, cs_stored = sem("ups_done"), sem("cs_ready"), [sem("cs_stored0"), sem("cs_stored1")]
        state_stored, n_made, n_t = sem("state_stored"), sem("n_made"), sem("n_t")
        n_ev, n_stored = sem("n_ev"), sem("n_stored")
        hc_ready = sem("hc_ready")
        stat_ready = sem("stat_ready")
        mr_in, mr_out = sem("mr_in"), sem("mr_out")
        hs_ready = sem("hs_ready")
        hs_t = sem("hs_t")
        hn_hi, hn_half, hn_done = sem("hn_hi"), sem("hn_half"), sem("hn_done")

        def chunks(row):
            return row[:, 0:SEQ].rearrange("p (c t) -> p c t", t=P)

        def samples(row):
            return row[:, SEQ:T].rearrange("p (b t) -> p b t", b=NB)

        def pe_gates(pe):
            products(pe, GATES, 0, u, KD, m=HEADS, n=8, col=0, bank=0, signal=False,
                     made=lambda k: u_made(pe, 2, k))
            pe.wait_ge(evac[1], GATES // 2)
            products(pe, GATES, 0, u, KD, m=HEADS, n=8, col=HEADS, bank=3)
            pe.wait_ge(evac[0], GATES // 2 + 1)
            pe.wait_ge(rows_ready, 1)
            for k, src in enumerate((aa, we, e_row)):
                for c in range(NTT):
                    w = P if c < NTT - 1 else TS
                    ins = pe.transpose(ps[0:w, 6, (k * NTT + c) * HEADS:(k * NTT + c + 1) * HEADS],
                                       src[:, c * P:c * P + w], ident[0:HEADS, 0:HEADS])
            ins.then_inc(col_t, 1)

        def act_gates(act, chain):
            split_hi(act, QKVO, 0, KD)
            act.wait_ge(mm_done, GATES + 1)
            act.wait_ge(bif_loaded, 16)
            act.activation(by3(li), ps[0:HEADS, 0:3, 0:GW], ACT.Identity, scale=1 / WS, bias=b_if[:, 0:1])
            act.activation(by3(fx), ps[0:HEADS, 3:6, 0:GW], ACT.Identity, scale=1 / WS,
                           bias=b_if[:, 1:2]).then_inc(evac[0], 1)
            act.wait_ge(r_dve, 1)
            chain.link(act.activation(fe, fa, ACT.Exp, scale=-1.0))
            act.activation(fl, fe, ACT.Ln, bias=1.0).then_inc(r_act, 1)
            act.wait_ge(r_dve, 2)
            act.activation(we, we, ACT.Exp)
            act.activation(i_row, i_row, ACT.Exp)
            act.activation(decay[:, :], decay[:, :], ACT.Exp)
            act.activation(e_row, mt, ACT.Exp, scale=-1.0).then_inc(rows_ready, 1)

        def dve_gates(dve, chain):
            split_lo(dve, QKVO, 0, KD)
            dve.wait_ge(spilled, 16)
            chain.link(dve.memset(reset, 1.0))
            dve.memset(chunks(reset)[:, :, 0:1], 0.0)
            chain.mark(dve.memset(samples(reset)[:, :, 0:1], 0.0))
            chain.mark(dve.memset(m_prev[:, 0:1], 0.0))
            chain.mark(dve.memset(acol[:, :, :, :], 0.0))
            chain.mark(dve.memset(hT[:, 6, 0:2 * 288], 0.0))
            dve.wait_ge(evac[0], GATES // 2 + 1)
            dve.scalar_tensor_tensor(fa, fx, -1.0, fx, ALU.mult, ALU.max).then_inc(r_dve, 1)
            chain.link(dve.tensor_scalar(mt, fx, 0.0, None, ALU.min))
            dve.wait_ge(r_act, 1)
            chain.link(dve.tensor_tensor(fl, mt, fl, ALU.subtract))
            chain.link(dve.tensor_tensor_scan(bc, reset, fl, 0.0, ALU.mult, ALU.add))
            chain.link(dve.tensor_tensor(aa, li, bc, ALU.subtract))
            dve.wait_ge(m0_loaded, 16)
            for c in range(8):
                m_c, a_c = m_row[:, c * P:(c + 1) * P], aa[:, c * P:(c + 1) * P]
                chain.link(dve.tensor_tensor_scan(m_c, a_c, a_c, m_prev[:, c:c + 1], ALU.max, ALU.max))
                if c < 7:
                    chain.link(dve.tensor_tensor(m_prev[:, c + 1:c + 2], bc[:, c * P + P - 1:c * P + P],
                                                 m_row[:, c * P + P - 1:c * P + P], ALU.add))
            for t in range(NS):
                before = m_prev[:, 8:16] if t == 0 else samples(m_row)[:, :, t - 1]
                chain.link(dve.tensor_tensor(samples(m_row)[:, :, t], before, samples(aa)[:, :, t], ALU.max))
            chain.mark(dve.tensor_copy(m_last[:, 0:8], chunks(m_row)[:, :, P - 1]))
            chain.link(dve.tensor_copy(m_last[:, 8:16], samples(m_row)[:, :, NS - 1]))
            dve.tensor_tensor(chunks(we), chunks(aa), m_last[:, 0:8].rearrange("p (c a) -> p c a", a=1).to_broadcast(
                [HEADS, 8, P]), ALU.subtract)
            dve.tensor_tensor(samples(we), samples(aa), m_last[:, 8:16].rearrange("p (c a) -> p c a", a=1)
                              .to_broadcast([HEADS, NB, NS]), ALU.subtract)
            dve.tensor_tensor(chunks(i_row), m_prev[:, 0:8].rearrange("p (c a) -> p c a", a=1).to_broadcast(
                [HEADS, 8, P]), chunks(m_row), ALU.subtract)
            dve.tensor_tensor(samples(i_row), m_prev[:, 8:16].rearrange("p (c a) -> p c a", a=1).to_broadcast(
                [HEADS, NB, NS]), samples(m_row), ALU.subtract)
            dve.tensor_tensor(decay[:, :], m_prev[:, :], m_last[:, :], ALU.subtract)
            chain.link(dve.tensor_tensor(mt, bc, m_row, ALU.add))
            dve.tensor_copy(m_out[:, 0:1], mt[:, SEQ - 1:SEQ])
            dve.tensor_copy(m_out[:, 1:1 + NB], samples(mt)[:, :, NS - 1]).then_inc(r_dve, 1)
            dve.wait_ge(col_t, 1)
            dve.tensor_copy(acol[:, :, 0:8, :], ps[:, 6, 0:3 * NTT * HEADS].rearrange(
                "p (k c h) -> p k c h", k=3, c=NTT)[:, :, 0:8, :])
            chain.mark(dve.tensor_copy(acol[0:TS, :, 8:9, :], ps[0:TS, 6, 0:3 * NTT * HEADS].rearrange(
                "p (k c h) -> p k c h", k=3, c=NTT)[:, :, 8:9, :]))
            chain.mark(dve.memset(vn[:, :, MLD:ML1], 1.0))
            chain.sync()

        def head_src(h, m):
            return w_cols(w_in1[0], ds((m // 2) * D + (m % 2) * P + h * MLD, P))

        def act_mlstm(act, chain):
            per = 2 * NTT
            with act.Fori(0, HEADS) as h:
                chain.enter(h, per)

                def tokens(t, out):
                    n, bank = (t, 7) if out is vn else (5 + t, 7 - t % 2)
                    act.wait_ge(vn_t, 10 * h + n + 1)
                    if t < 4:
                        act.activation(out[:, 2 * t:2 * t + 2, 0:MLD],
                                       ps[:, bank, :].rearrange("p (a e) -> p a e", a=2), ACT.Copy).then_inc(vn_ev, 1)
                    else:
                        act.activation(out[0:TS, 8, 0:MLD], ps[0:TS, 7, 0:MLD], ACT.Copy).then_inc(vn_ev, 1)

                def normaliser(b):
                    used = NB * h + (b - CSL + 1 if b >= CSL else 0)
                    act.wait_ge(inter_done, used)
                    act.wait_ge(cs_ready, used)
                    act.activation(cs[b % CSL][:, :, MLD:ML1], n_h[:, b, :].rearrange("p (k a) -> p k a", a=1).to_broadcast(
                        [P, 2, ML1 - MLD]), ACT.Copy).then_inc(nc_ready, 1)

                def statistics(c):
                    w = P if c < NTT - 1 else TS
                    act.wait_ge(hc_ready, NTT * h + c + 1)
                    chain.link(act.activation(junk[0:w, :], hc[0:w, c, :], ACT.Copy, accum_out=sums[0:w, c:c + 1]))
                    chain.link(act.activation(neg_mean[0:w, c:c + 1], sums[0:w, c:c + 1], ACT.Copy, scale=-1 / MLD))
                    act.activation(junk[0:w, :], hc[0:w, c, :], ACT.Square, bias=neg_mean[0:w, c:c + 1],
                                   accum_out=sqs[0:w, c:c + 1]).then_inc(stat_ready, 1)
                    act.wait_ge(stat_ready, NTT * h + c + 1)
                for m in range(8):
                    c, r_ = QKVO + m, 4 * h
                    split_hi(act, c + 1, r_, KD)
                    if m in (2, 3):
                        continue
                    act.wait_ge(mm_done, at(c, r_))
                    if m == 0:
                        act.wait_ge(hn_half, h)
                    dst = {0: q1, 4: v1, 6: o1}[m - m % 2][:, m % 2, :]
                    act.activation(by3(dst), group(3 * (c % 2)), ACT.Sigmoid if m >= 6 else ACT.Copy,
                                   scale=1 / WS).then_inc(evac[c % 2], 1)
                tokens(0, vn)
                act.wait_ge(bc_t, 3 * h + 1)
                act.activation(by3(m_bc), group(0), ACT.Copy).then_inc(bc_act, 1)
                for t in range(1, 5):
                    tokens(t, vn)
                act.wait_ge(dx_ready, h + 1)
                act.activation(dec[:, 0:SEQ], dec[:, 0:SEQ], ACT.Exp, scale=-1.0)
                act.activation(dec[0:TS, SEQ:SEQ + TS], dec[0:TS, SEQ:SEQ + TS], ACT.Exp,
                               scale=-1.0).then_inc(dec_ready, 1)
                for t in range(5):
                    tokens(t, hc)
                act.wait_ge(selh_ready, h + 1)
                for b in range(CSL):
                    normaliser(b)
                for c in range(8):
                    statistics(c)
                act.wait_ge(mr_in, 2 * h + 1)
                act.activation(roots[:, 1, 0:8], roots[:, 0, 0:8], ACT.Abs_reciprocal_sqrt).then_inc(mr_out, 1)
                for b in range(CSL, NB):
                    normaliser(b)
                statistics(8)
                act.wait_ge(mr_in, 2 * h + 2)
                act.activation(roots[0:TS, 1, 8:9], roots[0:TS, 0, 8:9], ACT.Abs_reciprocal_sqrt).then_inc(mr_out, 1)
                for k in range(2):
                    act.wait_ge(hs_t, 2 * h + k + 1)
                    alone(act)
                    act.activation(hn[:, 0, ds(2 * h + k, 1), :], one(flat(3 - 3 * k, T)), ACT.Copy,
                                   scale=g_h[:, k:k + 1]).then_inc(hn_hi, 1)
            chain.leave(HEADS)

        def pe_mlstm(pe):
            with pe.Fori(0, HEADS) as h:
                for m in range(8):
                    if m < 2:
                        pe.wait_ge((hn_half, hn_done)[m], h)
                    products(pe, QKVO + m, 4 * h, u, KD)
                def tokens(t, src, bank, done):
                    for tt in range(2 * t, min(2 * t + 2, NTT)):
                        w = P if tt < NTT - 1 else TS
                        for k in range(2):
                            o = (tt % 2) * MLD + k * P
                            ins = pe.transpose(ps[0:w, bank, o:o + P], src[:, k, tt * P:tt * P + w], ident[:, :])
                    ins.then_inc(done, 1)
                pe.wait_ge(evac[0], out_of_banks(QKVO + 5, 4 * h))
                pe.wait_ge(evac[1], out_of_banks(QKVO + 4, 4 * h))
                tokens(0, k1, 6, kn_t)
                tokens(0, v1, 7, vn_t)
                pe.wait_ge(selh_ready, h + 1)
                pe.wait_ge(evac[0], out_of_banks(QKVO + 7, 4 * h))
                pe.wait_ge(evac[1], out_of_banks(QKVO + 6, 4 * h))
                for src, bank in ((m_row, 0), (i_row, 3)):
                    for g in range(3):
                        ins = pe.matmul(ps[:, bank + g, 0:GW], sel_h[:, :], src[:, g * GW:(g + 1) * GW],
                                        start=True, stop=True)
                    ins.then_inc(bc_t, 1)
                pe.matmul(ps[:, 5, 400:416], sel_h[:, :], decay[:, :], start=True, stop=True).then_inc(bc_t, 1)
                for t in range(1, 5):
                    pe.wait_ge(kn_ev, 5 * h + t)
                    tokens(t, k1, 6, kn_t)
                    pe.wait_ge(vn_ev, 10 * h + t)
                    tokens(t, v1, 7, vn_t)
                pe.wait_ge(bc_act, h + 1)
                for c in range(NTT):
                    w = P if c < NTT - 1 else TS
                    for k in range(2):
                        ins = pe.matmul(ps[0:w, c // 4, (c % 4) * P:(c % 4) * P + w], k1[:, k, c * P:c * P + w],
                                        q1[:, k, c * P:c * P + w], start=(k == 0), stop=(k == 1))
                ins.then_inc(st_done, 1)
                for t in range(5):
                    if t == 1:
                        pe.wait_ge(kn_ev, 5 * h + 5)
                    else:
                        pe.wait_ge(vn_ev, 10 * h + 5 + max(t - 1, 0))
                    tokens(t, o1, 7 - t % 2, vn_t)
                pe.wait_ge(kn_ev, 5 * h + 5)
                pe.wait_ge(vn_ev, 10 * h + 5)
                pe.wait_ge(bc_dve, 2 * h + 2)

                def update(c):
                    if c >= 2:
                        pe.wait_ge(state_ready, 8 * h + c - 1)
                    if c == 1:
                        pe.wait_ge(vn_ev, 10 * h + 10)
                    for k in range(2):
                        ins = pe.matmul(ps[:, 3 + 2 * (c % 2) + k, 0:ML1], wk[:, c, k * P:(k + 1) * P], vn[:, c, :],
                                        start=True, stop=True)
                    ins.then_inc(up_done, 1)

                def numerators(c):
                    if c == 0:
                        pe.wait_ge(sd_ready, h + 1)
                        pe.wait_ge(qi_ready, h + 1)
                        pe.wait_ge(vn_ev, 10 * h + 10)
                    else:
                        pe.wait_ge(state_ready, 8 * h + c)
                    if c >= 2:
                        pe.wait_ge(hc_ready, NTT * h + c - 1)
                    o = ps[:, 7 if c % 2 == 0 else 0, 0:ML1]
                    for k in range(2 if c else 0):
                        pe.matmul(o, q1[:, k, c * P:(c + 1) * P], state[c % 2][:, k, :], start=(k == 0), stop=False)
                    pe.matmul(o, sd[:, c * P:(c + 1) * P], vn[:, c, :], start=(c == 0), stop=True).then_inc(
                        num_done, 1)
                update(0)
                for c in range(8):
                    if c < 7:
                        update(c + 1)
                    numerators(c)
                pe.matmul(ps[0:TS, 2, 0:ML1], sd[0:TS, SEQ:SEQ + TS], vn[0:TS, 8, :], start=True, stop=False)
                for b in range(NB):
                    pe.wait_ge(cs_loaded[b % CSL], 16 * (NB // CSL * h + b // CSL + 1))
                    pe.wait_ge(nc_ready, NB * h + b + 1)
                    for k in range(2):
                        ins = pe.matmul(ps[0:TS, 2, 0:ML1], q_pad[:, k, TS * b:TS * (b + 1)], cs[b % CSL][:, k, :],
                                        start=False, stop=(b == NB - 1 and k == 1))
                    ins.then_inc(inter_done, 1)
                    pe.wait_ge(wkb_ready, NB * h + b + 1)
                    if b < 2:
                        pe.wait_ge(state_ready, 8 * h + 7 + b)
                    else:
                        pe.wait_ge(cs_ready, NB * h + b - 1)
                    for k in range(2):
                        ins = pe.matmul(ps[:, 3 + 2 * (b % 2) + k, 0:ML1], wk_b[b % 2][:, k * P:(k + 1) * P],
                                        vn[0:TS, 8, :], start=True, stop=True)
                    ins.then_inc(ups_done, 1)
                pe.wait_ge(hs_ready, 2 * h + 1)
                pe.wait_ge(n_made, h + 1)
                for k in range(2):
                    ins = pe.transpose(ps[0:1 + NB, 7, k * P:(k + 1) * P], n_new[:, k, :], ident[:, :])
                ins.then_inc(n_t, 1)
                for k in range(2):
                    for c in range(8):
                        pe.transpose(flat(3 - 3 * k, T)[:, c * P:(c + 1) * P], hc[:, c, k * P:(k + 1) * P], ident[:, :])
                pe.wait_ge(hs_ready, 2 * h + 2)
                alone(pe)
                for k in range(2):
                    pe.transpose(ps[:, 5 - 3 * k, 0:TS], hc[0:TS, 8, k * P:(k + 1) * P],
                                 ident[0:TS, 0:TS]).then_inc(hs_t, 1)

        def dve_mlstm(dve, chain):
            per = 3 * NTT + 2 * 4 + NB + 1
            with dve.Fori(0, HEADS) as h:
                chain.enter(h, per)
                dve.wait_ge(hn_done, h)
                dve.tensor_copy(sel_h[:, :].rearrange("p (a n) -> p a n", a=1), sel[:, ds(h, 1), :])
                dve.tensor_copy(a_h[:, :, :], acol[:, :, :, ds(h, 1)].rearrange("p k c a -> p k (c a)"))
                dve.tensor_copy(g_h[:, :], gains[:, ds(GM + 2 * h, 2)])
                dve.tensor_copy(n_h[:, :, :], nT[:, :, ds(h, 1), :].rearrange("p b a k -> p (b a) k")).then_inc(
                    selh_ready, 1)
                for m in range(8):
                    c, r_ = QKVO + m, 4 * h
                    split_lo(dve, c + 1, r_, KD)
                    if m in (2, 3):
                        dve.wait_ge(mm_done, at(c, r_))
                        dve.tensor_scalar(by3(k1[:, m % 2, :]), group(3 * (c % 2)), MLD ** -0.5 / WS, None,
                                          ALU.mult).then_inc(evac[c % 2], 1)
                dve.wait_ge(selh_ready, h + 1)

                def weighted_keys(t):
                    dve.wait_ge(kn_t, 5 * h + t + 1)
                    for tt in range(2 * t, min(2 * t + 2, NTT)):
                        w = P if tt < NTT - 1 else TS
                        ins = dve.tensor_scalar(wk[0:w, tt, :], ps[0:w, 6, (tt % 2) * MLD:(tt % 2 + 1) * MLD],
                                                a_h[0:w, 1, tt:tt + 1], None, ALU.mult)
                    ins.then_inc(kn_ev, 1)
                weighted_keys(0)
                dve.wait_ge(bc_t, 3 * h + 3)
                dve.tensor_copy(by3(i_bc), group(3)).then_inc(bc_dve, 1)
                dve.tensor_copy(d_h[:, :], ps[:, 5, 400:416]).then_inc(bc_dve, 1)
                dve.wait_ge(bc_dve, 2 * h + 2)
                for t in range(1, 5):
                    weighted_keys(t)
                dve.wait_ge(bc_act, h + 1)
                dve.wait_ge(vn_t, 10 * h + 5)
                for c in range(8):
                    dve.scalar_tensor_tensor(dec[:, c * P:(c + 1) * P], m_bc[:, c * P:(c + 1) * P], a_h[:, 0, c:c + 1],
                                             dmask[:, :], ALU.subtract, ALU.max)
                dve.scalar_tensor_tensor(dec[0:TS, SEQ:SEQ + TS], m_bc[0:TS, SEQ:T], a_h[0:TS, 0, 8:9],
                                         dmask_s[:, :], ALU.subtract, ALU.max).then_inc(dx_ready, 1)
                dve.wait_ge(st_done, h + 1)
                for k in range(2):
                    ins = dve.tensor_tensor(q1[:, k, :], q1[:, k, :], i_bc, ALU.mult)
                chain.link(ins)
                dve.tensor_copy(q_pad.rearrange("p k (b n) -> p k b n", n=36)[:, :, :, 0:NS],
                                q1[:, :, SEQ:T].rearrange("p k (b t) -> p k b t", b=NB)).then_inc(qi_ready, 1)
                dve.wait_ge(dec_ready, h + 1)
                dve.wait_ge(kn_t, 5 * h + 5)
                dve.tensor_tensor(sd[:, 0:SEQ], flat(0, 1024), dec[:, 0:SEQ], ALU.mult)
                dve.tensor_tensor(sd[0:TS, SEQ:SEQ + TS], ps[0:TS, 2, 0:TS], dec[0:TS, SEQ:SEQ + TS],
                                  ALU.mult).then_inc(sd_ready, 1)

                def outputs(c, bank):
                    w = P if c < NTT - 1 else TS
                    den, d_, r_ = ps[0:w, bank, MLD:MLD + 1], den_[0:w, :], rec_[c % 2][0:w, :]
                    chain.link(dve.tensor_tensor(d_, den, a_h[0:w, 2, c:c + 1], ALU.max))
                    chain.link(dve.scalar_tensor_tensor(d_, den, -1.0, d_, ALU.mult, ALU.max))
                    chain.link(dve.reciprocal(r_, d_))
                    dve.scalar_tensor_tensor(hc[0:w, c, :], ps[0:w, bank, 0:MLD], r_, hc[0:w, c, :], ALU.mult,
                                             ALU.mult).then_inc(hc_ready, 1)

                def variances(c0, c1, w):
                    dve.wait_ge(stat_ready, NTT * h + c1)
                    dve.tensor_scalar(roots[0:w, 0, c0:c1], sqs[0:w, c0:c1], MLD * EPS, None, ALU.add).then_inc(
                        mr_in, 1)

                def deviations(c0, c1, w, n):
                    x, y, z = (roots[0:w, i, c0:c1] for i in range(3))
                    dve.wait_ge(mr_in, 2 * h + n + 1)
                    dve.wait_ge(mr_out, 2 * h + n + 1)
                    newton(dve, chain, x, y, z)

                def scaled(c, w):
                    return dve.tensor_scalar(hc[0:w, c, :], hc[0:w, c, :], neg_mean[0:w, c:c + 1],
                                             roots[0:w, 2, c:c + 1], ALU.add, ALU.mult)

                def next_state(c):
                    dve.wait_ge(up_done, 8 * h + c + 1)
                    up = ps[:, 3 + 2 * (c % 2):5 + 2 * (c % 2), 0:ML1]
                    if c >= 2:
                        dve.wait_ge(num_done, 8 * h + c)
                    if c == 0:
                        dve.wait_ge(state_stored, 16 * h)
                        dve.tensor_copy(state[1], up).then_inc(state_ready, 1)
                    else:
                        dve.wait_ge(state_ready, 8 * h + c)
                        dve.scalar_tensor_tensor(state[(c + 1) % 2], state[c % 2], d_h[:, c:c + 1], up, ALU.mult,
                                                 ALU.add).then_inc(state_ready, 1)
                for c in range(8):
                    next_state(c)
                    dve.wait_ge(num_done, 8 * h + c + 1)
                    outputs(c, 7 if c % 2 == 0 else 0)
                dve.wait_ge(state_ready, 8 * h + 8)
                dve.wait_ge(n_t, h)
                chain.mark(dve.tensor_copy(n_new[:, :, 0:1], state[0][:, :, MLD:MLD + 1]))
                for b in range(NB):
                    if b == 2:
                        variances(0, 8, P)
                    if b == 3:
                        deviations(0, 8, P, 0)
                    for c in (2 * b - 8, 2 * b - 7) if b >= 4 else ():
                        ins = scaled(c, P)
                    if b == NB - 1:
                        ins.then_inc(hs_ready, 1)
                    if b >= 2:
                        dve.wait_ge(ups_done, NB * h + b - 1)
                    dve.wait_ge(kn_ev, 5 * h + 5)
                    dve.tensor_scalar(wk_b[b % 2], wk[0:TS, 8, :], bmask[:, b:b + 1], None, ALU.mult).then_inc(
                        wkb_ready, 1)
                    dve.wait_ge(ups_done, NB * h + b + 1)
                    dve.wait_ge(cs_stored[b % 2], 16 * (NB // 2 * h + b // 2))
                    dve.scalar_tensor_tensor(cs_new[b % 2], cs[b % CSL], d_h[:, 8 + b:9 + b],
                                             ps[:, 3 + 2 * (b % 2):5 + 2 * (b % 2), 0:ML1], ALU.mult,
                                             ALU.add).then_inc(cs_ready, 1)
                    dve.wait_ge(cs_ready, NB * h + b + 1)
                    ins = dve.tensor_copy(n_new[:, :, 1 + b:2 + b], cs_new[b % 2][:, :, MLD:MLD + 1])
                    ins.then_inc(n_made, 1) if b == NB - 1 else chain.mark(ins)
                dve.wait_ge(inter_done, NB * h + NB)
                outputs(8, 2)
                dve.wait_ge(n_t, h + 1)
                dve.wait_ge(n_stored, 32 * h)
                dve.tensor_copy(n_nat, ps[0:1 + NB, 7, 0:MLD]).then_inc(n_ev, 1)
                variances(8, 9, TS)
                deviations(8, 9, TS, 1)
                scaled(8, TS).then_inc(hs_ready, 1)
                for k in range(2):
                    dve.wait_ge(hn_hi, 2 * h + k + 1)
                    dve.scalar_tensor_tensor(hn[:, 1, ds(2 * h + k, 1), :], one(flat(3 - 3 * k, T)), g_h[:, k:k + 1],
                                                   hn[:, 0, ds(2 * h + k, 1), :], ALU.mult,
                                                   ALU.subtract).then_inc((hn_half, hn_done)[k], 1)
            chain.leave(HEADS)

        nat = arena[:, 27, :]
        gains_nat, sc_nat, n_rows = nat[0:85, 0:P], nat[0:2 * NB, 128:128 + CH], nat[0:64, 640:768]
        conv_nat = arena[0:2 + 2 * NB, 26, 0:CH]
        y_nat = flat_rows(0, KF)[:, 0:NTT * D].rearrange("p (c f) -> p c f", c=NTT)
        conv_t, conv_ev, own_stored = sem("conv_t"), sem("conv_ev"), sem("own_stored")

        block = ctx.enter_context(nc.Block())

        @block.sync
        def _(sp):
            for tt in range(NTT):
                w = P if tt < NTT - 1 else TS
                src = x_p[0, tt * P:tt * P + w, :] if tt < NTT - 1 else x_s.rearrange("b t d -> (b t) d")
                sp.dma_start(arena[0:w, tt, 0:D], src).then_inc(x_loaded[tt], 16)
                if tt == 1:
                    sp.dma_start(gains_nat[0:64, :], norms.rearrange("l n (k p) -> (l n k) p", p=P)).then_inc(
                        gain_loaded, 16)
                    sp.dma_start(gains_nat[64:72, :], mh_g1.rearrange("a (k p) -> (a k) p", p=P)).then_inc(
                        gain_loaded, 16)
                    sp.dma_start(gains_nat[72:73, :], subln_g0).then_inc(gain_loaded, 16)
                    sp.dma_start(gains_nat[73:85, :], conv_w0.rearrange("a w (k p) -> (a w k) p", p=P)).then_inc(
                        gain_loaded, 16)
                    sp.dma_start(sc_nat, state_conv.rearrange("a b t c -> (a b t) c")).then_inc(gain_loaded, 16)
                    sp.dma_start(n_rows, state_n.rearrange("a b h (k p) -> (a b h k) p", p=P)).then_inc(
                        gain_loaded, 16)
            sp.dma_start(lam_rows, lam0.rearrange("a f d -> a (f d)").partition_broadcast(P)).then_inc(lam_loaded, 16)
            sp.dma_start(page_ids[:, :], page_table.rearrange("(a b) n -> a (b n)", a=1)).then_inc(ids_loaded, 16)
            sp.dma_start(b_if[:, :], b_if1.rearrange("a (g h) -> h (a g)", g=2),
                         allow_slow_non_contiguous=True).then_inc(bif_loaded, 16)
            sp.dma_start(m_prev[:, 8:16], state_m.rearrange("a b h -> h (a b)"),
                         allow_slow_non_contiguous=True).then_inc(m0_loaded, 16)
            q_k = lambda i, j: w_cols(w_in0[0], ds(3 * CH + j * CH + i * P, P))
            load_tile(sp, QK, 0, q_k(0, 0), KD, wait=False)
            load_tile(sp, QK + 1, 0, q_k(0, 1), KD, wait=False)
            with sp.Fori(1, HEADS) as i:
                for j in range(2):
                    load_tile(sp, QK + j, i, q_k(i, j), KD)
            with sp.Fori(0, 2) as i:
                for j in range(2):
                    load_tile(sp, V + j, i, w_cols(w_in0[0], ds(5 * CH + (2 * i + j) * P, P)), KD)
            with sp.Fori(0, 2) as i:
                for m in range(6):
                    first = (CH, 2 * CH, 0)[m % 3] + m // 3 * P
                    load_tile(sp, CXB + m, 3 * i, w_cols(w_in0[0], ds(first + 2 * i * P, P)), KD)
            load_tile(sp, WO0, 0, w_cols(w_out0[0], ds(0, P)), KD)
            load_tile(sp, WO0 + 1, 0, w_cols(w_out0[0], ds(P, P)), KD)
            load_pages(sp)
            with sp.Fori(1, 4) as i:
                for j in range(2):
                    load_tile(sp, WO0 + j, i, w_cols(w_out0[0], ds((2 * i + j) * P, P)), KD)
            load_ffn(sp, FF0, 0)
            load_tile(sp, GATES, 0, w_cols(w_in1[0], slice(4 * D, 4 * D + 8)), KD, n=8)
            with sp.Fori(0, HEADS) as h:
                for m in range(8):
                    load_tile(sp, QKVO + m, 4 * h, head_src(h, m), KD)
            with sp.Fori(0, 4) as i:
                for j in range(2):
                    load_tile(sp, WO1 + j, i, w_cols(w_out1[0], ds((2 * i + j) * P, P)), KD)
            load_ffn(sp, FF1, 1)
            for tt in range(NTT):
                w = P if tt < NTT - 1 else TS
                sp.wait_ge(y_ev, tt + 1)
                dst = y_p[0, tt * P:tt * P + w, :] if tt < NTT - 1 else y_s.rearrange("b t d -> (b t) d")
                sp.dma_start(dst, y_nat[0:w, tt, :]).then_inc(out_done, 16)
            sp.wait_ge(out_done, 16 * NTT)

        @block.gpsimd
        def _(pool):
            chain = Chain(pool, pool_c)
            for t, v in ((ident, 0.0), (ones, 1.0), (causal, 0.0), (dmask, 0.0), (dmask_s, 0.0), (smask, 0.0),
                         (bmask, 1.0), (sel, 1.0)):
                chain.mark(pool.memset(t[:], v))
            chain.sync()

            def where(t, op, fill, base, pattern, by):
                chain.link(pool.affine_select(out=t, in_=t, compare_op=op, fill=fill, base=base, pattern=pattern,
                                              channel_multiplier=by))
            where(ident[:, :], ALU.not_equal, 1.0, 0, [[-1, P]], 1)
            where(causal[:, :], ALU.is_ge, -BIG, 0, [[-1, P]], 1)
            where(dmask[:, :], ALU.is_ge, BIG, 0, [[1, P]], -1)
            where(dmask_s[:, :], ALU.is_ge, BIG, 0, [[1, TS]], -1)
            s4 = dmask_s[:, :].rearrange("p (b t) -> p b t", b=NB)
            where(s4, ALU.is_ge, BIG, 0, [[-NS, NB], [0, NS]], 1)
            m4 = smask[:, :].rearrange("p (b c t) -> p b c t", b=NB, c=2 * HEADS)
            where(m4, ALU.is_ge, -BIG, 0, [[NS, NB], [0, 2 * HEADS], [1, NS]], -1)
            where(m4, ALU.is_ge, -BIG, 0, [[-NS, NB], [0, 2 * HEADS], [0, NS]], 1)
            where(bmask[:, :], ALU.is_ge, 0.0, 0, [[-NS, NB]], 1)
            where(bmask[:, :], ALU.is_ge, 0.0, NS - 1, [[NS, NB]], -1)
            where(sel[:, :, :], ALU.is_ge, 0.0, 0, [[-1, HEADS], [0, P]], 1)
            where(sel[:, :, :], ALU.is_ge, 0.0, 0, [[1, HEADS], [0, P]], -1)
            pool.sem_inc(const_ready, 1)
            pool.sem_inc(ssq_added, KD)
            pool_lo(pool, 0)
            u_made(pool, 0, 6)
            pool.memset(conv_in[:, 0:2], 0.0).then_inc(const_ready, 1)
            pool.wait_ge(mix_ready, HEADS)
            pool.wait_ge(conv_ev, 1)
            pool.dma_start(conv_p[0, 0], conv_nat[0:2, :]).then_inc(conv_saved, 16)
            pool.dma_start(conv_s[0].rearrange("b t c -> (b t) c"), conv_nat[2:2 + 2 * NB, :]).then_inc(conv_saved, 16)
            pool.wait_ge(conv_saved, 32)
            def copy_head(h):
                pool.tensor_copy(one(v_h), vT[:, ds(h, 1), :]).then_inc(cur_ready, 1)
                pool.tensor_copy(one(k_h), kT[:, ds(h, 1), :]).then_inc(cur_ready, 1)
                pool.tensor_copy(one(q_h), qT[:, ds(h, 1), 0:SEQ]).then_inc(cur_ready, 1)

            def store_head(h):
                for ev, src, dst in ((v_ev, v_nat, v_p), (k_ev, k_nat, k_p)):
                    pool.wait_ge(ev, h + 1)
                    alone(pool)
                    pool.dma_start(dst[0, 0].rearrange("(c p) h e -> p c h e", p=P)[:, :, ds(h, 1), :],
                                   src.rearrange("p (c a e) -> p c a e", c=8, a=1)).then_inc(kv_stored, 16)
            copy_head(0)
            with pool.Fori(0, HEADS - 1) as h:
                store_head(h)
                pool.wait_ge(kv_stored, 32 * h + 32)
                pool.wait_ge(s_done, 16 * h + 16)
                copy_head(h + 1)
            store_head(HEADS - 1)
            pool.dma_start(k_s[0].rearrange("b t h e -> (b t) h e"), kv_s_nat[:, 0, :, :]).then_inc(own_stored, 16)
            pool.dma_start(v_s[0].rearrange("b t h e -> (b t) h e"), kv_s_nat[:, 1, :, :]).then_inc(own_stored, 16)
            for n in (1, 2, 3, 4):
                add_squares(pool, n)
                if n % 2:
                    pool_after(pool, n // 2)
                if n % 2 == 0:
                    pool_lo(pool, n // 2)
            h_made(pool, 1, KD - 1)
            pool.dma_start(spill, hT[:, :, :]).then_inc(spilled, 16)
            pool.wait_ge(r_dve, 2)
            pool.dma_start(m_p.rearrange("a b h -> h (a b)"), m_out[:, 0:1],
                           allow_slow_non_contiguous=True).then_inc(m_stored, 16)
            pool.dma_start(m_s.rearrange("a b h -> h (a b)"), m_out[:, 1:1 + NB],
                           allow_slow_non_contiguous=True).then_inc(m_stored, 16)
            pool.wait_ge(rows_ready, 1)
            with pool.Fori(0, HEADS) as h:
                def state_of(a, b):
                    return a[0, b, ds(h, 1), :, :].rearrange("a (k p) e -> p (a k) e", p=P)

                def load(b):
                    pool.wait_ge(cs_ready, NB * h + (b - CSL + 1 if b >= CSL else 0))
                    alone(pool)
                    pool.dma_start(cs[b % CSL][:, :, 0:MLD], state_of(state_C, b)).then_inc(cs_loaded[b % CSL], 16)
                for b in range(CSL):
                    load(b)
                pool.wait_ge(state_ready, 8 * h + 8)
                alone(pool)
                pool.dma_start(state_of(C_p, 0), state[0][:, :, 0:MLD]).then_inc(state_stored, 16)
                for b in range(NB):
                    pool.wait_ge(cs_ready, NB * h + b + 1)
                    alone(pool)
                    pool.dma_start(state_of(C_s, b), cs_new[b % 2][:, :, 0:MLD]).then_inc(cs_stored[b % 2], 16)
                    if b + CSL < NB:
                        load(b + CSL)
                pool.wait_ge(n_ev, h + 1)
                alone(pool)
                pool.dma_start(n_p[0, :, ds(h, 1), :].rearrange("b a d -> b (a d)"), n_nat[0:1, :]).then_inc(n_stored, 16)
                pool.dma_start(n_s[0, :, ds(h, 1), :].rearrange("b a d -> b (a d)"), n_nat[1:1 + NB, :]).then_inc(
                    n_stored, 16)
            pool.wait_ge(hn_done, HEADS)
            pool.wait_ge(n_stored, 32 * HEADS)
            for b in range(2):
                pool.wait_ge(cs_stored[b], 16 * HEADS * NB // 2)
            pool.dma_start(hT[:, :, :], spill).then_inc(restored, 16)
            for n in (5, 6, 7):
                add_squares(pool, n)
                if n == 5:
                    pool_after(pool, 2)
                if n == 6:
                    pool_lo(pool, 3)
            pool.wait_ge(kv_stored, 32 * HEADS)
            pool.wait_ge(own_stored, 32)
            pool.wait_ge(conv_saved, 32)
            pool.wait_ge(m_stored, 32)
            pool.wait_ge(state_stored, 16 * HEADS)

        @block.scalar
        def _(act):
            chain = Chain(act, act_c)
            act.wait_ge(lam_ready, 1)
            act.activation(lam_e, lam_e, ACT.Exp).then_inc(misc_ev, 1)
            split_hi(act, QK, 0, KD, first=True)
            for tt in range(NTT):
                w = P if tt < NTT - 1 else TS
                act.wait_ge(x_loaded[tt], 16)
                if tt >= 2:
                    act.wait_ge(sq_ready, tt - 1)
                ins = act.activation(sq[tt % 2][0:w, 0:D], arena[0:w, tt, 0:D], ACT.Square,
                                     accum_out=roots[0:w, 3, tt:tt + 1])
                if tt:
                    ins.then_inc(sq_ready, 1)
                if tt % 2:
                    continue
                act.wait_ge(x_t, tt + 1)
                act.activation(hT[:, :, tt * P:tt * P + w],
                               flat(2 * (tt % 3), 1024).rearrange("p (k t) -> p k t", t=P)[:, :, 0:w],
                               ACT.Copy).then_inc(x_ev[0], 1)
            act.wait_ge(x_ev[0], 5)
            act.wait_ge(x_ev[1], 4)
            act_before(act, 0, 0)
            act_proj0(act, chain)
            act_heads(act)
            act_samples(act)
            act_project(act, WO0, 1, KD)
            act_roots(act, norm_q(1), NTT)
            act_before(act, 2, 1)
            act_ffn(act, FF0, 0, 3, True)
            act_roots(act, norm_q(3), NTT)
            act_before(act, 4, 2)
            act_gates(act, chain)
            act_mlstm(act, chain)
            act_project(act, WO1, 5, KD)
            act_roots(act, norm_q(5), NTT)
            act_before(act, 6, 3)
            act_ffn(act, FF1, 1, 7, False)
            act_roots(act, norm_q(7), NTT)
            for tt in range(NTT):
                w = P if tt < NTT - 1 else TS
                act.wait_ge(y_t, tt + 1)
                act.activation(y_nat[0:w, tt, :], flat(3 + 2 * (tt % 2), 1024)[0:w, :], ACT.Copy).then_inc(y_ev, 1)

        @block.vector
        def _(dve):
            chain = Chain(dve, dve_c)
            chain.link(dve.memset(roots[:, :, :], 1.0))
            chain.mark(dve.memset(eps_col[:, :], D * EPS))
            dve.wait_ge(lam_loaded, 16)
            l4 = lam_rows.rearrange("p (f d) -> p f d", f=4)
            chain.link(dve.tensor_tensor(lam_prod.rearrange("p (f d) -> p f d", f=2), l4[:, 0:4:2, :], l4[:, 1:4:2, :],
                                         ALU.mult))
            dve.tensor_reduce(lam_e, lam_prod.rearrange("p (f d) -> p f d", f=2), AX.X, ALU.add).then_inc(lam_ready, 1)
            dve.wait_ge(misc_t, 1)
            t = ps[:, 7, :]
            dve.tensor_scalar(gains[:, 0:64], t[:, 0:64], math.sqrt(D), None, ALU.mult)
            dve.tensor_scalar(gains[:, GM:GM + 8], t[:, 64:72], math.sqrt(MLD), None, ALU.mult)
            dve.tensor_scalar(gains[:, GS:GS + 1], t[:, 72:73], math.sqrt(P) * (1 - LAM_INIT), None, ALU.mult)
            dve.tensor_copy(gains[:, GC:GC + 12], t[:, 73:85])
            dve.tensor_copy(nT[:, :, :, :].rearrange("p b h k -> p (b h k)"), t[:, 128:192])
            chain.link(dve.tensor_copy(stT[:, :, :].rearrange("p k n -> p (k n)"), t[:, 256:320]))
            dve.wait_ge(misc_ev, 1)
            chain.link(dve.scalar_tensor_tensor(neg_lam, lam_e[:, 1:2], -LAM_INIT, lam_e[:, 0:1], ALU.add,
                                                ALU.subtract))
            split_lo(dve, QK, 0, KD)
            for tt in range(1, NTT, 2):
                dve.wait_ge(x_t, tt + 1)
                dve.tensor_copy(hT[:, :, tt * P:(tt + 1) * P],
                                flat(2 * (tt % 3), 1024).rearrange("p (k t) -> p k t", t=P)).then_inc(x_ev[1], 1)
            dve_before(dve, chain, 0, 0, 0, 0)
            dve.wait_ge(const_ready, 2)
            dve_proj0(dve, chain)
            dve.wait_ge(conv_t, 1)
            dve.tensor_copy(conv_nat[:, :], ps[0:2 + 2 * NB, 7, :]).then_inc(conv_ev, 1)
            dve_heads(dve, chain)
            dve_samples(dve, chain)
            dve_splits(dve, WO0, 8, KD)
            dve_after(dve, chain, 1, 0, 1)
            dve_before(dve, chain, 2, 0, 2, 1)
            dve_ffn(dve, FF0, 0, True)
            dve_after(dve, chain, 3, 0, 3)
            dve_before(dve, chain, 4, 1, 0, 2)
            dve_gates(dve, chain)
            dve_mlstm(dve, chain)
            dve_splits(dve, WO1, 8, KD)
            dve.wait_ge(restored, 16)
            dve_after(dve, chain, 5, 1, 1)
            dve_before(dve, chain, 6, 1, 2, 3)
            dve_ffn(dve, FF1, 1, False)
            dve_last(dve, chain)

        @block.tensor
        def _(pe):
            pe.wait_ge(const_ready, 1)
            pe.wait_ge(gain_loaded, 96)
            pe.transpose(ps[:, 7, 0:85], gains_nat, ident[0:85, 0:85])
            pe.transpose(ps[:, 7, 128:192], n_rows, ident[0:64, 0:64])
            for k in range(HC):
                ins = pe.transpose(ps[:, 7, 256 + 2 * NB * k:256 + 2 * NB * (k + 1)], sc_nat[:, k * P:(k + 1) * P],
                                   ident[0:2 * NB, 0:2 * NB])
            ins.then_inc(misc_t, 1)
            for tt in range(NTT):
                w = P if tt < NTT - 1 else TS
                pe.wait_ge(x_loaded[tt], 16)
                if tt >= 3:
                    pe.wait_ge(x_ev[(tt - 3) % 2], (tt - 3) // 2 + 1)
                for k in range(KD):
                    ins = pe.transpose(flat(2 * (tt % 3), 1024)[:, k * P:k * P + w],
                                       arena[0:w, tt, k * P:(k + 1) * P], ident[0:w, 0:w])
                ins.then_inc(x_t, 1)
            pe_norm(pe, 0)
            over_pairs(pe, 8, lambda i, j, last: products(pe, QK + j, i, u, KD, made=None if j else lambda k: u_made(pe, 0, k)))
            over_pairs(pe, 4, lambda i, j, last: products(pe, V + j, i, u, KD))
            with pe.Fori(0, 2) as i:
                for m in range(6):
                    products(pe, CXB + m, 3 * i, u, KD)
            pe.wait_ge(evac[0], WO0 // 2)
            pe.wait_ge(evac[1], WO0 // 2)
            pe.wait_ge(mix_ready, HEADS)
            for k in range(HC):
                ins = pe.transpose(ps[0:2 + 2 * NB, 7, k * P:(k + 1) * P], conv_new[:, k, :], ident[:, :])
            ins.then_inc(conv_t, 1)
            pe.wait_ge(conv_ev, 1)
            pe_heads(pe)
            pe_samples(pe)
            over_pairs(pe, 8, lambda i, j, last: products(
                pe, WO0 + j, i, mix, KD, made=None if j else lambda k: pe.wait_ge(mix_ready, HEADS + (k >= HC))))
            pe_norm(pe, 1)
            pe_norm(pe, 2)
            pe_ffn(pe, FF0, 0, 1)
            pe_norm(pe, 3)
            pe_norm(pe, 4)
            pe_gates(pe)
            pe_mlstm(pe)
            pe.wait_ge(hn_half, HEADS)
            over_pairs(pe, 8, lambda i, j, last: products(
                pe, WO1 + j, i, hn, KD, made=None if j else lambda k: pe.wait_ge(hn_done, (k + 1) // 2) if k else None))
            pe_norm(pe, 5)
            pe_norm(pe, 6)
            pe_ffn(pe, FF1, 1, 3)
            pe_norm(pe, 7)
            for tt in range(NTT):
                w = P if tt < NTT - 1 else TS
                pe.wait_ge(h_ready, 3 * (KD - len(POOL_H)) + KD * (tt // 3 + 1))
                if tt >= 2:
                    pe.wait_ge(y_ev, tt - 1)
                for k in range(KD):
                    ins = pe.transpose(flat(3 + 2 * (tt % 2), 1024)[0:w, k * P:(k + 1) * P],
                                       hT[:, k, tt * P:tt * P + w], ident[:, :])
                ins.then_inc(y_t, 1)


INS = ["x_prompt", "x_sample", "cache_k", "cache_v", "state_conv", "state_C", "state_n", "state_m", "page_table",
       "norms", "w_in0", "conv_w0", "lam0", "subln_g0", "w_out0", "w_in1", "b_if1", "mh_g1", "w_out1", "w_gu", "w_down"]
OUTS = [(1, SEQ, D), (NB, NS, D), (1, 1, SEQ, HEADS, P), (1, 1, SEQ, HEADS, P), (1, 1, 2, CH),
        (1, 1, HEADS, MLD, MLD), (1, 1, HEADS, MLD), (1, 1, HEADS), (1, NB, NS, HEADS, P), (1, NB, NS, HEADS, P),
        (1, NB, 2, CH), (1, NB, HEADS, MLD, MLD), (1, NB, HEADS, MLD), (1, NB, HEADS)]


def kernel(**inputs):
    import numpy as np
    import concourse.bacc as bacc
    from concourse.bass_utils import run_bass_kernel_spmd

    nc = bacc.Bacc("TRN2", target_bir_lowering=False, num_devices=1,
                   dynamic_dma_scratch_size=4096)
    arrays, args = {}, []
    for name in INS:
        a = np.ascontiguousarray(inputs[name])
        arrays[f"in_{name}"] = a
        args.append(nc.dram_tensor(f"in_{name}", a.shape, mybir.dt.from_np(a.dtype), kind="ExternalInput").ap())
    for i, shape in enumerate(OUTS):
        args.append(nc.dram_tensor(f"out_{i}", shape, F32, kind="ExternalOutput").ap())
    build(nc, *args)
    r = run_bass_kernel_spmd(nc, [arrays], core_ids=[0])
    return tuple(r.results[0][f"out_{i}"] for i in range(len(OUTS)))
```
